# Optimizing a Trainium2 kernel written in Bass

```python
import math
import jax, jax.numpy as jnp
from jax import lax
import numpy as np

D_MODEL = 1024
BATCH = 1
SEQ = 256
DEPTH = 2

CHUNK = 64
N_A = DEPTH // 2
N_B = DEPTH - N_A
EPS = 1e-6

POOL_WINDOWS = (2, 4, 8, 16)
N_POOL = len(POOL_WINDOWS)
POOL_GD = D_MODEL // N_POOL

N_HEADS = 8
QK_NOPE = 128
QK_ROPE = 64
V_DIM = 128
Q_RANK = 384
KV_RANK = 256
ROPE_THETA = 10000.0
ATTN_SCALE = 1.0 / math.sqrt(QK_NOPE + QK_ROPE)
Q_BLOCK = 128

N_GROUPS = 4
EXPERTS_PER_GROUP = 8
N_EXPERTS = N_GROUPS * EXPERTS_PER_GROUP
TOP_K = 2
D_EXPERT = 512
ROW_BLOCK = 256


def rms_norm(x, g):
    xf = x.astype(jnp.float32)
    y = xf * lax.rsqrt(jnp.mean(xf * xf, axis=-1, keepdims=True) + EPS)
    return (y * g.astype(jnp.float32)).astype(x.dtype)

def rope_tables(seq, dtype):
    half = QK_ROPE // 2
    inv = ROPE_THETA ** (-jnp.arange(half, dtype=jnp.float32) / half)
    ang = jnp.arange(seq, dtype=jnp.float32)[:, None] * inv[None, :]
    return jnp.cos(ang).astype(dtype), jnp.sin(ang).astype(dtype)

def apply_rope(x, cos, sin):
    half = QK_ROPE // 2
    x1, x2 = x[..., :half], x[..., half:]
    return jnp.concatenate([x1 * cos - x2 * sin, x2 * cos + x1 * sin], axis=-1)

def pool_mixer(h, w, b, scale):
    B, S, D = h.shape
    hg = h.reshape(B, S, N_POOL, POOL_GD).astype(jnp.float32)
    csum = jnp.pad(jnp.cumsum(hg, axis=1), ((0, 0), (1, 0), (0, 0), (0, 0)))
    t = jnp.arange(S)
    means = []
    for g, win in enumerate(POOL_WINDOWS):
        lo = jnp.maximum(t + 1 - win, 0)
        cnt = (t + 1 - lo).astype(jnp.float32)
        means.append((csum[:, 1:, g] - csum[:, lo, g]) / cnt[:, None])
    pooled = (jnp.stack(means, axis=2) - hg).astype(h.dtype)
    y = jnp.einsum('bsgc,gcd->bsgd', pooled, w) + b
    return y.reshape(B, S, D) * scale

def shared_kv(x, kv_in_norm, w_dkv, kv_norm, w_uk, w_uv, cos, sin):
    B, S, _ = x.shape
    hs = rms_norm(x, kv_in_norm)
    ckv = hs @ w_dkv
    c_kv = rms_norm(ckv[..., :KV_RANK], kv_norm)
    k_rope = apply_rope(ckv[..., KV_RANK:], cos, sin)
    k_nope = (c_kv @ w_uk).reshape(B, S, N_HEADS, QK_NOPE)
    v = (c_kv @ w_uv).reshape(B, S, N_HEADS, V_DIM)
    return k_nope, k_rope, v

def mla_attention(h, k_nope, k_rope, v, wq_down, q_norm, wq_up, wo, cos, sin):
    B, S, _ = h.shape
    cq = rms_norm(h @ wq_down, q_norm)
    q = (cq @ wq_up).reshape(B, S, N_HEADS, QK_NOPE + QK_ROPE)
    q_nope = q[..., :QK_NOPE]
    q_rope = apply_rope(q[..., QK_NOPE:], cos[:, None, :], sin[:, None, :])
    nb = S // Q_BLOCK
    qn_b = q_nope.reshape(B, nb, Q_BLOCK, N_HEADS, QK_NOPE).transpose(1, 0, 2, 3, 4)
    qr_b = q_rope.reshape(B, nb, Q_BLOCK, N_HEADS, QK_ROPE).transpose(1, 0, 2, 3, 4)
    k_chunk = jnp.arange(S) // CHUNK

    def attend(args):
        qn, qr, i = args
        s = (jnp.einsum('bqhd,bkhd->bhqk', qn, k_nope)
             + jnp.einsum('bqhr,bkr->bhqk', qr, k_rope)).astype(jnp.float32) * ATTN_SCALE
        q_chunk = (i * Q_BLOCK + jnp.arange(Q_BLOCK)) // CHUNK
        mask = k_chunk[None, :] <= q_chunk[:, None]
        s = jnp.where(mask[None, None], s, -jnp.inf)
        p = jax.nn.softmax(s, axis=-1).astype(v.dtype)
        return jnp.einsum('bhqk,bkhd->bqhd', p, v)

    o = lax.map(attend, (qn_b, qr_b, jnp.arange(nb)))
    o = o.transpose(1, 0, 2, 3, 4).reshape(B, S, N_HEADS * V_DIM)
    return o @ wo

def hier_moe(h, rg_w, rg_b, re_w, re_b, w_gate, w_up, w_down):
    B, S, D = h.shape
    T = B * S
    ht = h.reshape(T, D)
    gp = jax.nn.softmax((ht @ rg_w + rg_b).astype(jnp.float32), axis=-1)
    g_idx = jnp.argmax(gp, axis=-1)
    g_prob = jnp.take_along_axis(gp, g_idx[:, None], axis=-1)[:, 0]
    el = (ht @ re_w + re_b).astype(jnp.float32).reshape(T, N_GROUPS, EXPERTS_PER_GROUP)
    el = jnp.take_along_axis(el, g_idx[:, None, None], axis=1)[:, 0]
    top_p, top_i = lax.top_k(jax.nn.softmax(el, axis=-1), TOP_K)
    gates = g_prob[:, None] * top_p / jnp.sum(top_p, axis=-1, keepdims=True)
    expert_ids = (g_idx[:, None] * EXPERTS_PER_GROUP + top_i).astype(jnp.int32)

    N = T * TOP_K
    flat_e = expert_ids.reshape(N)
    flat_tok = jnp.arange(N, dtype=jnp.int32) // TOP_K
    flat_g = gates.reshape(N)
    order = jnp.argsort(flat_e, stable=True)
    sorted_e = flat_e[order]
    counts = jnp.bincount(flat_e, length=N_EXPERTS).astype(jnp.int32)
    padded = ((counts + ROW_BLOCK - 1) // ROW_BLOCK) * ROW_BLOCK
    pad_end = jnp.cumsum(padded)
    pad_start = pad_end - padded
    start = jnp.cumsum(counts) - counts
    dest = pad_start[sorted_e] + (jnp.arange(N, dtype=jnp.int32) - start[sorted_e])
    n_blocks = N // ROW_BLOCK + N_EXPERTS
    n_rows = n_blocks * ROW_BLOCK
    row_tok = jnp.zeros((n_rows,), jnp.int32).at[dest].set(flat_tok[order])
    row_w = jnp.zeros((n_rows,), jnp.float32).at[dest].set(flat_g[order])
    block_e = jnp.clip(jnp.searchsorted(pad_end, jnp.arange(n_blocks) * ROW_BLOCK, side='right'),
                       0, N_EXPERTS - 1).astype(jnp.int32)
    xb = ht[row_tok].reshape(n_blocks, ROW_BLOCK, D)

    def expert_block(args):
        xr, e = args
        return (jax.nn.silu(xr @ w_gate[e]) * (xr @ w_up[e])) @ w_down[e]

    y = lax.map(expert_block, (xb, block_e)).reshape(n_rows, D).astype(jnp.float32)
    out = jnp.zeros((T, D), jnp.float32).at[row_tok].add(y * row_w[:, None])
    return out.astype(h.dtype).reshape(B, S, D)

def first_inputs(seed: int = 0) -> dict:
    key = jax.random.key(seed)
    ks = iter(jax.random.split(key, 32))
    f32 = jnp.float32

    def nrm(shape, fan_in):
        return jax.random.normal(next(ks), shape, f32) * (fan_in ** -0.5)

    def gain(shape):
        return 1.0 + 0.02 * jax.random.normal(next(ks), shape, f32)

    def small(shape, s=0.01):
        return s * jax.random.normal(next(ks), shape, f32)

    return {
        "x": jax.random.normal(next(ks), (BATCH, SEQ, D_MODEL), f32),
        "pool_norm": gain((N_A, D_MODEL)),
        "pool_w": nrm((N_A, N_POOL, POOL_GD, POOL_GD), POOL_GD),
        "pool_b": small((N_A, N_POOL, POOL_GD)),
        "pool_scale": gain((N_A, D_MODEL)),
        "kv_in_norm": gain((D_MODEL,)),
        "w_dkv": nrm((D_MODEL, KV_RANK + QK_ROPE), D_MODEL),
        "kv_norm": gain((KV_RANK,)),
        "w_uk": nrm((KV_RANK, N_HEADS * QK_NOPE), KV_RANK),
        "w_uv": nrm((KV_RANK, N_HEADS * V_DIM), KV_RANK),
        "attn_norm": gain((N_B, D_MODEL)),
        "wq_down": nrm((N_B, D_MODEL, Q_RANK), D_MODEL),
        "q_norm": gain((N_B, Q_RANK)),
        "wq_up": nrm((N_B, Q_RANK, N_HEADS * (QK_NOPE + QK_ROPE)), Q_RANK),
        "wo": nrm((N_B, N_HEADS * V_DIM, D_MODEL), N_HEADS * V_DIM),
        "ffn_norm": gain((DEPTH, D_MODEL)),
        "router_group_w": nrm((DEPTH, D_MODEL, N_GROUPS), D_MODEL),
        "router_group_b": small((DEPTH, N_GROUPS)),
        "router_expert_w": nrm((DEPTH, D_MODEL, N_EXPERTS), D_MODEL),
        "router_expert_b": small((DEPTH, N_EXPERTS)),
        "w_gate": nrm((DEPTH, N_EXPERTS, D_MODEL, D_EXPERT), D_MODEL),
        "w_up": nrm((DEPTH, N_EXPERTS, D_MODEL, D_EXPERT), D_MODEL),
        "w_down": nrm((DEPTH, N_EXPERTS, D_EXPERT, D_MODEL), D_EXPERT),
        "final_norm": gain((D_MODEL,)),
    }

def first_block(x, pool_norm, pool_w, pool_b, pool_scale, kv_in_norm, w_dkv, kv_norm, w_uk, w_uv,
              attn_norm, wq_down, q_norm, wq_up, wo, ffn_norm, router_group_w, router_group_b,
              router_expert_w, router_expert_b, w_gate, w_up, w_down, final_norm):
    S = x.shape[1]
    cos, sin = rope_tables(S, x.dtype)
    k_nope = k_rope = v = None
    for l in range(DEPTH):
        if l < N_A:
            x = x + pool_mixer(rms_norm(x, pool_norm[l]), pool_w[l], pool_b[l], pool_scale[l])
        else:
            if l == N_A:
                k_nope, k_rope, v = shared_kv(x, kv_in_norm, w_dkv, kv_norm, w_uk, w_uv, cos, sin)
            j = l - N_A
            x = x + mla_attention(rms_norm(x, attn_norm[j]), k_nope, k_rope, v,
                                  wq_down[j], q_norm[j], wq_up[j], wo[j], cos, sin)
        x = x + hier_moe(rms_norm(x, ffn_norm[l]), router_group_w[l], router_group_b[l],
                         router_expert_w[l], router_expert_b[l], w_gate[l], w_up[l], w_down[l])
    return rms_norm(x, final_norm)


RMS_EPS = 1e-6
D_FF = 2816

DA_HEADS = 4
DA_HEAD_DIM = 64
DA_V_DIM = 2 * DA_HEAD_DIM
DA_WIDTH = DA_HEADS * DA_V_DIM

ML_HEADS = 4
ML_QK_DIM = 64
ML_V_DIM = 128
ML_WIDTH = ML_HEADS * ML_V_DIM
ML_CONV = 4
ML_QK_COLS = 2 * ML_HEADS * ML_QK_DIM

MIX_WIDTH = DA_WIDTH + ML_WIDTH

COLS = (DA_HEADS * 2 * DA_HEAD_DIM, DA_HEADS * 2 * DA_HEAD_DIM, DA_WIDTH,
        ML_QK_COLS, ML_WIDTH, ML_WIDTH, 2 * ML_HEADS)
SPLIT_IDX = tuple(int(s) for s in np.cumsum(COLS)[:-1])
IN_COLS = int(sum(COLS))


def _rmsnorm(x, g):
    xf = x.astype(jnp.float32)
    y = xf * lax.rsqrt(jnp.mean(xf * xf, axis=-1, keepdims=True) + RMS_EPS)
    return (y * g.astype(jnp.float32)).astype(x.dtype)

def _swiglu(h, w_in, w_out):
    gate, up = jnp.split(h @ w_in, 2, axis=-1)
    return (jax.nn.silu(gate) * up) @ w_out

def _rope(t, seq_len):
    d = t.shape[-1]
    inv_freq = ROPE_THETA ** (-jnp.arange(0, d, 2, dtype=jnp.float32) / d)
    ang = jnp.arange(seq_len, dtype=jnp.float32)[:, None] * inv_freq[None, :]
    cos, sin = jnp.cos(ang), jnp.sin(ang)
    t1, t2 = t[..., : d // 2], t[..., d // 2:]
    return jnp.concatenate([t1 * cos - t2 * sin, t2 * cos + t1 * sin], axis=-1)

def _diff_attention(q, k, v, lam_vecs, subln_g, lam_init):
    B, S, _ = q.shape
    q = q.reshape(B, S, DA_HEADS, 2, DA_HEAD_DIM).transpose(0, 2, 3, 1, 4)
    k = k.reshape(B, S, DA_HEADS, 2, DA_HEAD_DIM).transpose(0, 2, 3, 1, 4)
    v = v.reshape(B, S, DA_HEADS, DA_V_DIM).transpose(0, 2, 1, 3)
    q = _rope(q, S) * (DA_HEAD_DIM ** -0.5)
    k = _rope(k, S)
    lam = (jnp.exp(jnp.sum(lam_vecs[0] * lam_vecs[1]))
           - jnp.exp(jnp.sum(lam_vecs[2] * lam_vecs[3])) + lam_init)
    n_blk = S // Q_BLOCK
    q_blocks = q.reshape(B, DA_HEADS, 2, n_blk, Q_BLOCK, DA_HEAD_DIM).transpose(3, 0, 1, 2, 4, 5)
    key_chunk = jnp.arange(S) // CHUNK

    def block(args):
        q_blk, blk = args
        s = jnp.einsum('bhcqd,bhckd->bhcqk', q_blk, k)
        q_chunk = (blk * Q_BLOCK + jnp.arange(Q_BLOCK)) // CHUNK
        mask = key_chunk[None, :] <= q_chunk[:, None]
        p = jax.nn.softmax(jnp.where(mask, s, -jnp.inf), axis=-1)
        a = p[:, :, 0] - lam * p[:, :, 1]
        return jnp.einsum('bhqk,bhkd->bhqd', a, v)

    o = lax.map(block, (q_blocks, jnp.arange(n_blk)))
    o = o.transpose(1, 0, 3, 2, 4).reshape(B, S, DA_HEADS, DA_V_DIM)
    o = _rmsnorm(o, subln_g) * (1.0 - lam_init)
    return o.reshape(B, S, DA_WIDTH)

def _causal_conv(t, w, b):
    S = t.shape[1]
    tp = jnp.pad(t, ((0, 0), (ML_CONV - 1, 0), (0, 0)))
    y = b
    for j in range(ML_CONV):
        y = y + w[j] * tp[:, j:j + S]
    return y

def _mlstm(qk, v, o, gates, conv_w, conv_b, gate_b, norm_g):
    B, S, _ = v.shape
    NC = S // CHUNK
    qk = jax.nn.silu(_causal_conv(qk, conv_w, conv_b))
    q, k = jnp.split(qk, 2, axis=-1)

    def chunks(t, d):
        return t.reshape(B, NC, CHUNK, ML_HEADS, d).transpose(0, 3, 1, 2, 4)

    q = chunks(q, ML_QK_DIM) * (ML_QK_DIM ** -0.5)
    k = chunks(k, ML_QK_DIM)
    v = chunks(v, ML_V_DIM)
    g = (gates + gate_b).reshape(B, NC, CHUNK, 2, ML_HEADS).transpose(3, 0, 4, 1, 2)
    log_i = g[0]
    log_f = jax.nn.log_sigmoid(g[1])
    b = jnp.cumsum(log_f, axis=-1)
    b_last = b[..., -1]
    a = b_last[..., None] - b + log_i

    def step(carry, xs):
        C, n, m = carry
        k_c, v_c, a_c, bl = xs
        m_new = jnp.maximum(bl + m, a_c.max(-1))
        w = jnp.exp(a_c - m_new[..., None])
        decay = jnp.exp(bl + m - m_new)
        C_new = decay[..., None, None] * C + jnp.einsum('bhl,bhle,bhld->bhed', w, v_c, k_c)
        n_new = decay[..., None] * n + jnp.einsum('bhl,bhld->bhd', w, k_c)
        return (C_new, n_new, m_new), (C, n, m)

    init = (jnp.zeros((B, ML_HEADS, ML_V_DIM, ML_QK_DIM), jnp.float32),
            jnp.zeros((B, ML_HEADS, ML_QK_DIM), jnp.float32),
            jnp.zeros((B, ML_HEADS), jnp.float32))
    xs = (k.transpose(2, 0, 1, 3, 4), v.transpose(2, 0, 1, 3, 4),
          a.transpose(2, 0, 1, 3), b_last.transpose(2, 0, 1))
    _, (C_prev, n_prev, m_prev) = lax.scan(step, init, xs)
    C_prev = C_prev.transpose(1, 2, 0, 3, 4)
    n_prev = n_prev.transpose(1, 2, 0, 3)
    m_prev = m_prev.transpose(1, 2, 0)

    causal = jnp.tril(jnp.ones((CHUNK, CHUNK), dtype=bool))
    D = jnp.where(causal, b[..., :, None] - b[..., None, :] + log_i[..., None, :], -jnp.inf)
    m_inter = b + m_prev[..., None]
    m = jnp.maximum(m_inter, D.max(-1))
    w = jnp.exp(D - m[..., None]) * jnp.einsum('bhcjd,bhcsd->bhcjs', q, k)
    decay = jnp.exp(m_inter - m)
    num = (jnp.einsum('bhcjs,bhcse->bhcje', w, v)
           + decay[..., None] * jnp.einsum('bhcjd,bhced->bhcje', q, C_prev))
    den = w.sum(-1) + decay * jnp.einsum('bhcjd,bhcd->bhcj', q, n_prev)
    h = num / jnp.maximum(jnp.abs(den), jnp.exp(-m))[..., None]
    h = h.transpose(0, 2, 3, 1, 4).reshape(B, S, ML_HEADS, ML_V_DIM)
    h = _rmsnorm(h, norm_g).reshape(B, S, ML_WIDTH)
    return jax.nn.sigmoid(o) * h

def _mixer(h, w_in, w_out, lam_vecs, subln_g, lam_init, conv_w, conv_b, gate_b, ml_norm_g):
    proj = (h @ w_in).astype(jnp.float32)
    da_q, da_k, da_v, ml_qk, ml_v, ml_o, ml_g = jnp.split(proj, SPLIT_IDX, axis=-1)
    y_da = _diff_attention(da_q, da_k, da_v, lam_vecs, subln_g, lam_init)
    y_ml = _mlstm(ml_qk, ml_v, ml_o, ml_g, conv_w, conv_b, gate_b, ml_norm_g)
    y = jnp.concatenate([y_da, y_ml], axis=-1).astype(h.dtype)
    return y @ w_out

def second_inputs(seed: int = 0) -> dict:
    key = jax.random.key(seed)
    ks = jax.random.split(key, 13)
    f32 = jnp.float32
    x = jax.random.normal(ks[0], (BATCH, SEQ, D_MODEL), f32)
    ffn_w_in = jax.random.normal(ks[1], (DEPTH, 2, D_MODEL, 2 * D_FF), f32) * D_MODEL ** -0.5
    ffn_w_out = jax.random.normal(ks[2], (DEPTH, 2, D_FF, D_MODEL), f32) * D_FF ** -0.5
    norm_gains = 1.0 + 0.05 * jax.random.normal(ks[3], (DEPTH, 6, D_MODEL), f32)
    mix_w_in = jax.random.normal(ks[4], (DEPTH, D_MODEL, IN_COLS), f32) * D_MODEL ** -0.5
    mix_w_out = jax.random.normal(ks[5], (DEPTH, MIX_WIDTH, D_MODEL), f32) * MIX_WIDTH ** -0.5
    da_lambda = 0.1 * jax.random.normal(ks[6], (DEPTH, 4, DA_HEAD_DIM), f32)
    da_subln_g = 1.0 + 0.05 * jax.random.normal(ks[7], (DEPTH, DA_V_DIM), f32)
    ml_conv_w = jax.random.normal(ks[8], (DEPTH, ML_CONV, ML_QK_COLS), f32) * ML_CONV ** -0.5
    ml_conv_b = 0.01 * jax.random.normal(ks[9], (DEPTH, ML_QK_COLS), f32)
    ml_gate_b = jnp.concatenate([
        0.1 * jax.random.normal(ks[10], (DEPTH, ML_HEADS), f32),
        jax.random.uniform(ks[11], (DEPTH, ML_HEADS), f32, minval=3.0, maxval=6.0)], axis=-1)
    ml_norm_g = 1.0 + 0.05 * jax.random.normal(ks[12], (DEPTH, ML_V_DIM), f32)
    return {'x': x, 'ffn_w_in': ffn_w_in, 'ffn_w_out': ffn_w_out, 'norm_gains': norm_gains,
            'mix_w_in': mix_w_in, 'mix_w_out': mix_w_out, 'da_lambda': da_lambda,
            'da_subln_g': da_subln_g, 'ml_conv_w': ml_conv_w, 'ml_conv_b': ml_conv_b,
            'ml_gate_b': ml_gate_b, 'ml_norm_g': ml_norm_g}

def second_block(x, ffn_w_in, ffn_w_out, norm_gains, mix_w_in, mix_w_out, da_lambda,
              da_subln_g, ml_conv_w, ml_conv_b, ml_gate_b, ml_norm_g):
    for l in range(DEPTH):
        g = norm_gains[l]
        h = _swiglu(_rmsnorm(x, g[0]), ffn_w_in[l, 0], ffn_w_out[l, 0])
        x = x + 0.5 * _rmsnorm(h, g[1])
        lam_init = 0.8 - 0.6 * math.exp(-0.3 * l)
        h = _mixer(_rmsnorm(x, g[2]), mix_w_in[l], mix_w_out[l], da_lambda[l], da_subln_g[l],
                   lam_init, ml_conv_w[l], ml_conv_b[l], ml_gate_b[l], ml_norm_g[l])
        x = x + _rmsnorm(h, g[3])
        h = _swiglu(_rmsnorm(x, g[4]), ffn_w_in[l, 1], ffn_w_out[l, 1])
        x = x + 0.5 * _rmsnorm(h, g[5])
    return x


def setup_inputs(seed=0):
    out = dict(first_inputs(seed))
    for name, value in second_inputs(seed + 1).items():
        if name != "x":
            out[name + "_2"] = value
    return out


def reference(
    x, pool_norm, pool_w, pool_b, pool_scale, kv_in_norm, w_dkv, kv_norm, w_uk, w_uv, attn_norm,
    wq_down, q_norm, wq_up, wo, ffn_norm, router_group_w, router_group_b, router_expert_w,
    router_expert_b, w_gate, w_up, w_down, final_norm, ffn_w_in_2, ffn_w_out_2, norm_gains_2,
    mix_w_in_2, mix_w_out_2, da_lambda_2, da_subln_g_2, ml_conv_w_2, ml_conv_b_2, ml_gate_b_2,
    ml_norm_g_2,
):
    x = first_block(
        x, pool_norm, pool_w, pool_b, pool_scale, kv_in_norm, w_dkv, kv_norm, w_uk, w_uv,
        attn_norm, wq_down, q_norm, wq_up, wo, ffn_norm, router_group_w, router_group_b,
        router_expert_w, router_expert_b, w_gate, w_up, w_down, final_norm,
    )
    return second_block(
        x, ffn_w_in_2, ffn_w_out_2, norm_gains_2, mix_w_in_2, mix_w_out_2, da_lambda_2,
        da_subln_g_2, ml_conv_w_2, ml_conv_b_2, ml_gate_b_2, ml_norm_g_2,
    )


_drawn_inputs = setup_inputs


def setup_inputs(seed=0):
    import zlib

    import numpy as np

    out = dict(_drawn_inputs(seed))
    spreads = {}
    factors = {'kv_norm': 5.195, 'q_norm': 8.0, 'router_group_b': 5.728, 'ml_conv_b_2': 7.256}
    for name, (base, spread) in spreads.items():
        noise = np.random.default_rng([zlib.crc32(name.encode()), seed]).standard_normal(out[name].shape)
        drawn = base * np.exp(spread * noise) if base else spread * noise
        out[name] = __import__('jax').numpy.asarray(drawn.astype(out[name].dtype))
    for name, factor in factors.items():
        out[name] = (out[name] * factor).astype(out[name].dtype)
    return out
```

```python
import math
from contextlib import ExitStack

import numpy as np

import concourse.bass as bass
from concourse import mybir

F32 = mybir.dt.float32
U32 = mybir.dt.uint32
ALU = mybir.AluOpType
ACT = mybir.ActivationFunctionType
AX = mybir.AxisListType

EPS = 1e-6
NS = 6
SLOT = 4096
C = 32
CAP = 32
NEG = -1e30
BIG = 65536.0

VEC = {}
_o = 0
for _n, _w in [("pool_norm", 8), ("kv_in", 8), ("attn", 8), ("ffn0", 8), ("ffn1", 8),
               ("ng00", 8), ("ng02", 8), ("ng04", 8), ("ng10", 8), ("ng12", 8), ("ng14", 8),
               ("kv_norm", 2), ("q_norm", 3), ("yg0", 8), ("yg1", 8),
               ("cw0", 16), ("cw1", 16), ("cb0", 4), ("cb1", 4), ("gb0", 2), ("gb1", 2),
               ("rw0", 288), ("rw1", 288)]:
    VEC[_n] = (_o, _w)
    _o += _w
NVEC = _o
CST = {}
_o = 0
for _n, _w in [("ident", 128), ("tri", 128), ("ones", 128), ("caus", 128), ("mask", 384),
               ("cos", 256), ("sin", 256), ("iota", 32), ("sel", 512)]:
    CST[_n] = (_o, _w)
    _o += _w
NCST = _o
ROWS = {}
_o = 0
for _n, _w in [("pool_b", 1024), ("pool_scale", 1024), ("final", 1024), ("r0", 36), ("r1", 36),
               ("lam0", 256), ("lam1", 256), ("ng01", 1024), ("ng03", 1024), ("ng05", 1024),
               ("ng11", 1024), ("ng13", 1024), ("ng15", 1024)]:
    ROWS[_n] = (_o, _w)
    _o += _w
NROWS = _o
PLAN = ["pool", "moe0", "mla", "moe1", "fin", "ffn00", "mix0", "ffn01", "ffn10", "mix1", "ffn11"]


class Eng:

    def __init__(self, sem):
        self.sem, self.n, self.ops, self.seen = sem, 0, [], {}

    def wait(self, *toks):
        for t in toks:
            if t is None:
                continue
            if isinstance(t, list):
                self.wait(*t)
                continue
            sem, v = t
            if v > 0 and self.seen.get(sem.name, 0) < v:
                self.seen[sem.name] = v
                self.ops.append(lambda e, sem=sem, v=v: e.wait_ge(sem, v))

    def __call__(self, fn, *toks, sig=True):
        self.wait(*toks)
        if sig:
            self.n += 1
            self.ops.append(lambda e: fn(e).then_inc(self.sem, 1))
        else:
            self.ops.append(fn)
        return (self.sem, self.n)

    def last(self):
        return (self.sem, self.n)

    def play(self, e):
        for op in self.ops:
            op(e)


def build(nc, W, plan):
    ctx = ExitStack()
    with ctx:
        def sb(name, shape, dt=F32):
            return ctx.enter_context(nc.sbuf_tensor(name, shape, dt))

        def sem(name):
            return ctx.enter_context(nc.semaphore(name))

        RING = sb("RING", [128, NS, SLOT])
        X = sb("X", [128, 2, 1024])
        XS = sb("XS", [128, 2, 1024])
        HT = sb("HT", [128, 8, 256])
        CS = sb("CS", [128, NCST])
        VE = sb("VE", [128, NVEC])
        RB = sb("RB", [128, 3, 1024])
        RR = sb("RR", [128, 72])
        JK = sb("JK", [128, 1024])
        SM = sb("SM", [128, 512])
        MH = sb("MH", [128, 16])
        WK = sb("WK", [128, 12800])
        IX = sb("IX", [128, 32], U32)
        FLAG = sb("FLAG", [128, 2], U32)
        PS = ctx.enter_context(nc.psum_tensor("PS", [128, 8, 512], F32))

        pe, act, dve, pool, sp = (Eng(sem(n)) for n in ("s_pe", "s_act", "s_dve", "s_pool", "s_sp"))
        slot_sem = [sem(f"s_slot{i}") for i in range(NS)]

        def cs(name, p=128):
            o, w = CST[name]
            return CS[0:p, o:o + w]

        def ve(name):
            o, w = VEC[name]
            return VE[:, o:o + w]

        loads, freed, slot_n, breaks = [], {}, [0] * NS, {}

        def take(*parts):
            i = len(loads)
            s = i % NS
            view = RING[:, s, :]
            slot_n[s] += 16 * len(parts)
            loads.append((s, [(d(view), src) for d, src in parts]))
            return i, view, (slot_sem[s], slot_n[s])

        def give(i, tok):
            freed[i] = tok

        def dma_sem_load(name, dst, src, *toks):
            s = sem(name)
            act.wait(*toks)
            act.ops.append(lambda e: e.dma_start(dst, src).then_inc(s, 16))
            return (s, 16)

        def row(name, dst, *toks):
            o, w = ROWS[name]
            return dma_sem_load("d_" + name, dst, W["rows"][:, o:o + w].partition_broadcast(128)
                                if W["rows"].shape[0] != 1 else W["rows"][0:1, o:o + w].to_broadcast([128, w]), *toks)

        def barrier():
            for e in (pe, act, dve, pool):
                e.wait(*[o.last() for o in (pe, act, dve, pool)])

        def mm(out, lhsT, rhs, start, stop, *toks, sig=False):
            return pe(lambda e: e.matmul(out, lhsT, rhs, start=start, stop=stop), *toks, sig=sig)

        def tr(out, in_, p, *toks, sig=False):
            ident = CS[0:p, 0:p]
            return pe(lambda e: e.transpose(out, in_, ident), *toks, sig=sig)

        def ts(out, in0, s1, s2, o0, o1, *toks):
            if s2 is None:
                return dve(lambda e: e.tensor_scalar(out, in0, s1, None, o0), *toks)
            return dve(lambda e: e.tensor_scalar(out, in0, s1, s2, o0, o1), *toks)

        def tt(out, a, b, op, *toks):
            return dve(lambda e: e.tensor_tensor(out, a, b, op), *toks)

        def stt(out, a, s, b, o0, o1, *toks):
            return dve(lambda e: e.scalar_tensor_tensor(out, a, s, b, o0, o1), *toks)

        def av(out, in_, func, *toks, **kw):
            return act(lambda e: e.activation(out, in_, func, **kw), *toks)

        def cp(out, in_, *toks):
            return dve(lambda e: e.tensor_copy(out, in_), *toks)

        def rsq(out, ss, n, *toks):
            t = pool(lambda e: e.tensor_scalar(out, ss, 1.0 / n, EPS, ALU.mult, ALU.add), *toks)
            return pool(lambda e: e.tensor_tensor(out, out, MH[:, 0:out.shape[1]], ALU.pow), t)

        t_cs = dma_sem_load("d_cs", CS[:, :], W["cst"])
        t_ve = dma_sem_load("d_ve", VE[:, :], W["vec"])
        t_x = dma_sem_load("d_x", X[:, :, :], W["x"].rearrange("(b p) n -> p b n", p=128))
        t_r = [row("pool_b", RB[:, 0, :]), row("pool_scale", RB[:, 1, :]), row("final", RB[:, 2, :]),
               row("r0", RR[:, 0:36]), row("r1", RR[:, 36:72])]
        for e in (pe, act, dve, pool):
            e.wait(t_cs, t_ve, t_x, *t_r)

        pool(lambda e: e.memset(MH[:, :], -0.5))
        pool.wait(pool.last())

        def norm_xs(src=None):
            ss, rs = SM[:, 0:2], SM[:, 2:4]
            t0 = av(JK[:, :], X[:, 0, :], ACT.Square, accum_out=ss[:, 0:1])
            t1 = av(JK[:, :], X[:, 1, :], ACT.Square, t0, accum_out=ss[:, 1:2])
            t = rsq(rs, ss, 1024, t1)
            a = ts(XS[:, 0, :], X[:, 0, :], rs[:, 0:1], None, ALU.mult, None, t)
            b = av(XS[:, 1, :], X[:, 1, :], ACT.Copy, t, scale=rs[:, 1:2])
            return [a, b]

        def transposed(outs, src, toks, banks=(0, 1, 2, 3), nch=8, free=None):
            res = []
            for j in range(nch // 2):
                bk = banks[j]
                for cc in range(2):
                    c = 2 * j + cc
                    for b in range(2):
                        t = tr(PS[:, bk, cc * 256 + b * 128:cc * 256 + b * 128 + 128],
                               src[:, b, c * 128:c * 128 + 128], 128, toks, sig=(cc + b == 2))
                got = []
                for gain, dst in outs:
                    if j % 2 == 0:
                        got.append(tt(dst[:, 2 * j:2 * j + 2, :], PS[:, bk, :].rearrange("p (c n) -> p c n", c=2),
                                      gain[:, 2 * j:2 * j + 2].unsqueeze(2).to_broadcast([128, 2, 256]),
                                      ALU.mult, t))
                    else:
                        for cc in range(2):
                            c = 2 * j + cc
                            got.append(av(dst[:, c, :], PS[:, bk, cc * 256:cc * 256 + 256], ACT.Copy, t,
                                          scale=gain[:, c:c + 1]))
                res += got
            return res

        def post_norm(banks, rowv, half, toks):
            ss, rs = SM[:, 4:6], SM[:, 6:8]
            for b in range(2):
                t = av(JK[:, :].rearrange("p (a n) -> p a n", a=2), PS[:, banks[b]:banks[b] + 2, :], ACT.Square,
                       toks, act.last(), accum_out=ss[:, b:b + 1])
            t = rsq(rs, ss, 1024, t)
            if half != 1.0:
                t = ts(rs, rs, half, None, ALU.mult, None, t)
            for b in range(2):
                j = JK[:, :] if b else XS[:, 0, :]
                t1 = stt(j.rearrange("p (a n) -> p a n", a=2), PS[:, banks[b]:banks[b] + 2, :], rs[:, b:b + 1],
                         rowv.rearrange("p (a n) -> p a n", a=2), ALU.mult, ALU.mult, t)
                tt(X[:, b, :], X[:, b, :], j, ALU.add, t1)

        def stage_pool():
            i, v, tw = take((lambda v: v[:, 0:2048], W["pm"]),
                            (lambda v: v[:, 2048:4096].rearrange("p (a d) -> p a d", a=8),
                             W["pool_w"][0].rearrange("g (cc p) d -> p (g cc) d", p=128)))
            M = v[:, 0:2048].rearrange("p (b g t) -> p b g t", b=2, g=4)
            PW = v[:, 2048:4096].rearrange("p (a d) -> p a d", a=8)
            tx = norm_xs()
            pg = ve("pool_norm")
            for g in range(4):
                for cc in range(2):
                    c = 2 * g + cc
                    for b in range(2):
                        t = mm(PS[:, g, cc * 256:cc * 256 + 256], XS[:, b, c * 128:c * 128 + 128], M[:, b, g, :],
                               b == 0, b == 1, tx, tw, sig=(b == 1))
                te = tt(HT[:, 2 * g:2 * g + 2, :], PS[:, g, :].rearrange("p (c n) -> p c n", c=2),
                        pg[:, 2 * g:2 * g + 2].unsqueeze(2).to_broadcast([128, 2, 256]), ALU.mult, t)
                for b in range(2):
                    o = PS[:, 4 + 2 * b + g // 2, (g % 2) * 256:(g % 2) * 256 + 256]
                    for cc in range(2):
                        t = mm(o, HT[:, 2 * g + cc, b * 128:b * 128 + 128], PW[:, 2 * g + cc, :], cc == 0, cc == 1, te,
                               sig=(cc == 1))
            give(i, t)
            for b in range(2):
                j = JK[:, :].rearrange("p (a n) -> p a n", a=2)
                t1 = tt(j, PS[:, 4 + 2 * b:6 + 2 * b, :], RB[:, 0, :].rearrange("p (a n) -> p a n", a=2), ALU.add,
                        t, dve.last())
                t1 = tt(JK[:, :], JK[:, :], RB[:, 1, :], ALU.mult, t1)
                tt(X[:, b, :], X[:, b, :], JK[:, :], ALU.add, t1)

        def stage_moe(l):
            tx = norm_xs()
            gain = ve(f"ffn{l}")
            th = transposed([(gain, HT)], XS, tx)
            rw = ve(f"rw{l}").rearrange("p (c n) -> p c n", c=8)
            for b in range(2):
                for c in range(8):
                    t = mm(PS[:, 4, b * 36:b * 36 + 36], HT[:, c, b * 128:b * 128 + 128], rw[:, c, :], c == 0, c == 7,
                           th, sig=(c == 7))
            w = [0]

            def al(n):
                w[0] += n
                return WK[:, w[0] - n:w[0]]
            S = al(2048).rearrange("p (b n) -> p b n", b=2)
            G = al(2048).rearrange("p (b n) -> p b n", b=2)
            XE = al(2048).rearrange("p (k c n) -> p k c n", k=2, c=8)
            GT = al(512).rearrange("p (k n) -> p k n", k=2)
            HG = al(512).rearrange("p (k n) -> p k n", k=4)
            HE = al(256).rearrange("p (k n) -> p k n", k=2)
            Y = al(1024)
            L = al(72).rearrange("p (b n) -> p b n", b=2)
            G8 = al(16).rearrange("p (b n) -> p b n", b=2)
            M8 = al(16).rearrange("p (b n) -> p b n", b=2)
            V8 = al(16).rearrange("p (b n) -> p b n", b=2)
            E8 = al(16).rearrange("p (b n) -> p b n", b=2)
            T4 = al(64).rearrange("p (b g e) -> p b g e", b=2, g=4)
            OH = al(8).rearrange("p (b n) -> p b n", b=2)
            IG = al(2)
            IE = al(4).rearrange("p (b n) -> p b n", b=2)
            NM, SG, GP, DD, EE, W1, W2 = (al(2) for _ in range(7))
            A1, A2, A, GM, PO = (al(64).rearrange("p (b n) -> p b n", b=2) for _ in range(5))
            io = cs("iota")
            t = tt(L, PS[:, 4, 0:72].rearrange("p (b n) -> p b n", b=2),
                   RR[:, 36 * l:36 * l + 36].unsqueeze(1).to_broadcast([128, 2, 36]), ALU.add, t)
            t8 = dve(lambda e: e.memset(G8, -3e38))
            t = cp(G8[:, :, 0:4], L[:, :, 0:4], t, t8)
            for b in range(2):
                ta = dve(lambda e, b=b: e.max(M8[:, b, :], G8[:, b, :]), t)
                ta = dve(lambda e, b=b: e.max_index(IX[:, b * 8:b * 8 + 8], M8[:, b, :], G8[:, b, :]), ta)
            tg = cp(IG, IX[:, 0:16].rearrange("p (b n) -> p b n", b=2)[:, :, 0], ta)
            tn = ts(NM, M8[:, :, 0], -1.0, None, ALU.mult, None, ta)
            for b in range(2):
                te = av(SM[:, 16 + 4 * b:20 + 4 * b], L[:, b, 0:4], ACT.Exp, tn, bias=NM[:, b:b + 1],
                        accum_out=SG[:, b:b + 1])
            tp = dve(lambda e: e.reciprocal(GP, SG), te)
            t = tt(OH, io[:, 0:4].unsqueeze(1).to_broadcast([128, 2, 4]), IG.unsqueeze(2).to_broadcast([128, 2, 4]),
                   ALU.is_equal, tg)
            t = tt(T4, L[:, :, 4:36].rearrange("p b (g e) -> p b g e", g=4),
                   OH.unsqueeze(3).to_broadcast([128, 2, 4, 8]), ALU.mult, t)
            for b in range(2):
                t = dve(lambda e, b=b: e.tensor_reduce(E8[:, b, :], T4[:, b, :, :].rearrange("p g e -> p e g"), AX.X,
                                                       ALU.add), t)
            for b in range(2):
                ta = dve(lambda e, b=b: e.max(V8[:, b, :], E8[:, b, :]), t)
                ta = dve(lambda e, b=b: e.max_index(IX[:, 16 + b * 8:24 + b * 8], V8[:, b, :], E8[:, b, :]), ta)
            t = cp(IE, IX[:, 16:32].rearrange("p (b n) -> p b n", b=2)[:, :, 0:2], ta)
            t = stt(IE, IG.unsqueeze(2).to_broadcast([128, 2, 2]), 8.0, IE, ALU.mult, ALU.add, t)
            td = tt(DD, V8[:, :, 1], V8[:, :, 0], ALU.subtract, ta)
            td = av(EE, DD, ACT.Exp, td)
            t1 = ts(W1, EE, 1.0, None, ALU.add, None, td)
            t1 = dve(lambda e: e.reciprocal(W1, W1), t1)
            t1 = tt(W1, W1, GP, ALU.mult, t1, tp)
            t1 = tt(W2, W1, EE, ALU.mult, t1)
            i32 = io.unsqueeze(1).to_broadcast([128, 2, 32])
            ta = tt(A1, i32, IE[:, :, 0:1].to_broadcast([128, 2, 32]), ALU.is_equal, t)
            tb = tt(A2, i32, IE[:, :, 1:2].to_broadcast([128, 2, 32]), ALU.is_equal, t)
            tA = tt(A, A1, A2, ALU.add, tb)
            ta = tt(A1, A1, W1.unsqueeze(2).to_broadcast([128, 2, 32]), ALU.mult, tA, t1)
            tb = tt(A2, A2, W2.unsqueeze(2).to_broadcast([128, 2, 32]), ALU.mult, tA, t1)
            tG = tt(GM, A1, A2, ALU.add, ta, tb)
            mm(PS[:, 5, 0:32], cs("tri"), A[:, 0, :], True, True, tA)
            mm(PS[:, 5, 32:64], cs("ones"), A[:, 0, :], True, False)
            mm(PS[:, 5, 32:64], cs("tri"), A[:, 1, :], False, True)
            mm(PS[:, 5, 64:96], cs("ones"), A[:, 0, :], True, False)
            tq = mm(PS[:, 5, 64:96], cs("ones"), A[:, 1, :], False, True, sig=True)
            t = ts(PO, A, -BIG, BIG, ALU.mult, ALU.add, tA)
            t = tt(PO, PO, PS[:, 5, 0:64].rearrange("p (b n) -> p b n", b=2), ALU.add, t, tq)
            GO = SM[:, 128:192].rearrange("p (b n) -> p b n", b=2)
            t1 = ts(GO, PO, float(CAP), None, ALU.is_ge, None, t)
            tGO = tt(GO, GO, GM, ALU.mult, t1, tG)
            t1 = dve(lambda e: e.tensor_reduce(SM[:, 192:193], PS[:, 5, 64:96], AX.X, ALU.max), tq)
            t1 = ts(SM[:, 192:193], SM[:, 192:193], float(CAP), None, ALU.is_gt, None, t1)
            flag = FLAG[0:1, l:l + 1]
            tflag = cp(FLAG[:, l:l + 1], SM[:, 192:193], t1)
            if CAP < C:
                t1 = ts(A1, PO, float(CAP), BIG, ALU.is_ge, ALU.mult, t, tG)
                t = tt(PO, PO, A1, ALU.add, t1, tGO)
            for b in range(2):
                t1 = tt(S[:, b, :].rearrange("p (e s) -> p e s", e=32), io[:, 0:C].unsqueeze(1).to_broadcast([128, 32, C]),
                        PO[:, b, :].unsqueeze(2).to_broadcast([128, 32, C]), ALU.is_equal, t)
                tS = tt(G[:, b, :].rearrange("p (e s) -> p e s", e=32), S[:, b, :].rearrange("p (e s) -> p e s", e=32),
                        GM[:, b, :].unsqueeze(2).to_broadcast([128, 32, C]), ALU.mult, t1, tG)
            barrier()
            wd = W["w_down"][l]
            sl = {}

            def load_gu(e):
                for k in ("w_gate", "w_up"):
                    sl[k, e] = take((lambda v: v.rearrange("p (c n) -> p c n", c=8),
                                     W[k][l, e].rearrange("(c p) n -> p c n", p=128)))

            def load_d(e):
                sl["d", e] = take((lambda v: v.rearrange("p (c n) -> p c n", c=4),
                                   wd[e].rearrange("(c p) n -> p c n", p=128)))
            bank = {k: None for k in range(8)}
            hg, he, ga, gt = {}, {}, {}, {}

            def gather(g):
                for r in range(2):
                    bk = 2 + r
                    for c in range(4):
                        for b in range(2):
                            t = mm(PS[:, bk, c * 128:c * 128 + 128],
                                   XS[:, b, (4 * r + c) * 128:(4 * r + c) * 128 + 128], S[:, b, g * 128:g * 128 + 128],
                                   b == 0, b == 1, bank[bk], sig=(c == 3 and b == 1))
                    old = ga.get(g - 2)
                    bank[bk] = ga[g] = tt(XE[:, g % 2, 4 * r:4 * r + 4, :], PS[:, bk, :].rearrange("p (c n) -> p c n", c=4),
                                          gain[:, 4 * r:4 * r + 4].unsqueeze(2).to_broadcast([128, 4, 128]), ALU.mult,
                                          t, last_gu.get(4 * (g - 2) + 3))
                for b in range(2):
                    t = tr(PS[:, 3, b * 128:b * 128 + 128], G[:, b, g * 128:g * 128 + 128], 128, bank[3], sig=(b == 1))
                bank[3] = gt[g] = av(GT[:, g % 2, :], PS[:, 3, 0:256], ACT.Copy, t, comb.get(g - 2))
            last_gu, comb = {}, {}

            def gateup(e):
                g, j = divmod(e, 4)
                pb = e % 2
                for n, k in enumerate(("w_gate", "w_up")):
                    i, v, tw = sl[k, e]
                    v = v.rearrange("p (c n) -> p c n", c=8)
                    for c in range(8):
                        for q in range(4):
                            t = mm(PS[32 * q:32 * q + 32, pb, n * 128:n * 128 + 128],
                                   XE[:, g % 2, c, 32 * j:32 * j + 32], v[:, c, 128 * q:128 * q + 128], c == 0, c == 7,
                                   tw, ga[g], bank[pb], sig=(c == 7 and q == 3))
                    give(i, t)
                ta = av(HG[:, pb, :], PS[:, pb, 0:128], ACT.Silu, t, hg.get(e - 2))
                last_gu[e] = t
                hg[e] = bank[pb] = tt(HG[:, 2 + pb, :], HG[:, pb, :], PS[:, pb, 128:256], ALU.mult, t, ta, he.get(e - 2))

            def down(e):
                g, j = divmod(e, 4)
                pb = e % 2
                t = tr(PS[:, 3, 0:128], HG[:, 2 + pb, :], 128, hg[e], bank[3], sig=True)
                he[e] = bank[3] = cp(HE[:, pb, :], PS[:, 3, 0:128], t, dn.get(e - 2))
                i, v, tw = sl["d", e]
                v = v.rearrange("p (c n) -> p c n", c=4)
                for h in range(2):
                    for c in range(4):
                        t = mm(PS[32 * j:32 * j + 32, 4 + h, :], HE[:, pb, 32 * c:32 * c + 32],
                               v[:, c, 512 * h:512 * h + 512], c == 0, c == 3, tw, he[e],
                               bank[4 + h] if j == 0 else None, sig=(c == 3))
                dn[e] = t
                give(i, t)
                if j == 3:
                    a = av(Y[:, 0:512], PS[:, 4, :], ACT.Copy, t, comb.get(g - 1))
                    d = cp(Y[:, 512:1024], PS[:, 5, :], t, comb.get(g - 1))
                    bank[4], bank[5] = a, d
                    ydone[g] = [a, d]
            dn, ydone = {}, {}

            def combine(g):
                for b in range(2):
                    for h in range(2):
                        t = mm(PS[:, 6 + h, :], GT[:, g % 2, b * 128:b * 128 + 128], Y[:, h * 512:h * 512 + 512], True,
                               True, ydone[g], gt[g], bank[6 + h], sig=True)
                        bank[6 + h] = tt(X[:, b, h * 512:h * 512 + 512], X[:, b, h * 512:h * 512 + 512],
                                         PS[:, 6 + h, :], ALU.add, t)
                comb[g] = t

            for e in range(33):
                if e < 32:
                    if e % 4 == 0:
                        gather(e // 4)
                    load_gu(e)
                    gateup(e)
                if e >= 1:
                    load_d(e - 1)
                    down(e - 1)
                    if (e - 1) % 4 == 0 and e > 1:
                        combine((e - 1) // 4 - 1)
            combine(7)
            overflow(l, GO, flag, tflag)

        def overflow(l, GO, flag, tflag):
            names = ("pe", "act", "dve", "sp")
            o = {n: Eng(sem(f"o_{n}{l}")) for n in names}
            lds = [sem(f"o_ld{l}{k}") for k in range(2)]
            outer = {"pe": pe, "act": act, "dve": dve}
            begun = [x.last() for x in outer.values()]
            for x in o.values():
                x.wait(*begun)
            BUF = [WK[:, 6144 * k:6144 * k + 6144] for k in range(2)]
            HFO = WK[:, 12288:12800].rearrange("p (f n) -> p f n", f=2)
            GS = JK[:, 0:512].rearrange("p (f n) -> p f n", f=2)
            used, tsilu, thf, tadd, tdown = {}, {}, {}, {}, {}
            for n in range(64):
                e, hf = divmod(n, 2)
                k = n % 2
                wg, wu, wd = (BUF[k][:, 2048 * z:2048 * z + 2048] for z in range(3))
                o["sp"].wait(used.get(n - 2))
                for dst, src in ((wg, W["w_gate"][l, e][:, 256 * hf:256 * hf + 256]),
                                 (wu, W["w_up"][l, e][:, 256 * hf:256 * hf + 256]),
                                 (wd, W["w_down"][l, e][256 * hf:256 * hf + 256, :])):
                    m = 2 if dst is wd else 8
                    o["sp"].ops.append(lambda g, dst=dst, src=src, k=k, m=m: g.dma_start(
                        dst.rearrange("p (c n) -> p c n", c=m), src.rearrange("(c p) n -> p c n", p=128)
                    ).then_inc(lds[k], 16))
                tl = (lds[k], 48 * (n // 2 + 1))
                gv, uv = (z.rearrange("p (c n) -> p c n", c=8) for z in (wg, wu))
                dv = wd.rearrange("p (c n) -> p c n", c=2)
                for f in range(2):
                    for z, v in enumerate((gv, uv)):
                        for c in range(8):
                            t = o["pe"](lambda g, f=f, z=z, v=v, c=c: g.matmul(
                                PS[:, f, z * 256:z * 256 + 256], v[:, c, f * 128:f * 128 + 128], HT[:, c, :],
                                start=c == 0, stop=c == 7), tl, thf.get((n - 1, f)), sig=(c == 7))
                    ta = o["act"](lambda g, f=f: g.activation(GS[:, f, :], PS[:, f, 0:256], ACT.Silu), t,
                                  thf.get((n - 1, f)))
                    thf[n, f] = o["dve"](lambda g, f=f: g.tensor_tensor(HFO[:, f, :], GS[:, f, :], PS[:, f, 256:512],
                                                                        ALU.mult), t, ta, tdown.get(n - 1))
                for f in range(2):
                    for b in range(2):
                        for h in range(2):
                            tdown[n] = used[n] = o["pe"](lambda g, f=f, b=b, h=h, dv=dv, hf=hf: g.matmul(
                                PS[:, 4 + 2 * b + h, :], HFO[:, f, b * 128:b * 128 + 128], dv[:, f, h * 512:h * 512 + 512],
                                start=(f == 0 and hf == 0), stop=(f == 1 and hf == 1)), thf[n, 1],
                                tadd.get(e - 1), sig=(b + h == 2))
                if hf == 1:
                    for b in range(2):
                        xv = X[:, b, :].rearrange("p (a n) -> p a n", a=2)
                        tadd[e] = o["dve"](lambda g, b=b, xv=xv, e=e: g.scalar_tensor_tensor(
                            xv, PS[:, 4 + 2 * b:6 + 2 * b, :], GO[:, b, e:e + 1], xv, ALU.mult, ALU.add), tdown[n],
                            tadd.get(e - 1))
            done = [o[n].last() for n in ("pe", "act", "dve")]
            for x in o.values():
                x.wait(*done)

            def enter(g, inner):
                v = g.value_load(flag, min_val=0, max_val=1)
                with g.If(v > 0):
                    inner.play(g)
            for n, x in outer.items():
                x.wait(tflag)
                x.ops.append(lambda g, n=n: enter(g, o[n]))
            breaks[len(loads)] = (tflag, lambda g: enter(g, o["sp"]))

        def stage_fin():
            tx = norm_xs()
            for b in range(2):
                tt(X[:, b, :], XS[:, b, :], RB[:, 2, :], ALU.mult, tx)

        def stage_ffn(l, k):
            rt = row(f"ng{l}{1 if k == 0 else 5}", RB[:, k, :], dve.last())
            tx = norm_xs()
            th = transposed([(ve(f"ng{l}{0 if k == 0 else 4}"), HT)], XS, tx)
            HF = WK[:, 0:22 * 256].rearrange("p (f n) -> p f n", f=22)
            GS = WK[:, 5632:5632 + 512].rearrange("p (k n) -> p k n", k=2)
            win, wout = W["ffn_w_in"][l, k], W["ffn_w_out"][l, k]
            bank = {bk: None for bk in range(8)}
            gs = {}
            hf = None
            for s in range(6):
                wdt = 512 if s < 5 else 256

                def cols(o, w):
                    return win[:, o:o + w].rearrange("(c p) n -> p c n", p=128)
                if s < 5:
                    sg = take((lambda v: v.rearrange("p (c n) -> p c n", c=8), cols(512 * s, 512)))
                    su = take((lambda v: v.rearrange("p (c n) -> p c n", c=8), cols(2816 + 512 * s, 512)))
                else:
                    sg = take((lambda v: v[:, 0:2048].rearrange("p (c n) -> p c n", c=8), cols(2560, 256)),
                              (lambda v: v[:, 2048:4096].rearrange("p (c n) -> p c n", c=8), cols(5376, 256)))
                    su = sg
                gv = sg[1] if s < 5 else sg[1][:, 0:2048]
                uv = su[1] if s < 5 else sg[1][:, 2048:4096]
                gv, uv = (z.rearrange("p (c n) -> p c n", c=8) for z in (gv, uv))
                for fq in range(wdt // 128):
                    f = 4 * s + fq
                    bk = 4 + f % 4
                    for n, (v, tw) in enumerate(((gv, sg[2]), (uv, su[2]))):
                        for c in range(8):
                            t = mm(PS[:, bk, n * 256:n * 256 + 256], v[:, c, fq * 128:fq * 128 + 128], HT[:, c, :],
                                   c == 0, c == 7, tw, th, bank[bk], sig=(c == 7))
                        if n == 0:
                            tgate = t
                    ta = av(GS[:, f % 2, :], PS[:, bk, 0:256], ACT.Silu, t, gs.get(f - 2))
                    gs[f] = bank[bk] = hf = tt(HF[:, f, :], GS[:, f % 2, :], PS[:, bk, 256:512], ALU.mult, t, ta)
                if su is not sg:
                    give(sg[0], tgate)
                give(su[0], t)
            barrier()
            for s in range(6):
                n = 4 if s < 5 else 2
                i, v, tw = take((lambda v, n=n: v[:, 0:1024 * n].rearrange("p (c n) -> p c n", c=n),
                                 wout[512 * s:512 * s + 128 * n, :].rearrange("(c p) n -> p c n", p=128)))
                v = v.rearrange("p (c n) -> p c n", c=4)
                for c in range(n):
                    f = 4 * s + c
                    for b in range(2):
                        for h in range(2):
                            t = mm(PS[:, 2 * b + h, :], HF[:, f, b * 128:b * 128 + 128], v[:, c, h * 512:h * 512 + 512],
                                   f == 0, f == 21, tw, gs[f], sig=(b + h == 2))
                give(i, t)
            dve.wait(rt)
            post_norm((0, 2), RB[:, k, :], 0.5, [t])

        def banks_pool(ids):
            return {"ids": list(ids), "at": 0, "tok": {i: None for i in ids}}

        def nb(bp):
            i = bp["ids"][bp["at"] % len(bp["ids"])]
            bp["at"] += 1
            return i

        def stage_mla():
            w = [0]

            def al(n):
                w[0] += n
                assert w[0] <= 12800
                return WK[:, w[0] - n:w[0]]
            QN = al(2048).rearrange("p (h n) -> p h n", h=8)
            HK = QN
            KN = al(2048).rearrange("p (h n) -> p h n", h=8)
            V = al(2048).rearrange("p (b n) -> p b n", b=2)
            QR = al(1024).rearrange("p (h n) -> p h n", h=4)
            CKT = al(512).rearrange("p (c n) -> p c n", c=2)
            CQT = al(768).rearrange("p (c n) -> p c n", c=3)
            CKX = al(512).rearrange("p (b n) -> p b n", b=2)
            CQX = al(768).rearrange("p (b n) -> p b n", b=2)
            KR = al(256)
            P = al(768).rearrange("p (k n) -> p k n", k=2)
            PT = al(768).rearrange("p (k n) -> p k n", k=2)
            T1, T2 = al(256), al(256)
            cos, sin = cs("cos"), cs("sin")
            tx = norm_xs()
            th = transposed([(ve("attn"), HT), (ve("kv_in"), HK)], XS, tx)
            ik, v, tw = take((lambda v: v[:, 0:2560].rearrange("p (c n) -> p c n", c=8),
                              W["w_dkv"].rearrange("(c p) n -> p c n", p=128)))
            wk = v[:, 0:2560].rearrange("p (c n) -> p c n", c=8)
            iq, vq, twq = take((lambda v: v[:, 0:3072].rearrange("p (c n) -> p c n", c=8),
                                W["wq_down"][0].rearrange("(c p) n -> p c n", p=128)))
            wq = vq[:, 0:3072].rearrange("p (c n) -> p c n", c=8)
            for b in range(2):
                for c in range(8):
                    tk = mm(PS[:, 4, b * 256:b * 256 + 256], HK[:, c, b * 128:b * 128 + 128], wk[:, c, 0:256], c == 0,
                            c == 7, tw, th, sig=(c == 7))
            for c in range(8):
                for d in range(2):
                    mm(PS[64 * d:64 * d + 64, 5, 0:256], wk[:, c, 256:320], HK[:, c, :], c == 0, c == 7)
            for c in range(8):
                for d in range(4):
                    o = 288 if d % 2 == 0 else 256
                    tr_ = mm(PS[32 * d:32 * d + 32, 5, 256:512], wk[:, c, o:o + 32], HK[:, c, :], c == 0, c == 7,
                             sig=(c == 7 and d == 3))
            give(ik, tr_)
            for b in range(2):
                for c in range(8):
                    tq = mm(PS[:, 6 + b, 0:384], HT[:, c, b * 128:b * 128 + 128], wq[:, c, :], c == 0, c == 7, twq,
                            sig=(c == 7))
            give(iq, tq)
            ss, rs = SM[:, 8:12], SM[:, 12:16]
            for b in range(2):
                av(JK[:, 0:256], PS[:, 4, b * 256:b * 256 + 256], ACT.Square, tk, act.last(), accum_out=ss[:, b:b + 1])
            for b in range(2):
                av(JK[:, 0:384], PS[:, 6 + b, 0:384], ACT.Square, tq, act.last(), accum_out=ss[:, 2 + b:3 + b])
            t1 = rsq(rs[:, 0:2], ss[:, 0:2], 256, act.last())
            t2 = rsq(rs[:, 2:4], ss[:, 2:4], 384, act.last())
            for b in range(2):
                ta = ts(CKX[:, b, :], PS[:, 4, b * 256:b * 256 + 256], rs[:, b:b + 1], None, ALU.mult, None, t1)
                tb = av(CQX[:, b, :], PS[:, 6 + b, 0:384], ACT.Copy, t2, scale=rs[:, 2 + b:3 + b])
            t3 = tt(T1, PS[:, 5, 0:256], cos, ALU.mult, tr_)
            t4 = tt(T2, PS[:, 5, 256:512], sin, ALU.mult, tr_)
            tkr = tt(KR, T1, T2, ALU.add, t3, t4)
            for c in range(2):
                for b in range(2):
                    t = tr(PS[:, 0, c * 256 + b * 128:c * 256 + b * 128 + 128], CKX[:, b, c * 128:c * 128 + 128], 128,
                           ta, sig=(b + c == 2))
            tck = tt(CKT, PS[:, 0, :].rearrange("p (c n) -> p c n", c=2),
                     ve("kv_norm").unsqueeze(2).to_broadcast([128, 2, 256]), ALU.mult, t)
            for c in range(3):
                for b in range(2):
                    t = tr(PS[:, 1 + c // 2, (c % 2) * 256 + b * 128:(c % 2) * 256 + b * 128 + 128],
                           CQX[:, b, c * 128:c * 128 + 128], 128, tb, sig=(b == 1))
            for c in range(3):
                tcq = ts(CQT[:, c, :], PS[:, 1 + c // 2, (c % 2) * 256:(c % 2) * 256 + 256], ve("q_norm")[:, c:c + 1],
                         None, ALU.mult, None, t)
            barrier()
            bp = banks_pool(range(8))
            iu, vu, tu = take((lambda v: v[:, 0:2048].rearrange("p (c n) -> p c n", c=2),
                               W["w_uk"].rearrange("(c p) n -> p c n", p=128)),
                              (lambda v: v[:, 2048:4096].rearrange("p (c n) -> p c n", c=2),
                               W["w_uv"].rearrange("(c p) n -> p c n", p=128)))
            uk = vu[:, 0:2048].rearrange("p (c n) -> p c n", c=2)
            uv = vu[:, 2048:4096].rearrange("p (c n) -> p c n", c=2)
            for h in range(8):
                if h % 2 == 0:
                    bk = nb(bp)
                for c in range(2):
                    t = mm(PS[:, bk, (h % 2) * 256:(h % 2) * 256 + 256], uk[:, c, h * 128:h * 128 + 128], CKT[:, c, :],
                           c == 0, c == 1, tu, bp["tok"][bk], sig=(c == 1))
                if h % 2 == 1:
                    bp["tok"][bk] = cp(KN[:, h - 1:h + 1, :], PS[:, bk, :].rearrange("p (h n) -> p h n", h=2), t)
            for b in range(2):
                for hf in range(2):
                    bk = nb(bp)
                    for c in range(2):
                        t = mm(PS[:, bk, :], CKT[:, c, b * 128:b * 128 + 128], uv[:, c, hf * 512:hf * 512 + 512], c == 0,
                               c == 1, bp["tok"][bk], sig=(c == 1))
                    bp["tok"][bk] = av(V[:, b, hf * 512:hf * 512 + 512], PS[:, bk, :], ACT.Copy, t)
            give(iu, t)
            for q in range(2):
                i, v, tw = take((lambda v: v[:, 0:2304].rearrange("p (c n) -> p c n", c=3),
                                 W["wq_up"][0][:, q * 768:q * 768 + 768].rearrange("(c p) n -> p c n", p=128)))
                v = v[:, 0:2304].rearrange("p (c n) -> p c n", c=3)
                for hh in range(4):
                    h = 4 * q + hh
                    if h % 2 == 0:
                        bk = nb(bp)
                    for c in range(3):
                        t = mm(PS[:, bk, (h % 2) * 256:(h % 2) * 256 + 256], v[:, c, hh * 192:hh * 192 + 128],
                               CQT[:, c, :], c == 0, c == 2, tw, bp["tok"][bk], sig=(c == 2))
                    if h % 2 == 1:
                        bp["tok"][bk] = av(QN[:, h - 1:h + 1, :], PS[:, bk, :].rearrange("p (h n) -> p h n", h=2),
                                           ACT.Copy, t)
                for pr in range(2):
                    bk = nb(bp)
                    for c in range(3):
                        for d in range(2):
                            o = (2 * pr + d) * 192 + 128
                            mm(PS[64 * d:64 * d + 64, bk, 0:256], v[:, c, o:o + 64], CQT[:, c, :], c == 0, c == 2,
                               bp["tok"][bk])
                    for c in range(3):
                        for d in range(4):
                            o = (2 * pr + d // 2) * 192 + 128 + (32 if d % 2 == 0 else 0)
                            t = mm(PS[32 * d:32 * d + 32, bk, 256:512], v[:, c, o:o + 32], CQT[:, c, :], c == 0, c == 2,
                                   sig=(c == 2 and d == 3))
                    t3 = tt(T1, PS[:, bk, 0:256], cos, ALU.mult, t, dve.last())
                    bp["tok"][bk] = t4 = tt(T2, PS[:, bk, 256:512], sin, ALU.mult, t)
                    tt(QR[:, 2 * q + pr, :], T1, T2, ALU.add, t3, t4)
                give(i, t)
            barrier()
            OT = HT
            scale = 1.0 / math.sqrt(192.0)
            mask = cs("mask")
            pt, pv, prob = {}, {}, {}
            bt = {bk: None for bk in range(8)}

            def scores(h):
                bk = h % 2
                pr, dp = h // 2, 64 * (h % 2)
                for i in range(2):
                    o = PS[:, bk, 0:128] if i == 0 else PS[:, bk, 128:384]
                    n = 128 + 128 * i
                    mm(o, QN[:, h, i * 128:i * 128 + 128], KN[:, h, 0:n], True, False, bt[bk])
                    t = mm(o, QR[dp:dp + 64, pr, i * 128:i * 128 + 128], KR[dp:dp + 64, 0:n], False, True, sig=True)
                p = P[:, h % 2, :]
                bt[bk] = t = stt(p, PS[:, bk, 0:384], scale, mask, ALU.mult, ALU.add, t, prob.get(h - 2))
                m, s = SM[:, 32 + 2 * (h % 2):34 + 2 * (h % 2)], SM[:, 40 + 2 * (h % 2):42 + 2 * (h % 2)]
                for i, (a, z) in enumerate(((0, 128), (128, 384))):
                    tm = dve(lambda e, i=i, a=a, z=z: e.tensor_reduce(m[:, i:i + 1], p[:, a:z], AX.X, ALU.max,
                                                                      negate=True), t)
                for i, (a, z) in enumerate(((0, 128), (128, 384))):
                    te = av(p[:, a:z], p[:, a:z], ACT.Exp, tm, bias=m[:, i:i + 1], accum_out=s[:, i:i + 1])
                tr1 = dve(lambda e: e.reciprocal(s, s), te)
                for i, (a, z) in enumerate(((0, 128), (128, 384))):
                    pt[h] = ts(p[:, a:z], p[:, a:z], s[:, i:i + 1], None, ALU.mult, None, tr1)

            def values(h):
                bk = 2 + h % 2
                p = P[:, h % 2, :]
                for j in range(3):
                    t = tr(PS[:, bk, j * 128:j * 128 + 128], p[:, j * 128:j * 128 + 128], 128, pt[h], bt[bk],
                           sig=(j == 2))
                prob[h] = t
                bt[bk] = t = av(PT[:, h % 2, :], PS[:, bk, 0:384], ACT.Copy, t, pv.get(h - 2))
                q = PT[:, h % 2, :]
                bo = 4 + h % 2
                v0, v1 = V[:, 0, h * 128:h * 128 + 128], V[:, 1, h * 128:h * 128 + 128]
                mm(PS[:, bo, 0:128], v0, q[:, 0:128], True, True, t, bt[bo])
                mm(PS[:, bo, 128:256], v0, q[:, 128:256], True, False)
                pv[h] = mm(PS[:, bo, 128:256], v1, q[:, 256:384], False, True, sig=True)
                bt[bo] = cp(OT[:, h, :], PS[:, bo, 0:256], pv[h])
            for h in range(9):
                if h < 8:
                    scores(h)
                if h:
                    values(h - 1)
            barrier()
            out_proj(W["wo"][0], OT)
            for b in range(2):
                tt(X[:, b, :].rearrange("p (a n) -> p a n", a=2), X[:, b, :].rearrange("p (a n) -> p a n", a=2),
                   PS[:, 2 * b:2 * b + 2, :], ALU.add, pe.last())

        def out_proj(w, src):
            for s in range(2):
                i, v, tw = take((lambda v: v.rearrange("p (c n) -> p c n", c=4),
                                 w[512 * s:512 * s + 512, :].rearrange("(c p) n -> p c n", p=128)))
                v = v.rearrange("p (c n) -> p c n", c=4)
                for c in range(4):
                    for b in range(2):
                        for h in range(2):
                            t = mm(PS[:, 2 * b + h, :], src[:, 4 * s + c, b * 128:b * 128 + 128],
                                   v[:, c, h * 512:h * 512 + 512], s + c == 0, s * 4 + c == 7, tw, sig=(b + h == 2))
                give(i, t)
            return t

        def stage_mix(l):
            rt = row(f"ng{l}3", RB[:, 2, :], dve.last())
            lo, lw = ROWS[f"lam{l}"]
            w = [0]

            def al(n):
                w[0] += n
                assert w[0] <= 12800, w[0]
                return WK[:, w[0] - n:w[0]]
            DQ = al(1024).rearrange("p (h n) -> p h n", h=4)
            DK = al(1024).rearrange("p (h n) -> p h n", h=4)
            DV = al(1024).rearrange("p (b n) -> p b n", b=2)
            QK = al(4 * 260).rearrange("p (c n) -> p c n", c=4)
            CO = al(1024).rearrange("p (c n) -> p c n", c=4)
            MV = al(8 * 129).rearrange("p (b h n) -> p b h n", b=2, h=4)
            SO = al(1024).rearrange("p (b n) -> p b n", b=2)
            GI, GF, FC, U, MM, NEM, T5 = (al(256) for _ in range(7))
            P = al(4 * 384).rearrange("p (k c n) -> p k c n", k=2, c=2)
            AT = al(768).rearrange("p (k n) -> p k n", k=2)
            LR = al(256)
            UT = al(8).rearrange("p (b h) -> p b h", b=2)
            NT = al(8).rearrange("p (b h) -> p b h", b=2)
            LT = al(8)
            T1 = al(512)
            YO = XS
            cos, sin = cs("cos"), cs("sin")
            lam_init = 0.8 - 0.6 * math.exp(-0.3 * l)
            tl = dma_sem_load(f"d_lam{l}", LR, W["rows"][0:1, lo:lo + lw].to_broadcast([128, lw]), dve.last())
            tx = norm_xs()
            th = transposed([(ve(f"ng{l}2"), HT)], XS, tx)
            t = tt(T1[:, 0:128].rearrange("p (a n) -> p a n", a=2), LR.rearrange("p (a k n) -> p a k n", a=2, k=2)[:, :, 0, :],
                   LR.rearrange("p (a k n) -> p a k n", a=2, k=2)[:, :, 1, :], ALU.mult, tl)
            t = dve(lambda e: e.tensor_reduce(LT[:, 0:2], T1[:, 0:128].rearrange("p (a n) -> p a n", a=2), AX.X, ALU.add), t)
            t = av(LT[:, 2:4], LT[:, 0:2], ACT.Exp, t)
            t = tt(LT[:, 4:5], LT[:, 2:3], LT[:, 3:4], ALU.subtract, t)
            tlam = ts(LT[:, 4:5], LT[:, 4:5], lam_init, None, ALU.add, None, t)
            NLAM = LT[:, 4:5]
            bp = banks_pool(range(4, 8))
            win = W["mix_w_in"][l]

            def slab(o, n=512):
                i, v, tw = take((lambda v: v[:, 0:8 * n].rearrange("p (c n) -> p c n", c=8),
                                 win[:, o:o + n].rearrange("(c p) n -> p c n", p=128)))
                return i, v[:, 0:8 * n].rearrange("p (c n) -> p c n", c=8), tw
            i, v, tw = slab(3072, 8)
            bk = nb(bp)
            for n in range(2):
                for c in range(8):
                    t = mm(PS[0:4, bk, n * 256:n * 256 + 256], v[:, c, 4 * n:4 * n + 4], HT[:, c, :], c == 0, c == 7,
                           tw, th, sig=(c == 7))
            give(i, t)
            gb = ve(f"gb{l}")
            r4 = slice(0, 4)
            ta = ts(GI[r4, :], PS[0:4, bk, 0:256], gb[r4, 0:1], None, ALU.add, None, t)
            tb = ts(GF[r4, :], PS[0:4, bk, 256:512], gb[r4, 1:2], None, ALU.add, None, t)
            bp["tok"][bk] = tb
            t = stt(FC[r4, :], GF[r4, :], -1.0, GF[r4, :], ALU.mult, ALU.max, tb)
            t = av(T5[r4, :], FC[r4, :], ACT.Exp, t, scale=-1.0)
            t = av(T5[r4, :], T5[r4, :], ACT.Ln, t, bias=1.0)
            t = stt(GF[r4, :], GF[r4, :], 0.0, T5[r4, :], ALU.min, ALU.subtract, t)
            tF = dve(lambda e: e.tensor_tensor_scan(FC[r4, :], GF[r4, :], GF[r4, :], 0.0, ALU.add, ALU.bypass), t)
            tU = tt(U[r4, :], GI[r4, :], FC[r4, :], ALU.subtract, tF, ta)
            tM = dve(lambda e: e.tensor_tensor_scan(MM[r4, :], U[r4, :], U[r4, :], 0.0, ALU.max, ALU.bypass), tU)
            t = tt(NEM[r4, :], FC[r4, :], MM[r4, :], ALU.add, tM)
            tN = av(NEM[r4, :], NEM[r4, :], ACT.Exp, t, scale=-1.0)
            tM = ts(MM[r4, :], MM[r4, :], -1.0, None, ALU.mult, None, t)
            for n, dst in ((0, DQ), (1, DK)):
                i, v, tw = slab(512 * n)
                for h in range(4):
                    bk = nb(bp)
                    for c in range(8):
                        mm(PS[:, bk, 0:256], v[:, c, h * 128:h * 128 + 128], HT[:, c, :], c == 0, c == 7, tw,
                           bp["tok"][bk])
                    for c in range(8):
                        for d in range(4):
                            o = h * 128 + 64 * (d // 2) + (32 if d % 2 == 0 else 0)
                            t = mm(PS[32 * d:32 * d + 32, bk, 256:512], v[:, c, o:o + 32], HT[:, c, :], c == 0, c == 7,
                                   sig=(c == 7 and d == 3))
                    t3 = tt(T1[:, 0:256], PS[:, bk, 0:256], cos, ALU.mult, t, dve.last())
                    bp["tok"][bk] = t4 = tt(T1[:, 256:512], PS[:, bk, 256:512], sin, ALU.mult, t)
                    tt(dst[:, h, :], T1[:, 0:256], T1[:, 256:512], ALU.add, t3, t4)
                give(i, t)

            def token_major(o, evac):
                i, v, tw = slab(o)
                for b in range(2):
                    bk = nb(bp)
                    for c in range(8):
                        t = mm(PS[:, bk, :], HT[:, c, b * 128:b * 128 + 128], v[:, c, :], c == 0, c == 7, tw,
                               bp["tok"][bk], sig=(c == 7))
                    bp["tok"][bk] = evac(b, PS[:, bk, :], t)
                give(i, t)
            token_major(1024, lambda b, ps, t: av(DV[:, b, :], ps, ACT.Copy, t))
            tz = dve(lambda e: e.memset(QK[:, :, 0:3], 0.0))
            i, v, tw = slab(1536)
            cw, cb = ve(f"cw{l}"), ve(f"cb{l}")
            for h in range(4):
                bk = nb(bp)
                for c in range(8):
                    t = mm(PS[:, bk, 0:256], v[:, c, h * 128:h * 128 + 128], HT[:, c, :], c == 0, c == 7, tw,
                           bp["tok"][bk], sig=(c == 7))
                t = bp["tok"][bk] = av(QK[:, h, 3:259], PS[:, bk, 0:256], ACT.Copy, t)
                t = ts(CO[:, h, :], QK[:, h, 0:256], cw[:, h:h + 1], cb[:, h:h + 1], ALU.mult, ALU.add, t, tz)
                for j in range(1, 4):
                    t = stt(CO[:, h, :], QK[:, h, j:j + 256], cw[:, 4 * j + h:4 * j + h + 1], CO[:, h, :], ALU.mult,
                            ALU.add, t)
                tco = av(CO[:, h, :], CO[:, h, :], ACT.Silu, t)
            give(i, pe.last())
            tz = dve(lambda e: e.memset(MV[:, :, :, 128:129], 1.0))
            token_major(2048, lambda b, ps, t: cp(MV[:, b, :, 0:128], ps.rearrange("p (h n) -> p h n", h=4), t))
            token_major(2560, lambda b, ps, t: av(SO[:, b, :], ps, ACT.Sigmoid, t))
            bk = nb(bp)
            for b in range(2):
                tr(PS[:, bk, b * 4:b * 4 + 4], U[0:4, b * 128:b * 128 + 128], 4, tU, bp["tok"][bk])
                t = tr(PS[:, bk, 8 + b * 4:12 + b * 4], NEM[0:4, b * 128:b * 128 + 128], 4, tN, sig=True)
            cp(UT, PS[:, bk, 0:8].rearrange("p (b h) -> p b h", b=2), t)
            cp(NT, PS[:, bk, 8:16].rearrange("p (b h) -> p b h", b=2), t)
            barrier()
            mask = cs("mask")
            bt = {bk: None for bk in range(8)}
            at, av_, pu = {}, {}, {}

            def scores(h):
                ex = []
                for d in range(2):
                    bk = 2 * (h % 2) + d
                    for i in range(2):
                        o = PS[:, bk, 0:128] if i == 0 else PS[:, bk, 128:384]
                        t = mm(o, DQ[64 * d:64 * d + 64, h, i * 128:i * 128 + 128],
                               DK[64 * d:64 * d + 64, h, 0:128 + 128 * i], True, True, bt[bk], sig=True)
                    p = P[:, h % 2, d, :]
                    bt[bk] = t = stt(p, PS[:, bk, 0:384], 0.125, mask, ALU.mult, ALU.add, t, pu.get(h - 2))
                    q = 4 * (h % 2) + 2 * d
                    m, s = SM[:, 32 + q:34 + q], SM[:, 40 + q:42 + q]
                    for i, (a, z) in enumerate(((0, 128), (128, 384))):
                        tm = dve(lambda e, i=i, a=a, z=z, m=m, p=p: e.tensor_reduce(m[:, i:i + 1], p[:, a:z], AX.X,
                                                                                     ALU.max, negate=True), t)
                    for i, (a, z) in enumerate(((0, 128), (128, 384))):
                        te = av(p[:, a:z], p[:, a:z], ACT.Exp, tm, bias=m[:, i:i + 1], accum_out=s[:, i:i + 1])
                    tr1 = dve(lambda e, s=s: e.reciprocal(s, s), te)
                    if d:
                        tr1 = ts(s, s, NLAM, None, ALU.mult, None, tr1)
                        for i, (a, z) in enumerate(((0, 128), (128, 384))):
                            t5 = ts(p[:, a:z], p[:, a:z], s[:, i:i + 1], None, ALU.mult, None, tr1)
                        q0 = 4 * (h % 2)
                        s0 = SM[:, 40 + q0:42 + q0]
                        for i, (a, z) in enumerate(((0, 128), (128, 384))):
                            at[h] = stt(P[:, h % 2, 0, a:z], P[:, h % 2, 0, a:z], s0[:, i:i + 1], p[:, a:z], ALU.mult,
                                        ALU.subtract, t5)

            def values(h):
                bk = 4 + h % 2
                for j in range(3):
                    t = tr(PS[:, bk, j * 128:j * 128 + 128], P[:, h % 2, 0, j * 128:j * 128 + 128], 128, at[h], bt[bk],
                           sig=(j == 2))
                pu[h] = t
                bt[bk] = t = av(AT[:, h % 2, :], PS[:, bk, 0:384], ACT.Copy, t, av_.get(h - 2))
                a = AT[:, h % 2, :]
                bo = 6 + h % 2
                v0, v1 = DV[:, 0, h * 128:h * 128 + 128], DV[:, 1, h * 128:h * 128 + 128]
                mm(PS[:, bo, 0:128], a[:, 0:128], v0, True, True, t, bt[bo])
                mm(PS[:, bo, 128:256], a[:, 128:256], v0, True, False)
                av_[h] = mm(PS[:, bo, 128:256], a[:, 256:384], v1, False, True, sig=True)
                bt[bo] = cp(YO[:, :, h * 128:h * 128 + 128], PS[:, bo, 0:256].rearrange("p (b n) -> p b n", b=2), av_[h])
            for h in range(5):
                if h < 4:
                    scores(h)
                if h:
                    values(h - 1)
            barrier()
            bt = {bk: None for bk in range(8)}
            E = P[:, :, 0, :]
            sel = cs("sel")
            caus = cs("caus")
            tw_, nu = {}, {}

            def wts(h):
                k = h % 2
                dp, ch = 64 * (h % 2), h // 2
                b0, b1 = 2 * k, 2 * k + 1
                mm(PS[:, b0, 0:256], sel[0:4, h * 128:h * 128 + 128], MM[0:4, :], True, True, bt[b0])
                t0 = mm(PS[:, b0, 256:384], sel[0:4, h * 128:h * 128 + 128], MM[0:4, 128:256], True, True, sig=True)
                mm(PS[:, b1, 0:256], CO[dp:dp + 64, 2 + ch, 0:128], CO[dp:dp + 64, ch, :], True, True, bt[b1])
                t1 = mm(PS[:, b1, 256:384], CO[dp:dp + 64, 2 + ch, 128:256], CO[dp:dp + 64, ch, 128:256], True, True,
                        sig=True)
                e = E[:, k, :]
                ta = ts(e[:, 0:256], PS[:, b0, 0:256], UT[:, 0, h:h + 1], 0.0, ALU.add, ALU.min, t0, nu.get(h - 2))
                tb = ts(e[:, 256:384], PS[:, b0, 256:384], UT[:, 1, h:h + 1], 0.0, ALU.add, ALU.min, t0)
                bt[b0] = tb
                te = av(e, e, ACT.Exp, ta, tb)
                t = stt(e, PS[:, b1, 0:384], 0.125, e, ALU.mult, ALU.mult, te, t1)
                bt[b1] = t
                tt(e[:, 0:128], e[:, 0:128], caus, ALU.mult, t)
                tw_[h] = tt(e[:, 256:384], e[:, 256:384], caus, ALU.mult, t)

            def num(h):
                k = h % 2
                e = E[:, k, :]
                bo = 4 + k
                mm(PS[:, bo, 0:129], e[:, 0:128], MV[:, 0, h, :], True, True, tw_[h], bt[bo])
                mm(PS[:, bo, 129:258], e[:, 128:256], MV[:, 0, h, :], True, False)
                nu[h] = t = mm(PS[:, bo, 129:258], e[:, 256:384], MV[:, 1, h, :], False, True, sig=True)
                o = PS[:, bo, 0:258].rearrange("p (b n) -> p b n", b=2)
                dn = SM[:, 64 + 2 * h:66 + 2 * h]
                t = ts(dn, o[:, :, 128], -1.0, None, ALU.mult, None, t)
                t = tt(dn, dn, o[:, :, 128], ALU.max, t)
                t = tt(dn, dn, NT[:, :, h], ALU.max, t)
                t = dve(lambda e_: e_.reciprocal(dn, dn), t)
                bt[bo] = tt(YO[:, :, 512 + h * 128:640 + h * 128], o[:, :, 0:128],
                            dn.unsqueeze(2).to_broadcast([128, 2, 128]), ALU.mult, t)
            for h in range(5):
                if h < 4:
                    wts(h)
                if h:
                    num(h - 1)
            ss, rs = SM[:, 80:96], SM[:, 96:112]
            for b in range(2):
                t = av(JK[:, :], YO[:, b, :], ACT.Square, dve.last(), act.last())
                t = dve(lambda e, b=b: e.tensor_reduce(ss[:, 8 * b:8 * b + 8], JK[:, :].rearrange("p (h n) -> p h n", h=8),
                                                       AX.X, ALU.add), t)
                act.wait(t)
            t = rsq(rs, ss, 128, t)
            rv = rs.rearrange("p (b h) -> p b h", b=2)
            t = ts(rv[:, :, 0:4], rv[:, :, 0:4], 1.0 - lam_init, None, ALU.mult, None, t)
            for b in range(2):
                y = YO[:, b, :].rearrange("p (h n) -> p h n", h=8)
                ta = tt(y, y, rv[:, b, :].unsqueeze(2).to_broadcast([128, 8, 128]), ALU.mult, t)
                ty = tt(YO[:, b, 512:1024], YO[:, b, 512:1024], SO[:, b, :], ALU.mult, ta)
            barrier()
            th = transposed([(ve(f"yg{l}"), HT)], YO, [ty])
            barrier()
            t = out_proj(W["mix_w_out"][l], HT)
            dve.wait(rt)
            post_norm((0, 2), RB[:, 2, :], 1.0, [t])

        stages = {"pool": stage_pool, "moe0": lambda: stage_moe(0), "moe1": lambda: stage_moe(1), "mla": stage_mla,
                  "fin": stage_fin, "mix0": lambda: stage_mix(0), "mix1": lambda: stage_mix(1)}
        for l in range(2):
            for k in range(2):
                stages[f"ffn{l}{k}"] = lambda l=l, k=k: stage_ffn(l, k)
        for name in plan:
            stages[name]()
            barrier()

        for i in range(len(loads) + 1):
            if i in breaks:
                sp.wait(breaks[i][0])
                sp.ops.append(breaks[i][1])
            if i == len(loads):
                break
            s, parts = loads[i]
            if i >= NS:
                sp.wait(freed[i - NS])
            for dst, src in parts:
                sp.ops.append(lambda e, dst=dst, src=src, s=s: e.dma_start(dst, src).then_inc(slot_sem[s], 16))
        s_out = sem("s_out")
        sp.wait(dve.last(), act.last(), pe.last())
        sp.ops.append(lambda e: e.dma_start(W["out"].rearrange("(b p) n -> p b n", p=128), X[:, :, :]).then_inc(s_out, 16))
        sp.ops.append(lambda e: e.wait_ge(s_out, 16))

        block = ctx.enter_context(nc.Block())

        @block.sync
        def _(e):
            sp.play(e)

        @block.tensor
        def _(e):
            pe.play(e)

        @block.vector
        def _(e):
            dve.play(e)

        @block.scalar
        def _(e):
            act.play(e)

        @block.gpsimd
        def _(e):
            pool.play(e)


def constants():
    cst = np.zeros((128, NCST), np.float32)

    def put(name, a):
        o, w = CST[name]
        cst[:a.shape[0], o:o + w] = a
    p = np.arange(128)
    put("ident", np.eye(128, dtype=np.float32))
    put("tri", (p[:, None] < p[None, :]).astype(np.float32))
    put("ones", np.ones((128, 128), np.float32))
    put("caus", (p[:, None] <= p[None, :]).astype(np.float32))
    k = np.arange(256)
    m0 = np.where(k[None, :128] // 64 <= p[:, None] // 64, 0.0, NEG)
    m1 = np.where(k[None, :] // 64 <= (p[:, None] + 128) // 64, 0.0, NEG)
    put("mask", np.concatenate([m0, m1], 1).astype(np.float32))
    inv = np.float32(10000.0) ** (-np.arange(32, dtype=np.float32) / np.float32(32))
    ang = (np.arange(256, dtype=np.float32)[None, :] * inv[:, None]).astype(np.float32)
    co, si = np.cos(ang), np.sin(ang)
    put("cos", np.concatenate([co, co, co, co], 0))
    put("sin", np.concatenate([-si, si, -si, si], 0))
    put("iota", np.broadcast_to(np.arange(32, dtype=np.float32), (128, 32)))
    sel = np.zeros((4, 4, 128), np.float32)
    for h in range(4):
        sel[h, h, :] = 1.0
    put("sel", sel.reshape(4, 512))
    pm = np.zeros((2, 128, 4, 256), np.float32)
    for g, win in enumerate((2, 4, 8, 16)):
        for t in range(256):
            lo = max(t + 1 - win, 0)
            for s in range(lo, t + 1):
                pm[s // 128, s % 128, g, t] = 1.0 / (t + 1 - lo)
            pm[t // 128, t % 128, g, t] -= 1.0
    return cst, np.ascontiguousarray(pm.transpose(1, 0, 2, 3).reshape(128, 2048))


def layouts(a):
    vec = np.zeros((128, NVEC), np.float32)

    def put(name, v):
        o, w = VEC[name]
        vec[:v.shape[0], o:o + w] = v
    for name, v in (("pool_norm", a["pool_norm"][0]), ("kv_in", a["kv_in_norm"]), ("attn", a["attn_norm"][0]),
                    ("ffn0", a["ffn_norm"][0]), ("ffn1", a["ffn_norm"][1]), ("kv_norm", a["kv_norm"]),
                    ("q_norm", a["q_norm"][0])):
        put(name, v.reshape(-1, 128).T)
    ng = a["norm_gains_2"]
    for l in range(2):
        for k in (0, 2, 4):
            put(f"ng{l}{k}", ng[l, k].reshape(8, 128).T)
        put(f"yg{l}", np.stack([a["da_subln_g_2"][l]] * 4 + [a["ml_norm_g_2"][l]] * 4, 1))
        put(f"cw{l}", a["ml_conv_w_2"][l].reshape(16, 128).T)
        put(f"cb{l}", a["ml_conv_b_2"][l].reshape(4, 128).T)
        put(f"gb{l}", a["ml_gate_b_2"][l].reshape(2, 4).T)
        rw = np.concatenate([a["router_group_w"][l], a["router_expert_w"][l]], 1)
        put(f"rw{l}", rw.reshape(8, 128, 36).transpose(1, 0, 2).reshape(128, 288))
    rows = np.zeros((1, NROWS), np.float32)

    def rput(name, v):
        o, w = ROWS[name]
        rows[0, o:o + w] = v.reshape(-1)
    rput("pool_b", a["pool_b"])
    rput("pool_scale", a["pool_scale"])
    rput("final", a["final_norm"])
    for l in range(2):
        rput(f"r{l}", np.concatenate([a["router_group_b"][l], a["router_expert_b"][l]]))
        rput(f"lam{l}", a["da_lambda_2"][l])
        for k in (1, 3, 5):
            rput(f"ng{l}{k}", ng[l, k])
    return vec, rows


BIGS = [("pool_w", "pool_w"), ("w_dkv", "w_dkv"), ("w_uk", "w_uk"), ("w_uv", "w_uv"), ("wq_down", "wq_down"),
        ("wq_up", "wq_up"), ("wo", "wo"), ("w_gate", "w_gate"), ("w_up", "w_up"), ("w_down", "w_down"),
        ("ffn_w_in", "ffn_w_in_2"), ("ffn_w_out", "ffn_w_out_2"), ("mix_w_in", "mix_w_in_2"),
        ("mix_w_out", "mix_w_out_2")]


def feeds(inputs):
    a = {k: np.asarray(v) for k, v in inputs.items()}
    cst, pm = constants()
    vec, rows = layouts(a)
    f = {"cst": cst, "pm": pm, "vec": vec, "rows": rows, "x": np.ascontiguousarray(a["x"].reshape(256, 1024))}
    for k, n in BIGS:
        f[k] = np.ascontiguousarray(a[n])
    return f


def declare(nc, f):
    W = {k: nc.dram_tensor("in_" + k, v.shape, mybir.dt.from_np(v.dtype), kind="ExternalInput").ap()
         for k, v in f.items()}
    W["out"] = nc.dram_tensor("out_0_dram", (256, 1024), F32, kind="ExternalOutput").ap()
    return W


def kernel(**inputs):
    import concourse.bacc as _bacc
    from concourse.bass_utils import run_bass_kernel_spmd as _run

    f = feeds(inputs)
    nc = _bacc.Bacc("TRN2", target_bir_lowering=False, num_devices=1)
    W = declare(nc, f)
    build(nc, W, PLAN)
    r = _run(nc, [{"in_" + k: v for k, v in f.items()}], core_ids=[0])
    return r.results[0]["out_0_dram"].reshape(1, 256, 1024)
```

```python
import math
from contextlib import ExitStack

import numpy as np

import concourse.bass as bass
from concourse import mybir

F32 = mybir.dt.float32
F32R = mybir.dt.float32r
U32 = mybir.dt.uint32
ALU = mybir.AluOpType
ACT = mybir.ActivationFunctionType
AX = mybir.AxisListType

EPS = 1e-6
NS = 6
SLOT = 4096
C = 32
CAP = 32
NEG = -1e30
BIG = 65536.0

VEC = {}
_o = 0
for _n, _w in [("pool_norm", 8), ("kv_in", 8), ("attn", 8), ("ffn0", 8), ("ffn1", 8),
               ("ng00", 8), ("ng02", 8), ("ng04", 8), ("ng10", 8), ("ng12", 8), ("ng14", 8),
               ("kv_norm", 2), ("q_norm", 3), ("yg0", 8), ("yg1", 8),
               ("cw0", 16), ("cw1", 16), ("cb0", 4), ("cb1", 4), ("gb0", 2), ("gb1", 2),
               ("rw0", 288), ("rw1", 288),
               ("gw0", 64), ("gw1", 64)]:
    VEC[_n] = (_o, _w)
    _o += _w
NVEC = _o
CST = {}
_o = 0
for _n, _w in [("ident", 128), ("tri", 128), ("ones", 128), ("caus", 128), ("mask", 384),
               ("cos", 256), ("sin", 256), ("iota", 32), ("sel", 512), ("swap", 128)]:
    CST[_n] = (_o, _w)
    _o += _w
NCST = _o
ROWS = {}
_o = 0
for _n, _w in [("pool_b", 1024), ("pool_scale", 1024), ("final", 1024), ("r0", 36), ("r1", 36),
               ("lam0", 256), ("lam1", 256), ("ng01", 1024), ("ng03", 1024), ("ng05", 1024),
               ("ng11", 1024), ("ng13", 1024), ("ng15", 1024)]:
    ROWS[_n] = (_o, _w)
    _o += _w
NROWS = _o
PLAN = ["pool", "moe0", "mla", "moe1", "fin", "ffn00", "mix0", "ffn01", "ffn10", "mix1", "ffn11"]


class Eng:

    def __init__(self, sem):
        self.sem, self.n, self.ops, self.seen = sem, 0, [], {}

    def wait(self, *toks):
        for t in toks:
            if t is None:
                continue
            if isinstance(t, list):
                self.wait(*t)
                continue
            sem, v = t
            if v > 0 and self.seen.get(sem.name, 0) < v:
                self.seen[sem.name] = v
                self.ops.append(lambda e, sem=sem, v=v: e.wait_ge(sem, v))

    def __call__(self, fn, *toks, sig=True):
        self.wait(*toks)
        if sig:
            self.n += 1
            self.ops.append(lambda e: fn(e).then_inc(self.sem, 1))
        else:
            self.ops.append(fn)
        return (self.sem, self.n)

    def last(self):
        return (self.sem, self.n)

    def play(self, e):
        for op in self.ops:
            op(e)


def build(nc, W, plan):
    ctx = ExitStack()
    with ctx:
        top = [(nc.sbuf_base + 63) // 64 * 64]

        def sb(name, shape, dt=F32, at=None):
            size = int(np.prod(shape[1:])) * 4
            off = top[0] if at is None else at
            if at is None:
                place[name] = off
                top[0] = (off + size + 31) // 32 * 32
            return nc.alloc_sbuf_tensor_at(name, shape, dt, offset=off)
        place = {}

        def sem(name):
            return ctx.enter_context(nc.semaphore(name))

        RING = sb("RING", [128, NS, SLOT])
        X = sb("X", [128, 2, 1024])
        XS = sb("XS", [128, 2, 1024])
        HT = sb("HT", [128, 8, 256])
        CS = sb("CS", [128, NCST])
        VE = sb("VE", [128, NVEC])
        RB = sb("RB", [128, 3, 1024])
        RR = sb("RR", [128, 72])
        JK = sb("JK", [128, 1024])
        SM = sb("SM", [128, 512])
        MH = sb("MH", [128, 16])
        WK = sb("WK", [128, 12800])
        IX = sb("IX", [128, 32], U32)
        FLAG = sb("FLAG", [128, 2], U32)
        WH = sb("WH", [128, 2, 2048], F32R, at=place["RING"] + 4 * SLOT * 4)
        WL = sb("WL", [128, 2, 2048], F32R, at=place["RING"] + 5 * SLOT * 4)
        HTH = sb("HTH", [128, 8, 256], F32R, at=place["HT"])
        HTL = sb("HTL", [128, 8, 256], F32R, at=place["XS"])
        HFH = sb("HFH", [128, 22, 256], F32R, at=place["WK"])
        HFL = sb("HFL", [128, 22, 256], F32R, at=place["WK"] + 22 * 1024)
        GWH = sb("GWH", [128, 64], F32R)
        GWL = sb("GWL", [128, 64], F32R)
        PS = ctx.enter_context(nc.psum_tensor("PS", [128, 8, 512], F32))

        pe, act, dve, pool, sp = (Eng(sem(n)) for n in ("s_pe", "s_act", "s_dve", "s_pool", "s_sp"))
        slot_sem = [sem(f"s_slot{i}") for i in range(NS)]

        def cs(name, p=128):
            o, w = CST[name]
            return CS[0:p, o:o + w]

        def ve(name):
            o, w = VEC[name]
            return VE[:, o:o + w]

        loads, freed, slot_n, breaks = [], {}, [0] * NS, {}
        active, at_slot, prior, slot_user, cover = [list(range(NS))], [0], {}, {}, {}

        def take(*parts):
            i = len(loads)
            s = active[0][at_slot[0] % len(active[0])]
            at_slot[0] += 1
            prior[i] = [slot_user.get(s), cover.pop(s, None)]
            slot_user[s] = i
            view = RING[:, s, :]
            slot_n[s] += 16 * len(parts)
            loads.append((s, [(d(view), src) for d, src in parts]))
            return i, view, (slot_sem[s], slot_n[s])

        def give(i, tok):
            freed[i] = tok

        def ring(n):
            if n == NS and len(active[0]) < NS:
                for s in range(4, NS):
                    cover[s] = [dve.last(), act.last(), pe.last()]
            active[0] = list(range(n))

        sp_n, sp_free = [0], {}

        def split(src, shape, tw):
            k = sp_n[0] % 2
            sp_n[0] += 1
            a, b = shape
            hi, lo = (z[:, k, 0:a * b].rearrange("p (a b) -> p a b", a=a) for z in (WH, WL))
            before = sp_free.get(sp_n[0] - 2)
            if sp_n[0] <= 2 or before is None:
                before = [freed.get(slot_user.get(s)) for s in (4, 5)]
            t1 = av(hi, src, ACT.Copy, tw, before)
            t2 = tt(lo, src, hi.bitcast(F32), ALU.subtract, t1, before)
            return hi, lo, [t1, t2], sp_n[0]

        wanted, issued = [], []

        def issue():
            if wanted:
                src, shape, tw, last = wanted.pop(0)()
                got = split(src, shape, tw)
                if last is not None:
                    give(last, got[2])
                issued.append(got)

        def next_split():
            if not issued:
                issue()
            issue()
            return issued.pop(0)

        def want_slabs(w, o, n, rows, cut, halves):
            box = {}

            def request(j):
                if j == 0:
                    box["t"] = take((lambda v: v[:, 0:rows * n].rearrange("p (c n) -> p c n", c=rows), w))
                i, v, tw = box["t"]
                v = v[:, 0:rows * n].rearrange("p (c n) -> p c n", c=rows)
                m = rows // halves if cut == "rows" else n // halves
                part = v[:, j * m:j * m + m, :] if cut == "rows" else v[:, :, j * m:j * m + m]
                return part, part.shape[1:], tw, i if j == halves - 1 else None
            return [lambda j=j: request(j) for j in range(halves)]

        def want_ffn(l, k):
            win, wout = W["ffn_w_in"][l, k], W["ffn_w_out"][l, k]

            def cols(o, w):
                return win[:, o:o + w].rearrange("(c p) n -> p c n", p=128)
            for s in range(5):
                g = want_slabs(cols(512 * s, 512), 0, 512, 8, "cols", 2)
                u = want_slabs(cols(2816 + 512 * s, 512), 0, 512, 8, "cols", 2)
                wanted.extend([g[0], u[0], g[1], u[1]])
            box = {}

            def tail(j):
                if j == 0:
                    box["t"] = take((lambda v: v[:, 0:2048].rearrange("p (c n) -> p c n", c=8), cols(2560, 256)),
                                    (lambda v: v[:, 2048:4096].rearrange("p (c n) -> p c n", c=8), cols(5376, 256)))
                i, v, tw = box["t"]
                return v[:, 2048 * j:2048 * j + 2048].rearrange("p (c n) -> p c n", c=8), (8, 256), tw, i if j else None
            wanted.extend([lambda: tail(0), lambda: tail(1)])
            for s in range(6):
                n = 4 if s < 5 else 2
                wanted.extend(want_slabs(wout[512 * s:512 * s + 128 * n, :].rearrange("(c p) n -> p c n", p=128), 0, 1024,
                                         n, "rows", n // 2))

        def want_mix(l):
            win = W["mix_w_in"][l]
            for o, cut in ((0, "cols"), (512, "cols"), (1024, "rows"), (1536, "cols"), (2048, "rows"), (2560, "rows")):
                wanted.extend(want_slabs(win[:, o:o + 512].rearrange("(c p) n -> p c n", p=128), 0, 512, 8, cut, 2))
            for s in range(2):
                wanted.extend(want_slabs(W["mix_w_out"][l][512 * s:512 * s + 512, :].rearrange("(c p) n -> p c n", p=128),
                                         0, 1024, 4, "rows", 2))

        def mm3(out, lt, rt_, start, stop, *toks, sig=False):
            (lh, ll), (rh, rl) = lt, rt_
            mm(out, ll, rh, start, False, *toks)
            mm(out, lh, rl, False, False)
            return mm(out, lh, rh, False, stop, sig=sig)

        def dma_sem_load(name, dst, src, *toks):
            s = sem(name)
            act.wait(*toks)
            act.ops.append(lambda e: e.dma_start(dst, src).then_inc(s, 16))
            return (s, 16)

        def row(name, dst, *toks):
            o, w = ROWS[name]
            return dma_sem_load("d_" + name, dst, W["rows"][:, o:o + w].partition_broadcast(128)
                                if W["rows"].shape[0] != 1 else W["rows"][0:1, o:o + w].to_broadcast([128, w]), *toks)

        def barrier():
            for e in (pe, act, dve, pool):
                e.wait(*[o.last() for o in (pe, act, dve, pool)])

        def mm(out, lhsT, rhs, start, stop, *toks, sig=False):
            return pe(lambda e: e.matmul(out, lhsT, rhs, start=start, stop=stop), *toks, sig=sig)

        def tr(out, in_, p, *toks, sig=False):
            ident = CS[0:p, 0:p]
            return pe(lambda e: e.transpose(out, in_, ident), *toks, sig=sig)

        def ts(out, in0, s1, s2, o0, o1, *toks):
            if s2 is None:
                return dve(lambda e: e.tensor_scalar(out, in0, s1, None, o0), *toks)
            return dve(lambda e: e.tensor_scalar(out, in0, s1, s2, o0, o1), *toks)

        def tt(out, a, b, op, *toks):
            return dve(lambda e: e.tensor_tensor(out, a, b, op), *toks)

        def stt(out, a, s, b, o0, o1, *toks):
            return dve(lambda e: e.scalar_tensor_tensor(out, a, s, b, o0, o1), *toks)

        def av(out, in_, func, *toks, **kw):
            return act(lambda e: e.activation(out, in_, func, **kw), *toks)

        def cp(out, in_, *toks):
            return dve(lambda e: e.tensor_copy(out, in_), *toks)

        def rsq(out, ss, n, *toks):
            t = pool(lambda e: e.tensor_scalar(out, ss, 1.0 / n, EPS, ALU.mult, ALU.add), *toks)
            return pool(lambda e: e.tensor_tensor(out, out, MH[:, 0:out.shape[1]], ALU.pow), t)

        t_cs = dma_sem_load("d_cs", CS[:, :], W["cst"])
        t_ve = dma_sem_load("d_ve", VE[:, :], W["vec"])
        t_x = dma_sem_load("d_x", X[:, :, :], W["x"].rearrange("(b p) n -> p b n", p=128))
        t_r = [row("pool_b", RB[:, 0, :]), row("pool_scale", RB[:, 1, :]), row("final", RB[:, 2, :]),
               row("r0", RR[:, 0:36]), row("r1", RR[:, 36:72])]
        for e in (pe, act, dve, pool):
            e.wait(t_cs, t_ve, t_x, *t_r)

        pool(lambda e: e.memset(MH[:, :], -0.5))
        pool.wait(pool.last())

        def norm_xs(src=None):
            ss, rs = SM[:, 0:2], SM[:, 2:4]
            t0 = av(JK[:, :], X[:, 0, :], ACT.Square, accum_out=ss[:, 0:1])
            t1 = av(JK[:, :], X[:, 1, :], ACT.Square, t0, accum_out=ss[:, 1:2])
            t = rsq(rs, ss, 1024, t1)
            a = ts(XS[:, 0, :], X[:, 0, :], rs[:, 0:1], None, ALU.mult, None, t)
            b = av(XS[:, 1, :], X[:, 1, :], ACT.Copy, t, scale=rs[:, 1:2])
            return [a, b]

        def transposed(outs, src, toks, banks=(0, 1, 2, 3), nch=8, free=None):
            res = []
            for j in range(nch // 2):
                bk = banks[j]
                for cc in range(2):
                    c = 2 * j + cc
                    for b in range(2):
                        t = tr(PS[:, bk, cc * 256 + b * 128:cc * 256 + b * 128 + 128],
                               src[:, b, c * 128:c * 128 + 128], 128, toks, sig=(cc + b == 2))
                got = []
                for gain, dst in outs:
                    if j % 2 == 0:
                        got.append(tt(dst[:, 2 * j:2 * j + 2, :], PS[:, bk, :].rearrange("p (c n) -> p c n", c=2),
                                      gain[:, 2 * j:2 * j + 2].unsqueeze(2).to_broadcast([128, 2, 256]),
                                      ALU.mult, t))
                    else:
                        for cc in range(2):
                            c = 2 * j + cc
                            got.append(av(dst[:, c, :], PS[:, bk, cc * 256:cc * 256 + 256], ACT.Copy, t,
                                          scale=gain[:, c:c + 1]))
                res += got
            return res

        def transposed3(gain, src, toks):
            for c in range(8):
                for b in range(2):
                    t = tr(PS[:, c // 2, (c % 2) * 256 + b * 128:(c % 2) * 256 + b * 128 + 128],
                           src[:, b, c * 128:c * 128 + 128], 128, toks, sig=(c % 2 + b == 2))
                if c % 2:
                    for cc in (c - 1, c):
                        av(HTH[:, cc, :], PS[:, cc // 2, (cc % 2) * 256:(cc % 2) * 256 + 256], ACT.Copy, t,
                           scale=gain[:, cc:cc + 1])
            done = []
            base = act.n - 8
            for c in range(8):
                d = stt(HTL[:, c, :], PS[:, c // 2, (c % 2) * 256:(c % 2) * 256 + 256], gain[:, c:c + 1],
                        HTH[:, c, :].bitcast(F32), ALU.mult, ALU.subtract, t, (act.sem, base + (c | 1) + 1))
                done.append([(act.sem, base + c + 1), d])
            return done

        def post_norm(banks, rowv, half, toks):
            ss, rs = SM[:, 4:6], SM[:, 6:8]
            for b in range(2):
                t = av(JK[:, :].rearrange("p (a n) -> p a n", a=2), PS[:, banks[b]:banks[b] + 2, :], ACT.Square,
                       toks, act.last(), accum_out=ss[:, b:b + 1])
            t = rsq(rs, ss, 1024, t)
            if half != 1.0:
                t = ts(rs, rs, half, None, ALU.mult, None, t)
            for b in range(2):
                j = JK[:, :] if b else XS[:, 0, :]
                t1 = stt(j.rearrange("p (a n) -> p a n", a=2), PS[:, banks[b]:banks[b] + 2, :], rs[:, b:b + 1],
                         rowv.rearrange("p (a n) -> p a n", a=2), ALU.mult, ALU.mult, t)
                tt(X[:, b, :], X[:, b, :], j, ALU.add, t1)

        def stage_pool():
            i, v, tw = take((lambda v: v[:, 0:2048], W["pm"]),
                            (lambda v: v[:, 2048:4096].rearrange("p (a d) -> p a d", a=8),
                             W["pool_w"][0].rearrange("g (cc p) d -> p (g cc) d", p=128)))
            M = v[:, 0:2048].rearrange("p (b g t) -> p b g t", b=2, g=4)
            PW = v[:, 2048:4096].rearrange("p (a d) -> p a d", a=8)
            tx = norm_xs()
            pg = ve("pool_norm")
            for g in range(4):
                for cc in range(2):
                    c = 2 * g + cc
                    for b in range(2):
                        t = mm(PS[:, g, cc * 256:cc * 256 + 256], XS[:, b, c * 128:c * 128 + 128], M[:, b, g, :],
                               b == 0, b == 1, tx, tw, sig=(b == 1))
                te = tt(HT[:, 2 * g:2 * g + 2, :], PS[:, g, :].rearrange("p (c n) -> p c n", c=2),
                        pg[:, 2 * g:2 * g + 2].unsqueeze(2).to_broadcast([128, 2, 256]), ALU.mult, t)
                for b in range(2):
                    o = PS[:, 4 + 2 * b + g // 2, (g % 2) * 256:(g % 2) * 256 + 256]
                    for cc in range(2):
                        t = mm(o, HT[:, 2 * g + cc, b * 128:b * 128 + 128], PW[:, 2 * g + cc, :], cc == 0, cc == 1, te,
                               sig=(cc == 1))
            give(i, t)
            for b in range(2):
                j = JK[:, :].rearrange("p (a n) -> p a n", a=2)
                t1 = tt(j, PS[:, 4 + 2 * b:6 + 2 * b, :], RB[:, 0, :].rearrange("p (a n) -> p a n", a=2), ALU.add,
                        t, dve.last())
                t1 = tt(JK[:, :], JK[:, :], RB[:, 1, :], ALU.mult, t1)
                tt(X[:, b, :], X[:, b, :], JK[:, :], ALU.add, t1)

        def stage_moe(l):
            ring(NS)
            tx = norm_xs()
            gain = ve(f"ffn{l}")
            th = transposed([(gain, HT)], XS, tx)
            rw = ve(f"rw{l}").rearrange("p (c n) -> p c n", c=8)
            for b in range(2):
                for c in range(8):
                    t = mm(PS[:, 4, b * 36:b * 36 + 36], HT[:, c, b * 128:b * 128 + 128], rw[:, c, :], c == 0, c == 7,
                           th, sig=(c == 7))
            w = [0]

            def al(n):
                w[0] += n
                return WK[:, w[0] - n:w[0]]
            S = al(2048).rearrange("p (b n) -> p b n", b=2)
            G = al(2048).rearrange("p (b n) -> p b n", b=2)
            XE = al(2048).rearrange("p (k c n) -> p k c n", k=2, c=8)
            GT = al(512).rearrange("p (k n) -> p k n", k=2)
            HG = al(512).rearrange("p (k n) -> p k n", k=4)
            HE = al(256).rearrange("p (k n) -> p k n", k=2)
            Y = al(1024)
            L = al(72).rearrange("p (b n) -> p b n", b=2)
            G8 = al(16).rearrange("p (b n) -> p b n", b=2)
            M8 = al(16).rearrange("p (b n) -> p b n", b=2)
            V8 = al(16).rearrange("p (b n) -> p b n", b=2)
            E8 = al(16).rearrange("p (b n) -> p b n", b=2)
            T4 = al(64).rearrange("p (b g e) -> p b g e", b=2, g=4)
            OH = al(8).rearrange("p (b n) -> p b n", b=2)
            IG = al(2)
            IE = al(4).rearrange("p (b n) -> p b n", b=2)
            NM, SG, GP, DD, EE, W1, W2 = (al(2) for _ in range(7))
            A1, A2, A, GM, PO = (al(64).rearrange("p (b n) -> p b n", b=2) for _ in range(5))
            io = cs("iota")
            t = tt(L, PS[:, 4, 0:72].rearrange("p (b n) -> p b n", b=2),
                   RR[:, 36 * l:36 * l + 36].unsqueeze(1).to_broadcast([128, 2, 36]), ALU.add, t)
            t8 = dve(lambda e: e.memset(G8, -3e38))
            t = cp(G8[:, :, 0:4], L[:, :, 0:4], t, t8)
            for b in range(2):
                ta = dve(lambda e, b=b: e.max(M8[:, b, :], G8[:, b, :]), t)
                ta = dve(lambda e, b=b: e.max_index(IX[:, b * 8:b * 8 + 8], M8[:, b, :], G8[:, b, :]), ta)
            tg = cp(IG, IX[:, 0:16].rearrange("p (b n) -> p b n", b=2)[:, :, 0], ta)
            tn = ts(NM, M8[:, :, 0], -1.0, None, ALU.mult, None, ta)
            for b in range(2):
                te = av(SM[:, 16 + 4 * b:20 + 4 * b], L[:, b, 0:4], ACT.Exp, tn, bias=NM[:, b:b + 1],
                        accum_out=SG[:, b:b + 1])
            tp = dve(lambda e: e.reciprocal(GP, SG), te)
            t = tt(OH, io[:, 0:4].unsqueeze(1).to_broadcast([128, 2, 4]), IG.unsqueeze(2).to_broadcast([128, 2, 4]),
                   ALU.is_equal, tg)
            t = tt(T4, L[:, :, 4:36].rearrange("p b (g e) -> p b g e", g=4),
                   OH.unsqueeze(3).to_broadcast([128, 2, 4, 8]), ALU.mult, t)
            for b in range(2):
                t = dve(lambda e, b=b: e.tensor_reduce(E8[:, b, :], T4[:, b, :, :].rearrange("p g e -> p e g"), AX.X,
                                                       ALU.add), t)
            for b in range(2):
                ta = dve(lambda e, b=b: e.max(V8[:, b, :], E8[:, b, :]), t)
                ta = dve(lambda e, b=b: e.max_index(IX[:, 16 + b * 8:24 + b * 8], V8[:, b, :], E8[:, b, :]), ta)
            t = cp(IE, IX[:, 16:32].rearrange("p (b n) -> p b n", b=2)[:, :, 0:2], ta)
            t = stt(IE, IG.unsqueeze(2).to_broadcast([128, 2, 2]), 8.0, IE, ALU.mult, ALU.add, t)
            td = tt(DD, V8[:, :, 1], V8[:, :, 0], ALU.subtract, ta)
            td = av(EE, DD, ACT.Exp, td)
            t1 = ts(W1, EE, 1.0, None, ALU.add, None, td)
            t1 = dve(lambda e: e.reciprocal(W1, W1), t1)
            t1 = tt(W1, W1, GP, ALU.mult, t1, tp)
            t1 = tt(W2, W1, EE, ALU.mult, t1)
            i32 = io.unsqueeze(1).to_broadcast([128, 2, 32])
            ta = tt(A1, i32, IE[:, :, 0:1].to_broadcast([128, 2, 32]), ALU.is_equal, t)
            tb = tt(A2, i32, IE[:, :, 1:2].to_broadcast([128, 2, 32]), ALU.is_equal, t)
            tA = tt(A, A1, A2, ALU.add, tb)
            ta = tt(A1, A1, W1.unsqueeze(2).to_broadcast([128, 2, 32]), ALU.mult, tA, t1)
            tb = tt(A2, A2, W2.unsqueeze(2).to_broadcast([128, 2, 32]), ALU.mult, tA, t1)
            tG = tt(GM, A1, A2, ALU.add, ta, tb)
            mm(PS[:, 5, 0:32], cs("tri"), A[:, 0, :], True, True, tA)
            mm(PS[:, 5, 32:64], cs("ones"), A[:, 0, :], True, False)
            mm(PS[:, 5, 32:64], cs("tri"), A[:, 1, :], False, True)
            mm(PS[:, 5, 64:96], cs("ones"), A[:, 0, :], True, False)
            tq = mm(PS[:, 5, 64:96], cs("ones"), A[:, 1, :], False, True, sig=True)
            t = ts(PO, A, -BIG, BIG, ALU.mult, ALU.add, tA)
            t = tt(PO, PO, PS[:, 5, 0:64].rearrange("p (b n) -> p b n", b=2), ALU.add, t, tq)
            GO = SM[:, 128:192].rearrange("p (b n) -> p b n", b=2)
            t1 = ts(GO, PO, float(CAP), None, ALU.is_ge, None, t)
            tGO = tt(GO, GO, GM, ALU.mult, t1, tG)
            t1 = dve(lambda e: e.tensor_reduce(SM[:, 192:193], PS[:, 5, 64:96], AX.X, ALU.max), tq)
            t1 = ts(SM[:, 192:193], SM[:, 192:193], float(CAP), None, ALU.is_gt, None, t1)
            flag = FLAG[0:1, l:l + 1]
            tflag = cp(FLAG[:, l:l + 1], SM[:, 192:193], t1)
            if CAP < C:
                t1 = ts(A1, PO, float(CAP), BIG, ALU.is_ge, ALU.mult, t, tG)
                t = tt(PO, PO, A1, ALU.add, t1, tGO)
            for b in range(2):
                t1 = tt(S[:, b, :].rearrange("p (e s) -> p e s", e=32), io[:, 0:C].unsqueeze(1).to_broadcast([128, 32, C]),
                        PO[:, b, :].unsqueeze(2).to_broadcast([128, 32, C]), ALU.is_equal, t)
                tS = tt(G[:, b, :].rearrange("p (e s) -> p e s", e=32), S[:, b, :].rearrange("p (e s) -> p e s", e=32),
                        GM[:, b, :].unsqueeze(2).to_broadcast([128, 32, C]), ALU.mult, t1, tG)
            barrier()
            wd = W["w_down"][l]
            sl = {}

            def load_gu(e):
                for k in ("w_gate", "w_up"):
                    sl[k, e] = take((lambda v: v.rearrange("p (c n) -> p c n", c=8),
                                     W[k][l, e].rearrange("(c p) n -> p c n", p=128)))

            def load_d(e):
                sl["d", e] = take((lambda v: v.rearrange("p (c n) -> p c n", c=4),
                                   wd[e].rearrange("(c p) n -> p c n", p=128)))
            bank = {k: None for k in range(8)}
            hg, he, ga, gt = {}, {}, {}, {}

            def gather(g):
                for r in range(2):
                    bk = 2 + r
                    for c in range(4):
                        for b in range(2):
                            t = mm(PS[:, bk, c * 128:c * 128 + 128],
                                   XS[:, b, (4 * r + c) * 128:(4 * r + c) * 128 + 128], S[:, b, g * 128:g * 128 + 128],
                                   b == 0, b == 1, bank[bk], sig=(c == 3 and b == 1))
                    old = ga.get(g - 2)
                    bank[bk] = ga[g] = tt(XE[:, g % 2, 4 * r:4 * r + 4, :], PS[:, bk, :].rearrange("p (c n) -> p c n", c=4),
                                          gain[:, 4 * r:4 * r + 4].unsqueeze(2).to_broadcast([128, 4, 128]), ALU.mult,
                                          t, last_gu.get(4 * (g - 2) + 3))
                for b in range(2):
                    t = tr(PS[:, 3, b * 128:b * 128 + 128], G[:, b, g * 128:g * 128 + 128], 128, bank[3], sig=(b == 1))
                bank[3] = gt[g] = av(GT[:, g % 2, :], PS[:, 3, 0:256], ACT.Copy, t, comb.get(g - 2))
            last_gu, comb = {}, {}

            def gateup(e):
                g, j = divmod(e, 4)
                pb = e % 2
                for n, k in enumerate(("w_gate", "w_up")):
                    i, v, tw = sl[k, e]
                    v = v.rearrange("p (c n) -> p c n", c=8)
                    for c in range(8):
                        for q in range(4):
                            t = mm(PS[32 * q:32 * q + 32, pb, n * 128:n * 128 + 128],
                                   XE[:, g % 2, c, 32 * j:32 * j + 32], v[:, c, 128 * q:128 * q + 128], c == 0, c == 7,
                                   tw, ga[g], bank[pb], sig=(c == 7 and q == 3))
                    give(i, t)
                ta = av(HG[:, pb, :], PS[:, pb, 0:128], ACT.Silu, t, hg.get(e - 2))
                last_gu[e] = t
                hg[e] = bank[pb] = tt(HG[:, 2 + pb, :], HG[:, pb, :], PS[:, pb, 128:256], ALU.mult, t, ta, he.get(e - 2))

            def down(e):
                g, j = divmod(e, 4)
                pb = e % 2
                t = tr(PS[:, 3, 0:128], HG[:, 2 + pb, :], 128, hg[e], bank[3], sig=True)
                he[e] = bank[3] = cp(HE[:, pb, :], PS[:, 3, 0:128], t, dn.get(e - 2))
                i, v, tw = sl["d", e]
                v = v.rearrange("p (c n) -> p c n", c=4)
                for h in range(2):
                    for c in range(4):
                        t = mm(PS[32 * j:32 * j + 32, 4 + h, :], HE[:, pb, 32 * c:32 * c + 32],
                               v[:, c, 512 * h:512 * h + 512], c == 0, c == 3, tw, he[e],
                               bank[4 + h] if j == 0 else None, sig=(c == 3))
                dn[e] = t
                give(i, t)
                if j == 3:
                    a = av(Y[:, 0:512], PS[:, 4, :], ACT.Copy, t, comb.get(g - 1))
                    d = cp(Y[:, 512:1024], PS[:, 5, :], t, comb.get(g - 1))
                    bank[4], bank[5] = a, d
                    ydone[g] = [a, d]
            dn, ydone = {}, {}

            def combine(g):
                for b in range(2):
                    for h in range(2):
                        t = mm(PS[:, 6 + h, :], GT[:, g % 2, b * 128:b * 128 + 128], Y[:, h * 512:h * 512 + 512], True,
                               True, ydone[g], gt[g], bank[6 + h], sig=True)
                        bank[6 + h] = tt(X[:, b, h * 512:h * 512 + 512], X[:, b, h * 512:h * 512 + 512],
                                         PS[:, 6 + h, :], ALU.add, t)
                comb[g] = t

            for e in range(33):
                if e < 32:
                    if e % 4 == 0:
                        gather(e // 4)
                    load_gu(e)
                    gateup(e)
                if e >= 1:
                    load_d(e - 1)
                    down(e - 1)
                    if (e - 1) % 4 == 0 and e > 1:
                        combine((e - 1) // 4 - 1)
            combine(7)
            overflow(l, GO, flag, tflag)

        def overflow(l, GO, flag, tflag):
            names = ("pe", "act", "dve", "sp")
            o = {n: Eng(sem(f"o_{n}{l}")) for n in names}
            lds = [sem(f"o_ld{l}{k}") for k in range(2)]
            outer = {"pe": pe, "act": act, "dve": dve}
            begun = [x.last() for x in outer.values()]
            for x in o.values():
                x.wait(*begun)
            BUF = [WK[:, 6144 * k:6144 * k + 6144] for k in range(2)]
            HFO = WK[:, 12288:12800].rearrange("p (f n) -> p f n", f=2)
            GS = JK[:, 0:512].rearrange("p (f n) -> p f n", f=2)
            used, tsilu, thf, tadd, tdown = {}, {}, {}, {}, {}
            for n in range(64):
                e, hf = divmod(n, 2)
                k = n % 2
                wg, wu, wd = (BUF[k][:, 2048 * z:2048 * z + 2048] for z in range(3))
                o["sp"].wait(used.get(n - 2))
                for dst, src in ((wg, W["w_gate"][l, e][:, 256 * hf:256 * hf + 256]),
                                 (wu, W["w_up"][l, e][:, 256 * hf:256 * hf + 256]),
                                 (wd, W["w_down"][l, e][256 * hf:256 * hf + 256, :])):
                    m = 2 if dst is wd else 8
                    o["sp"].ops.append(lambda g, dst=dst, src=src, k=k, m=m: g.dma_start(
                        dst.rearrange("p (c n) -> p c n", c=m), src.rearrange("(c p) n -> p c n", p=128)
                    ).then_inc(lds[k], 16))
                tl = (lds[k], 48 * (n // 2 + 1))
                gv, uv = (z.rearrange("p (c n) -> p c n", c=8) for z in (wg, wu))
                dv = wd.rearrange("p (c n) -> p c n", c=2)
                for f in range(2):
                    for z, v in enumerate((gv, uv)):
                        for c in range(8):
                            t = o["pe"](lambda g, f=f, z=z, v=v, c=c: g.matmul(
                                PS[:, f, z * 256:z * 256 + 256], v[:, c, f * 128:f * 128 + 128], HT[:, c, :],
                                start=c == 0, stop=c == 7), tl, thf.get((n - 1, f)), sig=(c == 7))
                    ta = o["act"](lambda g, f=f: g.activation(GS[:, f, :], PS[:, f, 0:256], ACT.Silu), t,
                                  thf.get((n - 1, f)))
                    thf[n, f] = o["dve"](lambda g, f=f: g.tensor_tensor(HFO[:, f, :], GS[:, f, :], PS[:, f, 256:512],
                                                                        ALU.mult), t, ta, tdown.get(n - 1))
                for f in range(2):
                    for b in range(2):
                        for h in range(2):
                            tdown[n] = used[n] = o["pe"](lambda g, f=f, b=b, h=h, dv=dv, hf=hf: g.matmul(
                                PS[:, 4 + 2 * b + h, :], HFO[:, f, b * 128:b * 128 + 128], dv[:, f, h * 512:h * 512 + 512],
                                start=(f == 0 and hf == 0), stop=(f == 1 and hf == 1)), thf[n, 1],
                                tadd.get(e - 1), sig=(b + h == 2))
                if hf == 1:
                    for b in range(2):
                        xv = X[:, b, :].rearrange("p (a n) -> p a n", a=2)
                        tadd[e] = o["dve"](lambda g, b=b, xv=xv, e=e: g.scalar_tensor_tensor(
                            xv, PS[:, 4 + 2 * b:6 + 2 * b, :], GO[:, b, e:e + 1], xv, ALU.mult, ALU.add), tdown[n],
                            tadd.get(e - 1))
            done = [o[n].last() for n in ("pe", "act", "dve")]
            for x in o.values():
                x.wait(*done)

            def enter(g, inner):
                v = g.value_load(flag, min_val=0, max_val=1)
                with g.If(v > 0):
                    inner.play(g)
            for n, x in outer.items():
                x.wait(tflag)
                x.ops.append(lambda g, n=n: enter(g, o[n]))
            breaks[len(loads)] = (tflag, lambda g: enter(g, o["sp"]))

        def stage_fin():
            tx = norm_xs()
            for b in range(2):
                tt(X[:, b, :], XS[:, b, :], RB[:, 2, :], ALU.mult, tx)

        def stage_ffn(l, k):
            ring(4)
            rt = row(f"ng{l}{1 if k == 0 else 5}", RB[:, k, :], dve.last())
            tx = norm_xs()
            th = transposed3(ve(f"ng{l}{0 if k == 0 else 4}"), XS, tx)
            GS = WK[:, 11264:11776].rearrange("p (k n) -> p k n", k=2)
            VV = WK[:, 11776:12288].rearrange("p (k n) -> p k n", k=2)
            bank = {bk: None for bk in range(8)}
            gs, hl = {}, {}
            for fp in range(11):
                for n in range(2):
                    hi, lo, tsp, key = next_split()
                    for fq in range(2):
                        f = 2 * fp + fq
                        bk = 4 + f % 4
                        for c in range(8):
                            t = mm3(PS[:, bk, n * 256:n * 256 + 256],
                                    (hi[:, c, fq * 128:fq * 128 + 128], lo[:, c, fq * 128:fq * 128 + 128]),
                                    (HTH[:, c, :], HTL[:, c, :]), c == 0, c == 7, tsp, th[c], bank[bk], sig=(c == 7))
                        if n:
                            ta = av(GS[:, f % 2, :], PS[:, bk, 0:256], ACT.Silu, t, gs.get(f - 2))
                            gs[f] = bank[bk] = tv = tt(VV[:, f % 2, :], GS[:, f % 2, :], PS[:, bk, 256:512], ALU.mult,
                                                       t, ta)
                            ta = av(HFH[:, f, :], VV[:, f % 2, :], ACT.Copy, tv)
                            hl[f] = [ta, tt(HFL[:, f, :], VV[:, f % 2, :], HFH[:, f, :].bitcast(F32), ALU.subtract, ta)]
                    sp_free[key] = t
            for fp in range(11):
                hi, lo, tsp, key = next_split()
                for c in range(2):
                    f = 2 * fp + c
                    for b in range(2):
                        for h in range(2):
                            t = mm3(PS[:, 2 * b + h, :],
                                    (HFH[:, f, b * 128:b * 128 + 128], HFL[:, f, b * 128:b * 128 + 128]),
                                    (hi[:, c, h * 512:h * 512 + 512], lo[:, c, h * 512:h * 512 + 512]),
                                    f == 0, f == 21, tsp, hl[f], th[7], sig=(b + h == 2))
                sp_free[key] = t
            dve.wait(rt)
            post_norm((0, 2), RB[:, k, :], 0.5, [t])

        def banks_pool(ids):
            return {"ids": list(ids), "at": 0, "tok": {i: None for i in ids}}

        def nb(bp):
            i = bp["ids"][bp["at"] % len(bp["ids"])]
            bp["at"] += 1
            return i

        def stage_mla():
            w = [0]

            def al(n):
                w[0] += n
                assert w[0] <= 12800
                return WK[:, w[0] - n:w[0]]
            QN = al(2048).rearrange("p (h n) -> p h n", h=8)
            HK = QN
            KN = al(2048).rearrange("p (h n) -> p h n", h=8)
            V = al(2048).rearrange("p (b n) -> p b n", b=2)
            QR = al(1024).rearrange("p (h n) -> p h n", h=4)
            CKT = al(512).rearrange("p (c n) -> p c n", c=2)
            CQT = al(768).rearrange("p (c n) -> p c n", c=3)
            CKX = al(512).rearrange("p (b n) -> p b n", b=2)
            CQX = al(768).rearrange("p (b n) -> p b n", b=2)
            KR = al(256)
            P = al(768).rearrange("p (k n) -> p k n", k=2)
            PT = al(768).rearrange("p (k n) -> p k n", k=2)
            T1, T2 = al(256), al(256)
            cos, sin = cs("cos"), cs("sin")
            tx = norm_xs()
            th = transposed([(ve("attn"), HT), (ve("kv_in"), HK)], XS, tx)
            ik, v, tw = take((lambda v: v[:, 0:2560].rearrange("p (c n) -> p c n", c=8),
                              W["w_dkv"].rearrange("(c p) n -> p c n", p=128)))
            wk = v[:, 0:2560].rearrange("p (c n) -> p c n", c=8)
            iq, vq, twq = take((lambda v: v[:, 0:3072].rearrange("p (c n) -> p c n", c=8),
                                W["wq_down"][0].rearrange("(c p) n -> p c n", p=128)))
            wq = vq[:, 0:3072].rearrange("p (c n) -> p c n", c=8)
            for b in range(2):
                for c in range(8):
                    tk = mm(PS[:, 4, b * 256:b * 256 + 256], HK[:, c, b * 128:b * 128 + 128], wk[:, c, 0:256], c == 0,
                            c == 7, tw, th, sig=(c == 7))
            for c in range(8):
                for d in range(2):
                    mm(PS[64 * d:64 * d + 64, 5, 0:256], wk[:, c, 256:320], HK[:, c, :], c == 0, c == 7)
            for c in range(8):
                for d in range(4):
                    o = 288 if d % 2 == 0 else 256
                    tr_ = mm(PS[32 * d:32 * d + 32, 5, 256:512], wk[:, c, o:o + 32], HK[:, c, :], c == 0, c == 7,
                             sig=(c == 7 and d == 3))
            give(ik, tr_)
            for b in range(2):
                for c in range(8):
                    tq = mm(PS[:, 6 + b, 0:384], HT[:, c, b * 128:b * 128 + 128], wq[:, c, :], c == 0, c == 7, twq,
                            sig=(c == 7))
            give(iq, tq)
            ss, rs = SM[:, 8:12], SM[:, 12:16]
            for b in range(2):
                av(JK[:, 0:256], PS[:, 4, b * 256:b * 256 + 256], ACT.Square, tk, act.last(), accum_out=ss[:, b:b + 1])
            for b in range(2):
                av(JK[:, 0:384], PS[:, 6 + b, 0:384], ACT.Square, tq, act.last(), accum_out=ss[:, 2 + b:3 + b])
            t1 = rsq(rs[:, 0:2], ss[:, 0:2], 256, act.last())
            t2 = rsq(rs[:, 2:4], ss[:, 2:4], 384, act.last())
            for b in range(2):
                ta = ts(CKX[:, b, :], PS[:, 4, b * 256:b * 256 + 256], rs[:, b:b + 1], None, ALU.mult, None, t1)
                tb = av(CQX[:, b, :], PS[:, 6 + b, 0:384], ACT.Copy, t2, scale=rs[:, 2 + b:3 + b])
            t3 = tt(T1, PS[:, 5, 0:256], cos, ALU.mult, tr_)
            t4 = tt(T2, PS[:, 5, 256:512], sin, ALU.mult, tr_)
            tkr = tt(KR, T1, T2, ALU.add, t3, t4)
            for c in range(2):
                for b in range(2):
                    t = tr(PS[:, 0, c * 256 + b * 128:c * 256 + b * 128 + 128], CKX[:, b, c * 128:c * 128 + 128], 128,
                           ta, sig=(b + c == 2))
            tck = tt(CKT, PS[:, 0, :].rearrange("p (c n) -> p c n", c=2),
                     ve("kv_norm").unsqueeze(2).to_broadcast([128, 2, 256]), ALU.mult, t)
            for c in range(3):
                for b in range(2):
                    t = tr(PS[:, 1 + c // 2, (c % 2) * 256 + b * 128:(c % 2) * 256 + b * 128 + 128],
                           CQX[:, b, c * 128:c * 128 + 128], 128, tb, sig=(b == 1))
            for c in range(3):
                tcq = ts(CQT[:, c, :], PS[:, 1 + c // 2, (c % 2) * 256:(c % 2) * 256 + 256], ve("q_norm")[:, c:c + 1],
                         None, ALU.mult, None, t)
            barrier()
            bp = banks_pool(range(8))
            iu, vu, tu = take((lambda v: v[:, 0:2048].rearrange("p (c n) -> p c n", c=2),
                               W["w_uk"].rearrange("(c p) n -> p c n", p=128)),
                              (lambda v: v[:, 2048:4096].rearrange("p (c n) -> p c n", c=2),
                               W["w_uv"].rearrange("(c p) n -> p c n", p=128)))
            uk = vu[:, 0:2048].rearrange("p (c n) -> p c n", c=2)
            uv = vu[:, 2048:4096].rearrange("p (c n) -> p c n", c=2)
            for h in range(8):
                if h % 2 == 0:
                    bk = nb(bp)
                for c in range(2):
                    t = mm(PS[:, bk, (h % 2) * 256:(h % 2) * 256 + 256], uk[:, c, h * 128:h * 128 + 128], CKT[:, c, :],
                           c == 0, c == 1, tu, bp["tok"][bk], sig=(c == 1))
                if h % 2 == 1:
                    bp["tok"][bk] = cp(KN[:, h - 1:h + 1, :], PS[:, bk, :].rearrange("p (h n) -> p h n", h=2), t)
            for b in range(2):
                for hf in range(2):
                    bk = nb(bp)
                    for c in range(2):
                        t = mm(PS[:, bk, :], CKT[:, c, b * 128:b * 128 + 128], uv[:, c, hf * 512:hf * 512 + 512], c == 0,
                               c == 1, bp["tok"][bk], sig=(c == 1))
                    bp["tok"][bk] = av(V[:, b, hf * 512:hf * 512 + 512], PS[:, bk, :], ACT.Copy, t)
            give(iu, t)
            for q in range(2):
                i, v, tw = take((lambda v: v[:, 0:2304].rearrange("p (c n) -> p c n", c=3),
                                 W["wq_up"][0][:, q * 768:q * 768 + 768].rearrange("(c p) n -> p c n", p=128)))
                v = v[:, 0:2304].rearrange("p (c n) -> p c n", c=3)
                for hh in range(4):
                    h = 4 * q + hh
                    if h % 2 == 0:
                        bk = nb(bp)
                    for c in range(3):
                        t = mm(PS[:, bk, (h % 2) * 256:(h % 2) * 256 + 256], v[:, c, hh * 192:hh * 192 + 128],
                               CQT[:, c, :], c == 0, c == 2, tw, bp["tok"][bk], sig=(c == 2))
                    if h % 2 == 1:
                        bp["tok"][bk] = av(QN[:, h - 1:h + 1, :], PS[:, bk, :].rearrange("p (h n) -> p h n", h=2),
                                           ACT.Copy, t)
                for pr in range(2):
                    bk = nb(bp)
                    for c in range(3):
                        for d in range(2):
                            o = (2 * pr + d) * 192 + 128
                            mm(PS[64 * d:64 * d + 64, bk, 0:256], v[:, c, o:o + 64], CQT[:, c, :], c == 0, c == 2,
                               bp["tok"][bk])
                    for c in range(3):
                        for d in range(4):
                            o = (2 * pr + d // 2) * 192 + 128 + (32 if d % 2 == 0 else 0)
                            t = mm(PS[32 * d:32 * d + 32, bk, 256:512], v[:, c, o:o + 32], CQT[:, c, :], c == 0, c == 2,
                                   sig=(c == 2 and d == 3))
                    t3 = tt(T1, PS[:, bk, 0:256], cos, ALU.mult, t, dve.last())
                    bp["tok"][bk] = t4 = tt(T2, PS[:, bk, 256:512], sin, ALU.mult, t)
                    tt(QR[:, 2 * q + pr, :], T1, T2, ALU.add, t3, t4)
                give(i, t)
            barrier()
            OT = HT
            scale = 1.0 / math.sqrt(192.0)
            mask = cs("mask")
            pt, pv, prob = {}, {}, {}
            bt = {bk: None for bk in range(8)}

            def scores(h):
                bk = h % 2
                pr, dp = h // 2, 64 * (h % 2)
                for i in range(2):
                    o = PS[:, bk, 0:128] if i == 0 else PS[:, bk, 128:384]
                    n = 128 + 128 * i
                    mm(o, QN[:, h, i * 128:i * 128 + 128], KN[:, h, 0:n], True, False, bt[bk])
                    t = mm(o, QR[dp:dp + 64, pr, i * 128:i * 128 + 128], KR[dp:dp + 64, 0:n], False, True, sig=True)
                p = P[:, h % 2, :]
                bt[bk] = t = stt(p, PS[:, bk, 0:384], scale, mask, ALU.mult, ALU.add, t, prob.get(h - 2))
                m, s = SM[:, 32 + 2 * (h % 2):34 + 2 * (h % 2)], SM[:, 40 + 2 * (h % 2):42 + 2 * (h % 2)]
                for i, (a, z) in enumerate(((0, 128), (128, 384))):
                    tm = dve(lambda e, i=i, a=a, z=z: e.tensor_reduce(m[:, i:i + 1], p[:, a:z], AX.X, ALU.max,
                                                                      negate=True), t)
                for i, (a, z) in enumerate(((0, 128), (128, 384))):
                    te = av(p[:, a:z], p[:, a:z], ACT.Exp, tm, bias=m[:, i:i + 1], accum_out=s[:, i:i + 1])
                tr1 = dve(lambda e: e.reciprocal(s, s), te)
                for i, (a, z) in enumerate(((0, 128), (128, 384))):
                    pt[h] = ts(p[:, a:z], p[:, a:z], s[:, i:i + 1], None, ALU.mult, None, tr1)

            def values(h):
                bk = 2 + h % 2
                p = P[:, h % 2, :]
                for j in range(3):
                    t = tr(PS[:, bk, j * 128:j * 128 + 128], p[:, j * 128:j * 128 + 128], 128, pt[h], bt[bk],
                           sig=(j == 2))
                prob[h] = t
                bt[bk] = t = av(PT[:, h % 2, :], PS[:, bk, 0:384], ACT.Copy, t, pv.get(h - 2))
                q = PT[:, h % 2, :]
                bo = 4 + h % 2
                v0, v1 = V[:, 0, h * 128:h * 128 + 128], V[:, 1, h * 128:h * 128 + 128]
                mm(PS[:, bo, 0:128], v0, q[:, 0:128], True, True, t, bt[bo])
                mm(PS[:, bo, 128:256], v0, q[:, 128:256], True, False)
                pv[h] = mm(PS[:, bo, 128:256], v1, q[:, 256:384], False, True, sig=True)
                bt[bo] = cp(OT[:, h, :], PS[:, bo, 0:256], pv[h])
            for h in range(9):
                if h < 8:
                    scores(h)
                if h:
                    values(h - 1)
            barrier()
            out_proj(W["wo"][0], OT)
            for b in range(2):
                tt(X[:, b, :].rearrange("p (a n) -> p a n", a=2), X[:, b, :].rearrange("p (a n) -> p a n", a=2),
                   PS[:, 2 * b:2 * b + 2, :], ALU.add, pe.last())

        def out_proj(w, src):
            for s in range(2):
                i, v, tw = take((lambda v: v.rearrange("p (c n) -> p c n", c=4),
                                 w[512 * s:512 * s + 512, :].rearrange("(c p) n -> p c n", p=128)))
                v = v.rearrange("p (c n) -> p c n", c=4)
                for c in range(4):
                    for b in range(2):
                        for h in range(2):
                            t = mm(PS[:, 2 * b + h, :], src[:, 4 * s + c, b * 128:b * 128 + 128],
                                   v[:, c, h * 512:h * 512 + 512], s + c == 0, s * 4 + c == 7, tw, sig=(b + h == 2))
                give(i, t)
            return t

        def out_proj3(th):
            for s in range(4):
                hi, lo, tsp, key = next_split()
                for c in range(2):
                    f = 2 * s + c
                    for b in range(2):
                        for h in range(2):
                            t = mm3(PS[:, 4 + 2 * b + h, :],
                                    (HTH[:, f, b * 128:b * 128 + 128], HTL[:, f, b * 128:b * 128 + 128]),
                                    (hi[:, c, h * 512:h * 512 + 512], lo[:, c, h * 512:h * 512 + 512]),
                                    f == 0, f == 7, tsp, th[f], sig=(b + h == 2))
                sp_free[key] = t
            return t

        def stage_mix(l):
            ring(4)
            rt = row(f"ng{l}3", RB[:, 2, :], dve.last())
            lo, lw = ROWS[f"lam{l}"]
            w = [0]

            def al(n):
                w[0] += n
                assert w[0] <= 12800, w[0]
                return WK[:, w[0] - n:w[0]]
            DQ = al(1024).rearrange("p (h n) -> p h n", h=4)
            DK = al(1024).rearrange("p (h n) -> p h n", h=4)
            DV = al(1024).rearrange("p (b n) -> p b n", b=2)
            QK = al(4 * 260).rearrange("p (c n) -> p c n", c=4)
            CO = al(1024).rearrange("p (c n) -> p c n", c=4)
            MV = al(8 * 129).rearrange("p (b h n) -> p b h n", b=2, h=4)
            SO = al(1024).rearrange("p (b n) -> p b n", b=2)
            GI, GF, FC, U, MM, NEM, T5 = (al(256) for _ in range(7))
            P = al(4 * 384).rearrange("p (k c n) -> p k c n", k=2, c=2)
            AT = al(768).rearrange("p (k n) -> p k n", k=2)
            LR = al(256)
            GTM = al(16)
            UT = al(8).rearrange("p (b h) -> p b h", b=2)
            NT = al(8).rearrange("p (b h) -> p b h", b=2)
            LT = al(8)
            T1 = al(512)
            R2 = al(256)
            TQ = T1.rearrange("p (k n) -> p k n", k=2)
            YO = XS
            cos, sin = cs("cos"), cs("sin")
            lam_init = 0.8 - 0.6 * math.exp(-0.3 * l)
            tl = dma_sem_load(f"d_lam{l}", LR, W["rows"][0:1, lo:lo + lw].to_broadcast([128, lw]), dve.last())
            tx = norm_xs()
            th = transposed3(ve(f"ng{l}2"), XS, tx)
            t = tt(T1[:, 0:128].rearrange("p (a n) -> p a n", a=2), LR.rearrange("p (a k n) -> p a k n", a=2, k=2)[:, :, 0, :],
                   LR.rearrange("p (a k n) -> p a k n", a=2, k=2)[:, :, 1, :], ALU.mult, tl)
            t = dve(lambda e: e.tensor_reduce(LT[:, 0:2], T1[:, 0:128].rearrange("p (a n) -> p a n", a=2), AX.X, ALU.add), t)
            t = av(LT[:, 2:4], LT[:, 0:2], ACT.Exp, t)
            t = tt(LT[:, 4:5], LT[:, 2:3], LT[:, 3:4], ALU.subtract, t)
            tlam = ts(LT[:, 4:5], LT[:, 4:5], lam_init, None, ALU.add, None, t)
            NLAM = LT[:, 4:5]
            bp = banks_pool(range(4, 8))
            bk = nb(bp)
            t1 = av(GWH[:, :], ve(f"gw{l}"), ACT.Copy)
            t2 = tt(GWL[:, :], ve(f"gw{l}"), GWH[:, :].bitcast(F32), ALU.subtract, t1)
            for b in range(2):
                for c in range(8):
                    t = mm3(PS[:, bk, b * 8:b * 8 + 8], (HTH[:, c, b * 128:b * 128 + 128], HTL[:, c, b * 128:b * 128 + 128]),
                            (GWH[:, 8 * c:8 * c + 8], GWL[:, 8 * c:8 * c + 8]), c == 0, c == 7, t1, t2, th[c],
                            sig=(c == 7))
            tz = bp["tok"][bk] = cp(GTM, PS[:, bk, 0:16], t)
            bk = nb(bp)
            for n in range(2):
                for b in range(2):
                    t = tr(PS[0:4, bk, n * 256 + b * 128:n * 256 + b * 128 + 128], GTM[:, b * 8 + 4 * n:b * 8 + 4 * n + 4],
                           128, tz, bp["tok"][bk], sig=(n + b == 2))
            gb = ve(f"gb{l}")
            r4 = slice(0, 4)
            ta = ts(GI[r4, :], PS[0:4, bk, 0:256], gb[r4, 0:1], None, ALU.add, None, t)
            tb = ts(GF[r4, :], PS[0:4, bk, 256:512], gb[r4, 1:2], None, ALU.add, None, t)
            bp["tok"][bk] = tb
            t = stt(FC[r4, :], GF[r4, :], -1.0, GF[r4, :], ALU.mult, ALU.max, tb)
            t = av(T5[r4, :], FC[r4, :], ACT.Exp, t, scale=-1.0)
            t = av(T5[r4, :], T5[r4, :], ACT.Ln, t, bias=1.0)
            t = stt(GF[r4, :], GF[r4, :], 0.0, T5[r4, :], ALU.min, ALU.subtract, t)
            tF = dve(lambda e: e.tensor_tensor_scan(FC[r4, :], GF[r4, :], GF[r4, :], 0.0, ALU.add, ALU.bypass), t)
            tU = tt(U[r4, :], GI[r4, :], FC[r4, :], ALU.subtract, tF, ta)
            tM = dve(lambda e: e.tensor_tensor_scan(MM[r4, :], U[r4, :], U[r4, :], 0.0, ALU.max, ALU.bypass), tU)
            t = tt(NEM[r4, :], FC[r4, :], MM[r4, :], ALU.add, tM)
            tN = av(NEM[r4, :], NEM[r4, :], ACT.Exp, t, scale=-1.0)
            tM = ts(MM[r4, :], MM[r4, :], -1.0, None, ALU.mult, None, t)
            pend = []

            def rotate():
                if pend:
                    bk, dst, k, tq = pend.pop()
                    t = mm(PS[:, bk, 256:512], cs("swap"), TQ[:, k, :], True, True, tq, sig=True)
                    t3 = tt(dst, TQ[:, k, :], cos, ALU.mult, tq)
                    t4 = bp["tok"][bk] = tt(R2, PS[:, bk, 256:512], sin, ALU.mult, t, rot[0])
                    rot[0] = rot[k + 1] = tt(dst, dst, R2, ALU.add, t3, t4)
            rot = {0: None, 1: None, 2: None}
            for n, dst in ((0, DQ), (1, DK)):
                for hs in range(2):
                    hi, lo, tsp, key = next_split()
                    for hh in range(2):
                        h = 2 * hs + hh
                        bk = nb(bp)
                        for c in range(8):
                            t = mm3(PS[:, bk, 0:256], (hi[:, c, hh * 128:hh * 128 + 128], lo[:, c, hh * 128:hh * 128 + 128]),
                                    (HTH[:, c, :], HTL[:, c, :]), c == 0, c == 7, tsp, bp["tok"][bk], th[c],
                                    sig=(c == 7))
                        tq = av(TQ[:, hh, :], PS[:, bk, 0:256], ACT.Copy, t, rot[hh + 1])
                        rotate()
                        pend.append((bk, dst[:, h, :], hh, tq))
                    sp_free[key] = t

            def token_major(evac):
                bks = [nb(bp), nb(bp)]
                for hs in range(2):
                    hi, lo, tsp, key = next_split()
                    for cc in range(4):
                        c = 4 * hs + cc
                        for b in range(2):
                            t = mm3(PS[:, bks[b], :], (HTH[:, c, b * 128:b * 128 + 128], HTL[:, c, b * 128:b * 128 + 128]),
                                    (hi[:, cc, :], lo[:, cc, :]), c == 0, c == 7, tsp, bp["tok"][bks[b]],
                                    sig=(cc == 3))
                    sp_free[key] = t
                for b in range(2):
                    bp["tok"][bks[b]] = evac(b, PS[:, bks[b], :], t)
            rotate()
            token_major(lambda b, ps, t: av(DV[:, b, :], ps, ACT.Copy, t))
            tz = dve(lambda e: e.memset(QK[:, :, 0:3], 0.0))
            cw, cb = ve(f"cw{l}"), ve(f"cb{l}")
            for h in range(4):
                bk = nb(bp)
                if h % 2 == 0:
                    hi, lo, tsp, key = next_split()
                o = (h % 2) * 128
                for c in range(8):
                    t = mm3(PS[:, bk, 0:256], (hi[:, c, o:o + 128], lo[:, c, o:o + 128]), (HTH[:, c, :], HTL[:, c, :]),
                            c == 0, c == 7, tsp, bp["tok"][bk], sig=(c == 7))
                sp_free[key] = t
                t = bp["tok"][bk] = av(QK[:, h, 3:259], PS[:, bk, 0:256], ACT.Copy, t)
                t = ts(CO[:, h, :], QK[:, h, 0:256], cw[:, h:h + 1], cb[:, h:h + 1], ALU.mult, ALU.add, t, tz)
                for j in range(1, 4):
                    t = stt(CO[:, h, :], QK[:, h, j:j + 256], cw[:, 4 * j + h:4 * j + h + 1], CO[:, h, :], ALU.mult,
                            ALU.add, t)
                tco = av(CO[:, h, :], CO[:, h, :], ACT.Silu, t)
            tz = dve(lambda e: e.memset(MV[:, :, :, 128:129], 1.0))
            token_major(lambda b, ps, t: cp(MV[:, b, :, 0:128], ps.rearrange("p (h n) -> p h n", h=4), t))
            token_major(lambda b, ps, t: av(SO[:, b, :], ps, ACT.Sigmoid, t))
            bk = nb(bp)
            for b in range(2):
                tr(PS[:, bk, b * 4:b * 4 + 4], U[0:4, b * 128:b * 128 + 128], 4, tU, bp["tok"][bk])
                t = tr(PS[:, bk, 8 + b * 4:12 + b * 4], NEM[0:4, b * 128:b * 128 + 128], 4, tN, sig=True)
            cp(UT, PS[:, bk, 0:8].rearrange("p (b h) -> p b h", b=2), t)
            cp(NT, PS[:, bk, 8:16].rearrange("p (b h) -> p b h", b=2), t)
            barrier()
            mask = cs("mask")
            bt = {bk: None for bk in range(8)}
            at, av_, pu = {}, {}, {}

            def scores(h):
                ex = []
                for d in range(2):
                    bk = 2 * (h % 2) + d
                    for i in range(2):
                        o = PS[:, bk, 0:128] if i == 0 else PS[:, bk, 128:384]
                        t = mm(o, DQ[64 * d:64 * d + 64, h, i * 128:i * 128 + 128],
                               DK[64 * d:64 * d + 64, h, 0:128 + 128 * i], True, True, bt[bk], sig=True)
                    p = P[:, h % 2, d, :]
                    bt[bk] = t = stt(p, PS[:, bk, 0:384], 0.125, mask, ALU.mult, ALU.add, t, pu.get(h - 2))
                    q = 4 * (h % 2) + 2 * d
                    m, s = SM[:, 32 + q:34 + q], SM[:, 40 + q:42 + q]
                    for i, (a, z) in enumerate(((0, 128), (128, 384))):
                        tm = dve(lambda e, i=i, a=a, z=z, m=m, p=p: e.tensor_reduce(m[:, i:i + 1], p[:, a:z], AX.X,
                                                                                     ALU.max, negate=True), t)
                    for i, (a, z) in enumerate(((0, 128), (128, 384))):
                        te = av(p[:, a:z], p[:, a:z], ACT.Exp, tm, bias=m[:, i:i + 1], accum_out=s[:, i:i + 1])
                    tr1 = dve(lambda e, s=s: e.reciprocal(s, s), te)
                    if d:
                        tr1 = ts(s, s, NLAM, None, ALU.mult, None, tr1)
                        for i, (a, z) in enumerate(((0, 128), (128, 384))):
                            t5 = ts(p[:, a:z], p[:, a:z], s[:, i:i + 1], None, ALU.mult, None, tr1)
                        q0 = 4 * (h % 2)
                        s0 = SM[:, 40 + q0:42 + q0]
                        for i, (a, z) in enumerate(((0, 128), (128, 384))):
                            at[h] = stt(P[:, h % 2, 0, a:z], P[:, h % 2, 0, a:z], s0[:, i:i + 1], p[:, a:z], ALU.mult,
                                        ALU.subtract, t5)

            def values(h):
                bk = 4 + h % 2
                for j in range(3):
                    t = tr(PS[:, bk, j * 128:j * 128 + 128], P[:, h % 2, 0, j * 128:j * 128 + 128], 128, at[h], bt[bk],
                           sig=(j == 2))
                pu[h] = t
                bt[bk] = t = av(AT[:, h % 2, :], PS[:, bk, 0:384], ACT.Copy, t, av_.get(h - 2))
                a = AT[:, h % 2, :]
                bo = 6 + h % 2
                v0, v1 = DV[:, 0, h * 128:h * 128 + 128], DV[:, 1, h * 128:h * 128 + 128]
                mm(PS[:, bo, 0:128], a[:, 0:128], v0, True, True, t, bt[bo])
                mm(PS[:, bo, 128:256], a[:, 128:256], v0, True, False)
                av_[h] = mm(PS[:, bo, 128:256], a[:, 256:384], v1, False, True, sig=True)
                bt[bo] = cp(YO[:, :, h * 128:h * 128 + 128], PS[:, bo, 0:256].rearrange("p (b n) -> p b n", b=2), av_[h])
            for h in range(5):
                if h < 4:
                    scores(h)
                if h:
                    values(h - 1)
            barrier()
            bt = {bk: None for bk in range(8)}
            E = P[:, :, 0, :]
            sel = cs("sel")
            caus = cs("caus")
            tw_, nu = {}, {}

            def wts(h):
                k = h % 2
                dp, ch = 64 * (h % 2), h // 2
                b0, b1 = 2 * k, 2 * k + 1
                mm(PS[:, b0, 0:256], sel[0:4, h * 128:h * 128 + 128], MM[0:4, :], True, True, bt[b0])
                t0 = mm(PS[:, b0, 256:384], sel[0:4, h * 128:h * 128 + 128], MM[0:4, 128:256], True, True, sig=True)
                mm(PS[:, b1, 0:256], CO[dp:dp + 64, 2 + ch, 0:128], CO[dp:dp + 64, ch, :], True, True, bt[b1])
                t1 = mm(PS[:, b1, 256:384], CO[dp:dp + 64, 2 + ch, 128:256], CO[dp:dp + 64, ch, 128:256], True, True,
                        sig=True)
                e = E[:, k, :]
                ta = ts(e[:, 0:256], PS[:, b0, 0:256], UT[:, 0, h:h + 1], 0.0, ALU.add, ALU.min, t0, nu.get(h - 2))
                tb = ts(e[:, 256:384], PS[:, b0, 256:384], UT[:, 1, h:h + 1], 0.0, ALU.add, ALU.min, t0)
                bt[b0] = tb
                te = av(e, e, ACT.Exp, ta, tb)
                t = stt(e, PS[:, b1, 0:384], 0.125, e, ALU.mult, ALU.mult, te, t1)
                bt[b1] = t
                tt(e[:, 0:128], e[:, 0:128], caus, ALU.mult, t)
                tw_[h] = tt(e[:, 256:384], e[:, 256:384], caus, ALU.mult, t)

            def num(h):
                k = h % 2
                e = E[:, k, :]
                bo = 4 + k
                mm(PS[:, bo, 0:129], e[:, 0:128], MV[:, 0, h, :], True, True, tw_[h], bt[bo])
                mm(PS[:, bo, 129:258], e[:, 128:256], MV[:, 0, h, :], True, False)
                nu[h] = t = mm(PS[:, bo, 129:258], e[:, 256:384], MV[:, 1, h, :], False, True, sig=True)
                o = PS[:, bo, 0:258].rearrange("p (b n) -> p b n", b=2)
                dn = SM[:, 64 + 2 * h:66 + 2 * h]
                t = ts(dn, o[:, :, 128], -1.0, None, ALU.mult, None, t)
                t = tt(dn, dn, o[:, :, 128], ALU.max, t)
                t = tt(dn, dn, NT[:, :, h], ALU.max, t)
                t = dve(lambda e_: e_.reciprocal(dn, dn), t)
                bt[bo] = tt(YO[:, :, 512 + h * 128:640 + h * 128], o[:, :, 0:128],
                            dn.unsqueeze(2).to_broadcast([128, 2, 128]), ALU.mult, t)
            for h in range(5):
                if h < 4:
                    wts(h)
                if h:
                    num(h - 1)
            ss, rs = SM[:, 80:96], SM[:, 96:112]
            for b in range(2):
                t = av(JK[:, :], YO[:, b, :], ACT.Square, dve.last(), act.last())
                t = dve(lambda e, b=b: e.tensor_reduce(ss[:, 8 * b:8 * b + 8], JK[:, :].rearrange("p (h n) -> p h n", h=8),
                                                       AX.X, ALU.add), t)
                act.wait(t)
            t = rsq(rs, ss, 128, t)
            rv = rs.rearrange("p (b h) -> p b h", b=2)
            t = ts(rv[:, :, 0:4], rv[:, :, 0:4], 1.0 - lam_init, None, ALU.mult, None, t)
            for b in range(2):
                y = YO[:, b, :].rearrange("p (h n) -> p h n", h=8)
                ta = tt(y, y, rv[:, b, :].unsqueeze(2).to_broadcast([128, 8, 128]), ALU.mult, t)
                ty = tt(YO[:, b, 512:1024], YO[:, b, 512:1024], SO[:, b, :], ALU.mult, ta)
            barrier()
            th = transposed3(ve(f"yg{l}"), YO, [ty])
            t = out_proj3(th)
            dve.wait(rt)
            post_norm((4, 6), RB[:, 2, :], 1.0, [t])

        stages = {"pool": stage_pool, "moe0": lambda: stage_moe(0), "moe1": lambda: stage_moe(1), "mla": stage_mla,
                  "fin": stage_fin, "mix0": lambda: stage_mix(0), "mix1": lambda: stage_mix(1)}
        for l in range(2):
            for k in range(2):
                stages[f"ffn{l}{k}"] = lambda l=l, k=k: stage_ffn(l, k)
        for name in plan:
            if name.startswith("ffn"):
                want_ffn(int(name[3]), int(name[4]))
            elif name.startswith("mix"):
                want_mix(int(name[3]))
        for name in plan:
            stages[name]()
            barrier()

        for i in range(len(loads) + 1):
            if i in breaks:
                sp.wait(breaks[i][0])
                sp.ops.append(breaks[i][1])
            if i == len(loads):
                break
            s, parts = loads[i]
            before, over = prior[i]
            if before is not None:
                sp.wait(freed[before])
            sp.wait(over)
            for dst, src in parts:
                sp.ops.append(lambda e, dst=dst, src=src, s=s: e.dma_start(dst, src).then_inc(slot_sem[s], 16))
        s_out = sem("s_out")
        sp.wait(dve.last(), act.last(), pe.last())
        sp.ops.append(lambda e: e.dma_start(W["out"].rearrange("(b p) n -> p b n", p=128), X[:, :, :]).then_inc(s_out, 16))
        sp.ops.append(lambda e: e.wait_ge(s_out, 16))

        block = ctx.enter_context(nc.Block())

        @block.sync
        def _(e):
            sp.play(e)

        @block.tensor
        def _(e):
            pe.play(e)

        @block.vector
        def _(e):
            dve.play(e)

        @block.scalar
        def _(e):
            act.play(e)

        @block.gpsimd
        def _(e):
            pool.play(e)


def constants():
    cst = np.zeros((128, NCST), np.float32)

    def put(name, a):
        o, w = CST[name]
        cst[:a.shape[0], o:o + w] = a
    p = np.arange(128)
    put("ident", np.eye(128, dtype=np.float32))
    put("tri", (p[:, None] < p[None, :]).astype(np.float32))
    put("ones", np.ones((128, 128), np.float32))
    put("caus", (p[:, None] <= p[None, :]).astype(np.float32))
    k = np.arange(256)
    m0 = np.where(k[None, :128] // 64 <= p[:, None] // 64, 0.0, NEG)
    m1 = np.where(k[None, :] // 64 <= (p[:, None] + 128) // 64, 0.0, NEG)
    put("mask", np.concatenate([m0, m1], 1).astype(np.float32))
    inv = np.float32(10000.0) ** (-np.arange(32, dtype=np.float32) / np.float32(32))
    ang = (np.arange(256, dtype=np.float32)[None, :] * inv[:, None]).astype(np.float32)
    co, si = np.cos(ang), np.sin(ang)
    put("cos", np.concatenate([co, co, co, co], 0))
    put("sin", np.concatenate([-si, si, -si, si], 0))
    put("iota", np.broadcast_to(np.arange(32, dtype=np.float32), (128, 32)))
    sel = np.zeros((4, 4, 128), np.float32)
    for h in range(4):
        sel[h, h, :] = 1.0
    put("sel", sel.reshape(4, 512))
    put("swap", (p[:, None] == (p[None, :] ^ 32)).astype(np.float32))
    pm = np.zeros((2, 128, 4, 256), np.float32)
    for g, win in enumerate((2, 4, 8, 16)):
        for t in range(256):
            lo = max(t + 1 - win, 0)
            for s in range(lo, t + 1):
                pm[s // 128, s % 128, g, t] = 1.0 / (t + 1 - lo)
            pm[t // 128, t % 128, g, t] -= 1.0
    return cst, np.ascontiguousarray(pm.transpose(1, 0, 2, 3).reshape(128, 2048))


def layouts(a):
    vec = np.zeros((128, NVEC), np.float32)

    def put(name, v):
        o, w = VEC[name]
        vec[:v.shape[0], o:o + w] = v
    for name, v in (("pool_norm", a["pool_norm"][0]), ("kv_in", a["kv_in_norm"]), ("attn", a["attn_norm"][0]),
                    ("ffn0", a["ffn_norm"][0]), ("ffn1", a["ffn_norm"][1]), ("kv_norm", a["kv_norm"]),
                    ("q_norm", a["q_norm"][0])):
        put(name, v.reshape(-1, 128).T)
    ng = a["norm_gains_2"]
    for l in range(2):
        for k in (0, 2, 4):
            put(f"ng{l}{k}", ng[l, k].reshape(8, 128).T)
        put(f"yg{l}", np.stack([a["da_subln_g_2"][l]] * 4 + [a["ml_norm_g_2"][l]] * 4, 1))
        put(f"cw{l}", a["ml_conv_w_2"][l].reshape(16, 128).T)
        put(f"cb{l}", a["ml_conv_b_2"][l].reshape(4, 128).T)
        put(f"gb{l}", a["ml_gate_b_2"][l].reshape(2, 4).T)
        put(f"gw{l}", a["mix_w_in_2"][l][:, 3072:].reshape(8, 128, 8).transpose(1, 0, 2).reshape(128, 64))
        rw = np.concatenate([a["router_group_w"][l], a["router_expert_w"][l]], 1)
        put(f"rw{l}", rw.reshape(8, 128, 36).transpose(1, 0, 2).reshape(128, 288))
    rows = np.zeros((1, NROWS), np.float32)

    def rput(name, v):
        o, w = ROWS[name]
        rows[0, o:o + w] = v.reshape(-1)
    rput("pool_b", a["pool_b"])
    rput("pool_scale", a["pool_scale"])
    rput("final", a["final_norm"])
    for l in range(2):
        rput(f"r{l}", np.concatenate([a["router_group_b"][l], a["router_expert_b"][l]]))
        rput(f"lam{l}", a["da_lambda_2"][l])
        for k in (1, 3, 5):
            rput(f"ng{l}{k}", ng[l, k])
    return vec, rows


BIGS = [("pool_w", "pool_w"), ("w_dkv", "w_dkv"), ("w_uk", "w_uk"), ("w_uv", "w_uv"), ("wq_down", "wq_down"),
        ("wq_up", "wq_up"), ("wo", "wo"), ("w_gate", "w_gate"), ("w_up", "w_up"), ("w_down", "w_down"),
        ("ffn_w_in", "ffn_w_in_2"), ("ffn_w_out", "ffn_w_out_2"), ("mix_w_in", "mix_w_in_2"),
        ("mix_w_out", "mix_w_out_2")]


def feeds(inputs):
    a = {k: np.asarray(v) for k, v in inputs.items()}
    cst, pm = constants()
    vec, rows = layouts(a)
    f = {"cst": cst, "pm": pm, "vec": vec, "rows": rows, "x": np.ascontiguousarray(a["x"].reshape(256, 1024))}
    for k, n in BIGS:
        f[k] = np.ascontiguousarray(a[n])
    return f


def declare(nc, f):
    W = {k: nc.dram_tensor("in_" + k, v.shape, mybir.dt.from_np(v.dtype), kind="ExternalInput").ap()
         for k, v in f.items()}
    W["out"] = nc.dram_tensor("out_0_dram", (256, 1024), F32, kind="ExternalOutput").ap()
    return W


def kernel(**inputs):
    import concourse.bacc as _bacc
    from concourse.bass_utils import run_bass_kernel_spmd as _run

    f = feeds(inputs)
    nc = _bacc.Bacc("TRN2", target_bir_lowering=False, num_devices=1)
    W = declare(nc, f)
    build(nc, W, PLAN)
    r = _run(nc, [{"in_" + k: v for k, v in f.items()}], core_ids=[0])
    return r.results[0]["out_0_dram"].reshape(1, 256, 1024)
```

```python
import math
from contextlib import ExitStack

import numpy as np

import concourse.bass as bass
from concourse import mybir

F32 = mybir.dt.float32
F32R = mybir.dt.float32r
U32 = mybir.dt.uint32
ALU = mybir.AluOpType
ACT = mybir.ActivationFunctionType
AX = mybir.AxisListType

EPS = 1e-6
NS = 7
HOME = 6
SLOT = 4096
C = 32
CAP = 32
NEG = -1e30
BIG = 65536.0

VEC = {}
_o = 0
for _n, _w in [("pool_norm", 8), ("kv_in", 8), ("attn", 8), ("ffn0", 8), ("ffn1", 8),
               ("ng00", 8), ("ng02", 8), ("ng04", 8), ("ng10", 8), ("ng12", 8), ("ng14", 8),
               ("kv_norm", 2), ("q_norm", 3), ("yg0", 8), ("yg1", 8),
               ("cw0", 16), ("cw1", 16), ("cb0", 4), ("cb1", 4), ("gb0", 2), ("gb1", 2),
               ("rw0", 288), ("rw1", 288),
               ("gw0", 64), ("gw1", 64)]:
    VEC[_n] = (_o, _w)
    _o += _w
NVEC = _o
CST = {}
_o = 0
for _n, _w in [("ident", 128), ("tri", 128), ("ones", 128), ("caus", 128), ("mask", 384),
               ("cos", 256), ("sin", 256), ("iota", 32), ("sel", 512), ("swap", 128)]:
    CST[_n] = (_o, _w)
    _o += _w
NCST = _o
ROWS = {}
_o = 0
for _n, _w in [("pool_b", 1024), ("pool_scale", 1024), ("final", 1024), ("r0", 36), ("r1", 36),
               ("lam0", 256), ("lam1", 256), ("ng01", 1024), ("ng03", 1024), ("ng05", 1024),
               ("ng11", 1024), ("ng13", 1024), ("ng15", 1024)]:
    ROWS[_n] = (_o, _w)
    _o += _w
NROWS = _o
PLAN = ["pool", "moe0", "mla", "moe1", "fin", "ffn00", "mix0", "ffn01", "ffn10", "mix1", "ffn11"]


class Eng:

    def __init__(self, sem):
        self.sem, self.n, self.ops, self.seen = sem, 0, [], {}

    def wait(self, *toks):
        for t in toks:
            if t is None:
                continue
            if isinstance(t, list):
                self.wait(*t)
                continue
            sem, v = t
            if v > 0 and self.seen.get(sem.name, 0) < v:
                self.seen[sem.name] = v
                self.ops.append(lambda e, sem=sem, v=v: e.wait_ge(sem, v))

    def __call__(self, fn, *toks, sig=True):
        self.wait(*toks)
        if sig:
            self.n += 1
            self.ops.append(lambda e: fn(e).then_inc(self.sem, 1))
        else:
            self.ops.append(fn)
        return (self.sem, self.n)

    def last(self):
        return (self.sem, self.n)

    def play(self, e):
        for op in self.ops:
            op(e)


def build(nc, W, plan):
    ctx = ExitStack()
    with ctx:
        top = [(nc.sbuf_base + 63) // 64 * 64]

        def sb(name, shape, dt=F32, at=None):
            size = int(np.prod(shape[1:])) * 4
            off = top[0] if at is None else at
            if at is None:
                place[name] = off
                top[0] = (off + size + 31) // 32 * 32
            return nc.alloc_sbuf_tensor_at(name, shape, dt, offset=off)
        place = {}

        def sem(name):
            return ctx.enter_context(nc.semaphore(name))

        RING = sb("RING", [128, HOME, SLOT])
        X = sb("X", [128, 2, 1024])
        XS = sb("XS", [128, 2, 1024])
        HT = sb("HT", [128, 8, 256])
        CS = sb("CS", [128, NCST])
        VE = sb("VE", [128, NVEC])
        RB = sb("RB", [128, 3, 1024])
        RR = sb("RR", [128, 72])
        JK = sb("JK", [128, 1024])
        SM = sb("SM", [128, 512])
        MH = sb("MH", [128, 16])
        WK = sb("WK", [128, 13440])
        IX = sb("IX", [128, 32], U32)
        FLAG = sb("FLAG", [128, 2], U32)
        WH = sb("WH", [128, 2, 2048], F32R, at=place["RING"] + 4 * SLOT * 4)
        WL = sb("WL", [128, 2, 2048], F32R, at=place["RING"] + 5 * SLOT * 4)
        HTH = sb("HTH", [128, 8, 256], F32R, at=place["HT"])
        HTL = sb("HTL", [128, 8, 256], F32R, at=place["XS"])
        WR = sb("WR", [128, 13440], F32R, at=place["WK"])
        HFH = sb("HFH", [128, 22, 256], F32R, at=place["WK"])
        HFL = sb("HFL", [128, 22, 256], F32R, at=place["WK"] + 22 * 1024)
        GWH = sb("GWH", [128, 64], F32R)
        GWL = sb("GWL", [128, 64], F32R)
        PS = ctx.enter_context(nc.psum_tensor("PS", [128, 8, 512], F32))

        pe, act, dve, pool, sp = (Eng(sem(n)) for n in ("s_pe", "s_act", "s_dve", "s_pool", "s_sp"))
        slot_sem = [sem(f"s_slot{i}") for i in range(NS)]

        def cs(name, p=128):
            o, w = CST[name]
            return CS[0:p, o:o + w]

        def ve(name):
            o, w = VEC[name]
            return VE[:, o:o + w]

        sent, got, read_row = [0], {}, {}
        loads, freed, slot_n, breaks = [], {}, [0] * NS, {}
        active, at_slot, prior, slot_user, cover = [list(range(NS))], [0], {}, {}, {}

        def take(*parts):
            i = len(loads)
            s = active[0][at_slot[0] % len(active[0])]
            at_slot[0] += 1
            prior[i] = [slot_user.get(s), cover.pop(s, None)]
            slot_user[s] = i
            view = RING[:, s, :] if s < HOME else WK[:, 13440 - SLOT:13440]
            slot_n[s] += 16 * len(parts)
            loads.append((s, [(d(view), src) for d, src in parts]))
            return i, view, (slot_sem[s], slot_n[s])

        def give(i, tok):
            freed[i] = tok

        def enter_break(i):
            sp.wait(breaks[i][0])
            sp.ops.append(breaks[i][1])

        def issue_loads(n):
            for i in range(sent[0], n):
                if i in breaks:
                    enter_break(i)
                s, parts = loads[i]
                before, over = prior[i]
                if before is not None:
                    sp.wait(freed[before])
                sp.wait(over)
                for dst, src in parts:
                    sp.ops.append(lambda e, dst=dst, src=src, s=s: e.dma_start(dst, src).then_inc(slot_sem[s], 16))
            sent[0] = n

        def ring(n):
            now = active[0]
            if n == len(now):
                return
            turn = [now[(at_slot[0] + k) % len(now)] for k in range(len(now))]
            if n == NS:
                for s in range(4, NS):
                    cover[s] = [dve.last(), act.last(), pe.last()]
            else:
                fresh[0] = 2
            active[0] = [s for s in turn if s < n] + [s for s in range(n) if s not in turn]
            at_slot[0] = 0

        sp_n, sp_free, fresh = [0], {}, [0]

        def split(src, shape, tw, mid):
            k = sp_n[0] % 2
            sp_n[0] += 1
            a, n = shape[0], int(np.prod(shape))
            flat = [z[:, k, 0:n].rearrange("p (a b) -> p a b", a=a) for z in (WH, WL)]
            hi, lo = flat if len(shape) == 2 else [
                z.rearrange("p a (b c) -> p a b c", b=shape[1]) for z in flat]
            before = sp_free.get(sp_n[0] - 2)
            if fresh[0]:
                fresh[0] -= 1
                before = [freed.get(slot_user.get(s)) for s in (4, 5)]
            t1 = av(hi, src, ACT.Copy, tw, before)
            if mid:
                mid()
            t2 = tt(lo, src, hi.bitcast(F32), ALU.subtract, t1, before)
            hi, lo = flat
            return hi, lo, [t1, t2], sp_n[0]

        wanted, issued = [], []

        def issue(mid=None):
            if not wanted:
                if mid:
                    mid()
            else:
                src, shape, tw, last = wanted.pop(0)()
                got = split(src, shape, tw, mid)
                if last is not None:
                    give(last, got[2])
                issued.append(got)

        def next_split(mid=None):
            if not issued:
                issue()
            issue(mid)
            return issued.pop(0)

        def want_slabs(w, o, n, rows, cut, halves):
            box = {}

            def request(j):
                if j == 0:
                    box["t"] = take((lambda v: v[:, 0:rows * n].rearrange("p (c n) -> p c n", c=rows), w))
                i, v, tw = box["t"]
                v = v[:, 0:rows * n].rearrange("p (c n) -> p c n", c=rows)
                m = rows // halves if cut == "rows" else n // halves
                part = v[:, j * m:j * m + m, :] if cut == "rows" else v[:, :, j * m:j * m + m]
                return part, part.shape[1:], tw, i if j == halves - 1 else None
            return [lambda j=j: request(j) for j in range(halves)]

        def want_ffn(l, k):
            win, wout = W["ffn_w_in"][l, k], W["ffn_w_out"][l, k]

            def cols(o, w):
                return win[:, o:o + w].rearrange("(c p) n -> p c n", p=128)
            for s in range(5):
                g = want_slabs(cols(512 * s, 512), 0, 512, 8, "cols", 2)
                u = want_slabs(cols(2816 + 512 * s, 512), 0, 512, 8, "cols", 2)
                wanted.extend([g[0], u[0], g[1], u[1]])
            box = {}

            def tail(j):
                if j == 0:
                    box["t"] = take((lambda v: v[:, 0:2048].rearrange("p (c n) -> p c n", c=8), cols(2560, 256)),
                                    (lambda v: v[:, 2048:4096].rearrange("p (c n) -> p c n", c=8), cols(5376, 256)))
                i, v, tw = box["t"]
                return v[:, 2048 * j:2048 * j + 2048].rearrange("p (c n) -> p c n", c=8), (8, 256), tw, i if j else None
            wanted.extend([lambda: tail(0), lambda: tail(1)])
            for s in range(6):
                n = 4 if s < 5 else 2
                wanted.extend(want_slabs(wout[512 * s:512 * s + 128 * n, :].rearrange("(c p) n -> p c n", p=128), 0, 1024,
                                         n, "rows", n // 2))

        def want_mla():
            def chunks(w):
                return w.rearrange("(c p) n -> p c n", p=128)

            def over(n, c, w, parts):
                box = {}

                def request(j):
                    if j == 0:
                        box["t"] = take(*[(lambda v, o=o: v[:, o:o + n].rearrange("p (c n) -> p c n", c=c), x)
                                          for o, x in w])
                    i, v, tw = box["t"]
                    pick, shape = parts[j]
                    return pick(v), shape, tw, i if j == len(parts) - 1 else None
                wanted.extend([lambda j=j: request(j) for j in range(len(parts))])

            def by(v, n, c):
                return v[:, 0:n].rearrange("p (c n) -> p c n", c=c)
            over(2560, 8, [(0, chunks(W["w_dkv"]))],
                 [(lambda v: by(v, 2560, 8)[:, :, 0:256], (8, 256)),
                  (lambda v: by(v, 2560, 8)[:, :, 256:320].unsqueeze(2).to_broadcast([128, 8, 2, 64]), (8, 2, 64))])
            over(3072, 8, [(0, chunks(W["wq_down"][0]))],
                 [(lambda v, j=j: by(v, 3072, 8)[:, 4 * j:4 * j + 4, :], (4, 384)) for j in range(2)])
            over(2048, 2, [(0, chunks(W["w_uk"])), (2048, chunks(W["w_uv"]))],
                 [(lambda v, j=j: by(v[:, 2048 * j:2048 * j + 2048], 2048, 2), (2, 1024)) for j in range(2)])
            for q in range(2):
                def heads(v):
                    return by(v, 2304, 3).rearrange("p c (h n) -> p c h n", h=4)
                over(2304, 3, [(0, chunks(W["wq_up"][0][:, q * 768:q * 768 + 768]))],
                     [(lambda v: heads(v)[:, :, :, 0:128], (3, 4, 128)), (lambda v: heads(v)[:, :, :, 128:192], (3, 4, 64))])
            for s in range(2):
                wanted.extend(want_slabs(chunks(W["wo"][0][512 * s:512 * s + 512, :]), 0, 1024, 4, "rows", 2))

        def want_mix(l):
            win = W["mix_w_in"][l]
            for o, cut in ((0, "cols"), (512, "cols"), (1024, "rows"), (1536, "cols"), (2048, "rows"), (2560, "rows")):
                wanted.extend(want_slabs(win[:, o:o + 512].rearrange("(c p) n -> p c n", p=128), 0, 512, 8, cut, 2))
            for s in range(2):
                wanted.extend(want_slabs(W["mix_w_out"][l][512 * s:512 * s + 512, :].rearrange("(c p) n -> p c n", p=128),
                                         0, 1024, 4, "rows", 2))

        def mm3(out, lt, rt_, start, stop, *toks, sig=False):
            (lh, ll), (rh, rl) = lt, rt_
            mm(out, ll, rh, start, False, *toks)
            mm(out, lh, rl, False, False)
            return mm(out, lh, rh, False, stop, sig=sig)

        def dma_sem_load(name, dst, src, *toks):
            s = sem(name)
            act.wait(*toks)
            act.ops.append(lambda e: e.dma_start(dst, src).then_inc(s, 16))
            return (s, 16)

        def row(name, dst, *toks):
            return dma_sem_load("d_" + name, dst, row_of(name), *toks)

        def rows_for(name):
            if name[:3] == "ffn":
                l, k = int(name[3]), int(name[4])
                got[name] = row(f"ng{l}{5 if k else 1}", RB[:, k, :], read_row.get(k))
            elif name[:3] == "mix":
                l = int(name[3])
                got[name] = row(f"ng{l}3", RB[:, 2, :], read_row.get(2))
                got["lam" + name] = row(f"lam{l}", SM[:, 256:512], read_row.get("lam"))

        def row_of(name):
            o, w = ROWS[name]
            return W["rows"][0:1, o:o + w].to_broadcast([128, w])

        def mm(out, lhsT, rhs, start, stop, *toks, sig=False):
            return pe(lambda e: e.matmul(out, lhsT, rhs, start=start, stop=stop), *toks, sig=sig)

        def tr(out, in_, p, *toks, sig=False):
            ident = CS[0:p, 0:p]
            return pe(lambda e: e.transpose(out, in_, ident), *toks, sig=sig)

        def ts(out, in0, s1, s2, o0, o1, *toks):
            if s2 is None:
                return dve(lambda e: e.tensor_scalar(out, in0, s1, None, o0), *toks)
            return dve(lambda e: e.tensor_scalar(out, in0, s1, s2, o0, o1), *toks)

        def tt(out, a, b, op, *toks):
            return dve(lambda e: e.tensor_tensor(out, a, b, op), *toks)

        def stt(out, a, s, b, o0, o1, *toks):
            return dve(lambda e: e.scalar_tensor_tensor(out, a, s, b, o0, o1), *toks)

        def av(out, in_, func, *toks, **kw):
            return act(lambda e: e.activation(out, in_, func, **kw), *toks)

        def cp(out, in_, *toks):
            return dve(lambda e: e.tensor_copy(out, in_), *toks)

        def rsq(out, ss, n, *toks, times=1.0):
            q = times ** -2.0
            t = pool(lambda e: e.tensor_scalar(out, ss, q / n, q * EPS, ALU.mult, ALU.add), *toks)
            return pool(lambda e: e.tensor_tensor(out, out, MH[:, 0:out.shape[1]], ALU.pow), t)

        def first(name, dst, src):
            s = sem(name)
            sp.ops.append(lambda e: e.dma_start(dst, src).then_inc(s, 16))
            return (s, 16)
        xsrc = W["x"].rearrange("(b p) n -> p b n", p=128)
        xt = [first("d_x0", X[:, 0, :], xsrc[:, 0, :]), first("d_x1", X[:, 1, :], xsrc[:, 1, :])]
        t_ve = first("d_ve", VE[:, :], W["vec"])
        t_cs = first("d_cs", CS[:, :], W["cst"])
        t_rows = {}

        def load_rows():
            for n, d in (("pool_b", RB[:, 0, :]), ("pool_scale", RB[:, 1, :]), ("r0", RR[:, 0:36]),
                         ("r1", RR[:, 36:72]), ("final", RB[:, 2, :])):
                t_rows[n] = first("d_" + n, d, row_of(n))
        pe.wait(t_cs)
        if plan[0] != "pool":
            load_rows()
            act.wait(*t_rows.values())
        else:
            in_pool = (take((lambda v: v[:, 0:2048], W["pm"])),
                       take((lambda v: v[:, 0:2048].rearrange("p (a d) -> p a d", a=8),
                             W["pool_w"][0].rearrange("g (cc p) d -> p (g cc) d", p=128))))
            issue_loads(2)
            load_rows()
        pool(lambda e: e.memset(MH[:, :], -0.5))
        pool.wait(pool.last())

        def norm_xs(*toks, each=None):
            ss, rs = SM[:, 0:2], SM[:, 2:4]
            sq, got = [], []
            for b in range(2):
                t = av(JK[:, :], X[:, b, :], ACT.Square, xt[b], act.last(), accum_out=ss[:, b:b + 1])
                sq.append(rsq(rs[:, b:b + 1], ss[:, b:b + 1], 1024, t))
                if b == 0:
                    got.append([av(XS[:, 0, :], X[:, 0, :], ACT.Copy, sq[0], *toks, scale=rs[:, 0:1])])
                    if each:
                        each(0, got[0])
            a = av(XS[:, 1, 0:512], X[:, 1, 0:512], ACT.Copy, sq[1], *toks, scale=rs[:, 1:2])
            d = ts(XS[:, 1, 512:1024], X[:, 1, 512:1024], rs[:, 1:2], None, ALU.mult, None, sq[1], xt[1], *toks)
            got.append([a, d])
            if each:
                each(1, got[1])
            for e in (act, dve):
                e.wait(t_ve, t_cs)
            return got

        def transposed(gain, dst, src, toks, then):
            got = None

            def one(c, b):
                return tr(PS[:, c // 2, (c % 2) * 256 + b * 128:(c % 2) * 256 + b * 128 + 128],
                          src[:, b, c * 128:c * 128 + 128], 128, toks[b], sig=(c % 2 + b == 2))
            for c in range(8):
                one(c, 0)
            for j in range(4):
                one(2 * j, 1)
                t = one(2 * j + 1, 1)
                if j:
                    then(j - 1, got)
                if j % 2 == 0:
                    got = [tt(dst[:, 2 * j:2 * j + 2, :], PS[:, j, :].rearrange("p (c n) -> p c n", c=2),
                              gain[:, 2 * j:2 * j + 2].unsqueeze(2).to_broadcast([128, 2, 256]), ALU.mult, t)]
                else:
                    got = [av(dst[:, c, :], PS[:, j, (c % 2) * 256:(c % 2) * 256 + 256], ACT.Copy, t,
                              scale=gain[:, c:c + 1]) for c in (2 * j, 2 * j + 1)]
            return then(3, got)

        def transposed3(gain, src, toks, chunks=range(8), banks=(0, 1, 2, 3), hi_after=None, lo_after=None,
                        free=None):
            c0 = chunks[0]
            place_of = {c: (banks[(c - c0) // 2], ((c - c0) % 2) * 256) for c in chunks}
            for b in range(2):
                for c in chunks:
                    bk, o = place_of[c]
                    t = tr(PS[:, bk, o + b * 128:o + b * 128 + 128], src(b, c), 128, toks[b], free,
                           sig=(b == 1 and (c - c0) % 2 == 1))
                    if b and (c - c0) % 2:
                        for cc in (c - 1, c):
                            o = place_of[cc][1]
                            av(HTH[:, cc, :], PS[:, bk, o:o + 256], ACT.Copy, t, hi_after, scale=gain[:, cc:cc + 1])
            done = {}
            base = act.n - len(chunks)
            for c in chunks:
                bk, o = place_of[c]
                h = (act.sem, base + (c - c0) + 1)
                d = stt(HTL[:, c, :], PS[:, bk, o:o + 256], gain[:, c:c + 1], HTH[:, c, :].bitcast(F32), ALU.mult,
                        ALU.subtract, t, (act.sem, base + ((c - c0) | 1) + 1), lo_after)
                done[c] = [h, d]
            return done

        def ahead(mid=None):
            if not issued:
                issue(mid)
            elif mid:
                mid()

        def post_norm(banks, rowv, half, toks, tmp, after=None):
            ss, rs = SM[:, 4:6], SM[:, 6:8]
            read = []

            def block(b):
                ps = PS[:, banks[b]:banks[b] + 2, :]
                t = av(JK[:, :].rearrange("p (a n) -> p a n", a=2), ps, ACT.Square, toks[b], act.last(),
                       accum_out=ss[:, b:b + 1])
                t = rsq(rs[:, b:b + 1], ss[:, b:b + 1], 1024, t, times=half)
                read.append(stt(tmp[b].rearrange("p (a n) -> p a n", a=2), ps, rs[:, b:b + 1],
                                rowv.rearrange("p (a n) -> p a n", a=2), ALU.mult, ALU.mult, t, toks[b], after))
                xt[b] = tt(X[:, b, :], X[:, b, :], tmp[b], ALU.add, read[b])
            block(0)
            ahead(lambda: block(1))
            return read

        def stage_pool():
            (i, v, tw), (iw, vw, tww) = in_pool
            M = v[:, 0:2048].rearrange("p (b g t) -> p b g t", b=2, g=4)
            PW = vw[:, 0:2048].rearrange("p (a d) -> p a d", a=8)
            tx = norm_xs()
            pg = ve("pool_norm")
            for g in range(4):
                for cc in range(2):
                    c = 2 * g + cc
                    mm(PS[:, g, cc * 256:cc * 256 + 256], XS[:, 0, c * 128:c * 128 + 128], M[:, 0, g, :], True, False,
                       tx[0], tx[1], tw)
                    t = mm(PS[:, g, cc * 256 + 128:cc * 256 + 256], XS[:, 1, c * 128:c * 128 + 128], M[:, 1, g, 128:256],
                           False, True, sig=True)
                te = tt(HT[:, 2 * g:2 * g + 2, :], PS[:, g, :].rearrange("p (c n) -> p c n", c=2),
                        pg[:, 2 * g:2 * g + 2].unsqueeze(2).to_broadcast([128, 2, 256]), ALU.mult, t)
                if g == 2:
                    tb = tt(RB[:, 0, :], RB[:, 0, :], RB[:, 1, :], ALU.mult, t_rows["pool_b"], t_rows["pool_scale"])
                    tx0 = tt(X[:, 0, :], X[:, 0, :], RB[:, 0, :], ALU.add, tb, tx[0])
                if g:
                    pool_out(g - 1, PW, [tprev, tww])
                tprev = te
            give(i, t)
            give(iw, pool_out(3, PW, [tprev, tww]))
            tx = [tx0, tt(X[:, 1, :], X[:, 1, :], RB[:, 0, :], ALU.add, tb, tx[1])]
            t = pe.last()
            for b in range(2):
                j = XS[:, b, :]
                t1 = tt(j.rearrange("p (a n) -> p a n", a=2), PS[:, 4 + 2 * b:6 + 2 * b, :],
                        RB[:, 1, :].rearrange("p (a n) -> p a n", a=2), ALU.mult, t)
                xt[b] = tt(X[:, b, :], X[:, b, :], j, ALU.add, t1, tx[b])
            read_row[0] = read_row[1] = t1

        def pool_out(g, PW, te):
            for b in range(2):
                o = PS[:, 4 + 2 * b + g // 2, (g % 2) * 256:(g % 2) * 256 + 256]
                for cc in range(2):
                    t = mm(o, HT[:, 2 * g + cc, b * 128:b * 128 + 128], PW[:, 2 * g + cc, :], cc == 0, cc == 1, te,
                           sig=(cc == 1))
            return t

        def stage_moe(l):
            ring(NS)
            tx = norm_xs(*x_after)
            gain = ve(f"ffn{l}")
            rw = ve(f"rw{l}").rearrange("p (c n) -> p c n", c=8)

            def logits(j, toks):
                for c in (2 * j, 2 * j + 1):
                    t = mm(PS[0:36, 5, 0:256], rw[:, c, :], HT[:, c, :], c == 0, c == 7, toks, sig=(c == 7))
                return t
            t = transposed(gain, HT, XS, tx, logits)
            lt = SM[0:36, 256:512]
            t = cp(lt, PS[0:36, 5, 0:256], t)
            for b in range(2):
                t = tr(PS[:, 4, b * 36:b * 36 + 36], lt[:, b * 128:b * 128 + 128], 36, t, sig=True)
            w = [0]

            def al(n):
                w[0] += n
                return WK[:, w[0] - n:w[0]]
            S = al(2048).rearrange("p (b n) -> p b n", b=2)
            G = al(2048).rearrange("p (b n) -> p b n", b=2)
            XE = al(2048).rearrange("p (k c n) -> p k c n", k=2, c=8)
            GT = al(512).rearrange("p (k n) -> p k n", k=2)
            HG = al(512).rearrange("p (k n) -> p k n", k=4)
            HE = al(256).rearrange("p (k n) -> p k n", k=2)
            Y = al(1024)
            L = al(72).rearrange("p (b n) -> p b n", b=2)
            G8 = al(16).rearrange("p (b n) -> p b n", b=2)
            M8 = al(16).rearrange("p (b n) -> p b n", b=2)
            V8 = al(16).rearrange("p (b n) -> p b n", b=2)
            E8 = al(16).rearrange("p (b n) -> p b n", b=2)
            T4 = al(64).rearrange("p (b g e) -> p b g e", b=2, g=4)
            OH = al(8).rearrange("p (b n) -> p b n", b=2)
            IG = al(2)
            IE = al(4).rearrange("p (b n) -> p b n", b=2)
            NM, SG, GP, DD, EE, W1, W2 = (al(2) for _ in range(7))
            A1, A2, A, GM, PO = (al(64).rearrange("p (b n) -> p b n", b=2) for _ in range(5))
            assert w[0] <= 13440 - SLOT, w[0]
            io = cs("iota")
            dve.wait(t_rows["r0"], t_rows["r1"])
            t = tt(L, PS[:, 4, 0:72].rearrange("p (b n) -> p b n", b=2),
                   RR[:, 36 * l:36 * l + 36].unsqueeze(1).to_broadcast([128, 2, 36]), ALU.add, t)
            t8 = dve(lambda e: e.memset(G8, -3e38))
            t = cp(G8[:, :, 0:4], L[:, :, 0:4], t, t8)
            for b in range(2):
                ta = dve(lambda e, b=b: e.max(M8[:, b, :], G8[:, b, :]), t)
                ta = dve(lambda e, b=b: e.max_index(IX[:, b * 8:b * 8 + 8], M8[:, b, :], G8[:, b, :]), ta)
            tg = cp(IG, IX[:, 0:16].rearrange("p (b n) -> p b n", b=2)[:, :, 0], ta)
            tn = ts(NM, M8[:, :, 0], -1.0, None, ALU.mult, None, ta)
            for b in range(2):
                te = av(SM[:, 16 + 4 * b:20 + 4 * b], L[:, b, 0:4], ACT.Exp, tn, bias=NM[:, b:b + 1],
                        accum_out=SG[:, b:b + 1])
            tp = dve(lambda e: e.reciprocal(GP, SG), te)
            t = tt(OH, io[:, 0:4].unsqueeze(1).to_broadcast([128, 2, 4]), IG.unsqueeze(2).to_broadcast([128, 2, 4]),
                   ALU.is_equal, tg)
            t = tt(T4, L[:, :, 4:36].rearrange("p b (g e) -> p b g e", g=4),
                   OH.unsqueeze(3).to_broadcast([128, 2, 4, 8]), ALU.mult, t)
            for b in range(2):
                t = dve(lambda e, b=b: e.tensor_reduce(E8[:, b, :], T4[:, b, :, :].rearrange("p g e -> p e g"), AX.X,
                                                       ALU.add), t)
            for b in range(2):
                ta = dve(lambda e, b=b: e.max(V8[:, b, :], E8[:, b, :]), t)
                ta = dve(lambda e, b=b: e.max_index(IX[:, 16 + b * 8:24 + b * 8], V8[:, b, :], E8[:, b, :]), ta)
            t = cp(IE, IX[:, 16:32].rearrange("p (b n) -> p b n", b=2)[:, :, 0:2], ta)
            t = stt(IE, IG.unsqueeze(2).to_broadcast([128, 2, 2]), 8.0, IE, ALU.mult, ALU.add, t)
            td = tt(DD, V8[:, :, 1], V8[:, :, 0], ALU.subtract, ta)
            td = av(EE, DD, ACT.Exp, td)
            t1 = ts(W1, EE, 1.0, None, ALU.add, None, td)
            t1 = dve(lambda e: e.reciprocal(W1, W1), t1)
            t1 = tt(W1, W1, GP, ALU.mult, t1, tp)
            t1 = tt(W2, W1, EE, ALU.mult, t1)
            i32 = io.unsqueeze(1).to_broadcast([128, 2, 32])
            ta = tt(A1, i32, IE[:, :, 0:1].to_broadcast([128, 2, 32]), ALU.is_equal, t)
            tb = tt(A2, i32, IE[:, :, 1:2].to_broadcast([128, 2, 32]), ALU.is_equal, t)
            tA = tt(A, A1, A2, ALU.add, tb)
            ta = tt(A1, A1, W1.unsqueeze(2).to_broadcast([128, 2, 32]), ALU.mult, tA, t1)
            tb = tt(A2, A2, W2.unsqueeze(2).to_broadcast([128, 2, 32]), ALU.mult, tA, t1)
            tG = tt(GM, A1, A2, ALU.add, ta, tb)
            mm(PS[:, 5, 0:32], cs("tri"), A[:, 0, :], True, True, tA)
            mm(PS[:, 5, 32:64], cs("ones"), A[:, 0, :], True, False)
            tq = mm(PS[:, 5, 32:64], cs("tri"), A[:, 1, :], False, True, sig=True)
            mm(PS[:, 6, 0:32], cs("ones"), A[:, 0, :], True, False)
            tall = mm(PS[:, 6, 0:32], cs("ones"), A[:, 1, :], False, True, sig=True)
            t = ts(PO, A, -BIG, BIG, ALU.mult, ALU.add, tA)
            t = tt(PO, PO, PS[:, 5, 0:64].rearrange("p (b n) -> p b n", b=2), ALU.add, t, tq)
            GO = SM[:, 128:192].rearrange("p (b n) -> p b n", b=2)
            flag = FLAG[0:1, l:l + 1]
            tall_free = []

            def left_over():
                t1 = ts(GO, PO, float(CAP), None, ALU.is_ge, None, t)
                t2 = tt(GO, GO, GM, ALU.mult, t1, tG)
                t1 = dve(lambda e: e.tensor_reduce(SM[:, 192:193], PS[:, 6, 0:32], AX.X, ALU.max), tall)
                tall_free.append(t1)
                t1 = ts(SM[:, 192:193], SM[:, 192:193], float(CAP), None, ALU.is_gt, None, t1)
                return [cp(FLAG[:, l:l + 1], SM[:, 192:193], t1), t2]
            if CAP < C:
                t1 = ts(A1, PO, float(CAP), BIG, ALU.is_ge, ALU.mult, t, tG)
                t = tt(PO, PO, A1, ALU.add, t1)
            tS, tGG = {}, {}
            for e0, n in ((0, 4), (4, 28)):
                if e0:
                    tflag = left_over()
                for b in range(2):
                    ts_ = tt(S[:, b, e0 * C:(e0 + n) * C].rearrange("p (e s) -> p e s", e=n),
                             io[:, 0:C].unsqueeze(1).to_broadcast([128, n, C]),
                             PO[:, b, e0:e0 + n].unsqueeze(2).to_broadcast([128, n, C]), ALU.is_equal, t)
                for g in range(e0 // 4, (e0 + n) // 4):
                    tS[g] = ts_

            build_gates = [(0, 4), (4, 28)]

            def gates():
                e0, n = build_gates.pop(0)
                for b in range(2):
                    tg_ = tt(G[:, b, e0 * C:(e0 + n) * C].rearrange("p (e s) -> p e s", e=n),
                             S[:, b, e0 * C:(e0 + n) * C].rearrange("p (e s) -> p e s", e=n),
                             GM[:, b, e0:e0 + n].unsqueeze(2).to_broadcast([128, n, C]), ALU.mult, tS[e0 // 4], tG)
                for g in range(e0 // 4, (e0 + n) // 4):
                    tGG[g] = tg_
            gates()
            av(SM[0:1, 200:201], MH[0:1, 0:1], ACT.Silu, act.last())
            wd = W["w_down"][l]
            sl = {}

            def load_gu(e):
                for k in ("w_gate", "w_up"):
                    sl[k, e] = take((lambda v: v.rearrange("p (c n) -> p c n", c=8),
                                     W[k][l, e].rearrange("(c p) n -> p c n", p=128)))

            def load_d(e):
                m = 4 if e < 31 else 2
                sl["d", e] = [take((lambda v: v[:, 0:1024 * m].rearrange("p (c n) -> p c n", c=m),
                                    wd[e][128 * c:128 * c + 128 * m, :].rearrange("(c p) n -> p c n", p=128)))
                              for c in range(0, 4, m)]
            bank = {k: None for k in range(8)}
            bank[6] = tall_free[0]
            hg, he, ga, gt = {}, {}, {}, {}

            def gather(g):
                for r in range(2):
                    bk = 2 + r
                    for c in range(4):
                        for b in range(2):
                            t = mm(PS[:, bk, c * 128:c * 128 + 128],
                                   XS[:, b, (4 * r + c) * 128:(4 * r + c) * 128 + 128], S[:, b, g * 128:g * 128 + 128],
                                   b == 0, b == 1, bank[bk], tS[g], sig=(c == 3 and b == 1))
                    bank[bk] = ga[g, r] = tt(XE[:, g % 2, 4 * r:4 * r + 4, :], PS[:, bk, :].rearrange("p (c n) -> p c n", c=4),
                                          gain[:, 4 * r:4 * r + 4].unsqueeze(2).to_broadcast([128, 4, 128]), ALU.mult,
                                          t, last_gu.get(4 * (g - 2) + 3))

            def gate_rows(g):
                for b in range(2):
                    t = tr(PS[:, 3, b * 128:b * 128 + 128], G[:, b, g * 128:g * 128 + 128], 128, bank[3], tGG[g],
                           sig=(b == 1))
                bank[3] = gt[g] = av(GT[:, g % 2, :], PS[:, 3, 0:256], ACT.Copy, t, comb.get(g - 2))
            last_gu, comb = {}, {}

            def gateup(e):
                g, j = divmod(e, 4)
                pb = e % 2
                for n, k in enumerate(("w_gate", "w_up")):
                    i, v, tw = sl[k, e]
                    v = v.rearrange("p (c n) -> p c n", c=8)
                    for c in range(8):
                        for q in range(4):
                            t = mm(PS[32 * q:32 * q + 32, pb, n * 128:n * 128 + 128],
                                   XE[:, g % 2, c, 32 * j:32 * j + 32], v[:, c, 128 * q:128 * q + 128], c == 0, c == 7,
                                   tw, ga[g, c // 4], bank[pb],
                                   sig=(c == 7 and q == 3))
                    give(i, t)
                ta = av(HG[:, pb, :], PS[:, pb, 0:128], ACT.Silu, t, hg.get(e - 2))
                last_gu[e] = t
                hg[e] = bank[pb] = tt(HG[:, 2 + pb, :], HG[:, pb, :], PS[:, pb, 128:256], ALU.mult, t, ta, he.get(e - 2))

            def down(e):
                g, j = divmod(e, 4)
                pb = e % 2
                t = tr(PS[:, 3, 0:128], HG[:, 2 + pb, :], 128, hg[e], bank[3], sig=True)
                he[e] = bank[3] = cp(HE[:, pb, :], PS[:, 3, 0:128], t, dn.get(e - 2))
                m = 4 // len(sl["d", e])
                for z, (i, v, tw) in enumerate(sl["d", e]):
                    v = v[:, 0:1024 * m].rearrange("p (c n) -> p c n", c=m)
                    for h in range(2):
                        for c in range(m):
                            f = m * z + c
                            t = mm(PS[32 * j:32 * j + 32, 4 + h, :], HE[:, pb, 32 * f:32 * f + 32],
                                   v[:, c, 512 * h:512 * h + 512], f == 0, f == 3, tw, he[e],
                                   bank[4 + h] if j == 0 else None, sig=(c == m - 1))
                    give(i, t)
                dn[e] = t
                if j == 3:
                    a = av(Y[:, 0:512], PS[:, 4, :], ACT.Copy, t, comb.get(g - 1))
                    d = cp(Y[:, 512:1024], PS[:, 5, :], t, comb.get(g - 1))
                    bank[4], bank[5] = a, d
                    ydone[g] = [a, d]
            dn, ydone = {}, {}

            def combine(g):
                for b in range(2):
                    for h in range(2):
                        t = mm(PS[:, 6 + h, :], GT[:, g % 2, b * 128:b * 128 + 128], Y[:, h * 512:h * 512 + 512], True,
                               True, ydone[g], gt[g], bank[6 + h], sig=True)
                        bank[6 + h] = xt[b] = tt(X[:, b, h * 512:h * 512 + 512], X[:, b, h * 512:h * 512 + 512],
                                                 PS[:, 6 + h, :], ALU.add, t)
                comb[g] = t

            for e in range(33):
                if e < 32:
                    if e % 4 == 0:
                        gather(e // 4)
                    if e == 1:
                        gates()
                    load_gu(e)
                    gateup(e)
                    if e % 4 == 0:
                        gate_rows(e // 4)
                    if e == 8 and l == 1:
                        rows_for("ffn00")
                if e >= 1:
                    load_d(e - 1)
                    down(e - 1)
                    if (e - 1) % 4 == 0 and e > 1:
                        combine((e - 1) // 4 - 1)
            combine(7)
            ps_after[:], x_after[:] = [], []
            overflow(l, GO, flag, tflag)

        def overflow(l, GO, flag, tflag):
            names = ("pe", "act", "dve", "sp")
            o = {n: Eng(sem(f"o_{n}{l}")) for n in names}
            lds = [sem(f"o_ld{l}{k}") for k in range(2)]
            outer = {"pe": pe, "act": act, "dve": dve}
            begun = [x.last() for x in outer.values()]
            for x in o.values():
                x.wait(*begun)
            BUF = [WK[:, 6144 * k:6144 * k + 6144] for k in range(2)]
            HFO = WK[:, 12288:12800].rearrange("p (f n) -> p f n", f=2)
            GS = JK[:, 0:512].rearrange("p (f n) -> p f n", f=2)
            used, tsilu, thf, tadd, tdown = {}, {}, {}, {}, {}
            for n in range(64):
                e, hf = divmod(n, 2)
                k = n % 2
                wg, wu, wd = (BUF[k][:, 2048 * z:2048 * z + 2048] for z in range(3))
                o["sp"].wait(used.get(n - 2))
                for dst, src in ((wg, W["w_gate"][l, e][:, 256 * hf:256 * hf + 256]),
                                 (wu, W["w_up"][l, e][:, 256 * hf:256 * hf + 256]),
                                 (wd, W["w_down"][l, e][256 * hf:256 * hf + 256, :])):
                    m = 2 if dst is wd else 8
                    o["sp"].ops.append(lambda g, dst=dst, src=src, k=k, m=m: g.dma_start(
                        dst.rearrange("p (c n) -> p c n", c=m), src.rearrange("(c p) n -> p c n", p=128)
                    ).then_inc(lds[k], 16))
                tl = (lds[k], 48 * (n // 2 + 1))
                gv, uv = (z.rearrange("p (c n) -> p c n", c=8) for z in (wg, wu))
                dv = wd.rearrange("p (c n) -> p c n", c=2)
                for f in range(2):
                    for z, v in enumerate((gv, uv)):
                        for c in range(8):
                            t = o["pe"](lambda g, f=f, z=z, v=v, c=c: g.matmul(
                                PS[:, f, z * 256:z * 256 + 256], v[:, c, f * 128:f * 128 + 128], HT[:, c, :],
                                start=c == 0, stop=c == 7), tl, thf.get((n - 1, f)), sig=(c == 7))
                    ta = o["act"](lambda g, f=f: g.activation(GS[:, f, :], PS[:, f, 0:256], ACT.Silu), t,
                                  thf.get((n - 1, f)))
                    thf[n, f] = o["dve"](lambda g, f=f: g.tensor_tensor(HFO[:, f, :], GS[:, f, :], PS[:, f, 256:512],
                                                                        ALU.mult), t, ta, tdown.get(n - 1))
                for f in range(2):
                    for b in range(2):
                        for h in range(2):
                            tdown[n] = used[n] = o["pe"](lambda g, f=f, b=b, h=h, dv=dv, hf=hf: g.matmul(
                                PS[:, 4 + 2 * b + h, :], HFO[:, f, b * 128:b * 128 + 128], dv[:, f, h * 512:h * 512 + 512],
                                start=(f == 0 and hf == 0), stop=(f == 1 and hf == 1)), thf[n, 1],
                                tadd.get(e - 1), sig=(b + h == 2))
                if hf == 1:
                    for b in range(2):
                        xv = X[:, b, :].rearrange("p (a n) -> p a n", a=2)
                        tadd[e] = o["dve"](lambda g, b=b, xv=xv, e=e: g.scalar_tensor_tensor(
                            xv, PS[:, 4 + 2 * b:6 + 2 * b, :], GO[:, b, e:e + 1], xv, ALU.mult, ALU.add), tdown[n],
                            tadd.get(e - 1))
            done = [o[n].last() for n in ("pe", "act", "dve")]
            for x in o.values():
                x.wait(*done)

            def enter(g, inner):
                v = g.value_load(flag, min_val=0, max_val=1)
                with g.If(v > 0):
                    inner.play(g)
            for n, x in outer.items():
                x.wait(tflag)
                x.ops.append(lambda g, n=n: enter(g, o[n]))
            breaks[len(loads)] = (tflag, lambda g: enter(g, o["sp"]))

        def stage_fin():
            ring(4)

            def norm():
                def gain(b, t):
                    xt[b] = tt(X[:, b, :], XS[:, b, :], RB[:, 2, :], ALU.mult, t, t_rows["final"])
                norm_xs(each=gain)
                read_row[2] = xt[1]
            ahead(norm)

        def stage_ffn(l, k):
            ring(4)
            tx = norm_xs(*x_after)
            ahead()
            th = transposed3(ve(f"ng{l}{0 if k == 0 else 4}"), lambda b, c: XS[:, b, c * 128:c * 128 + 128], tx,
                             free=ps_after)
            GS = WK[:, 11264:11776].rearrange("p (k n) -> p k n", k=2)
            VV = WK[:, 11776:12288].rearrange("p (k n) -> p k n", k=2)
            bank = {bk: ps_after for bk in range(8)}
            gs, hl, late = {}, {}, []

            def close():
                f, bk, t = late.pop()
                ta = av(GS[:, f % 2, :], PS[:, bk, 0:256], ACT.Silu, t, gs.get(f - 2))
                gs[f] = bank[bk] = tv = tt(VV[:, f % 2, :], GS[:, f % 2, :], PS[:, bk, 256:512], ALU.mult, t, ta)
                ta = av(HFH[:, f, :], VV[:, f % 2, :], ACT.Copy, tv)
                hl[f] = [ta, tt(HFL[:, f, :], VV[:, f % 2, :], HFH[:, f, :].bitcast(F32), ALU.subtract, ta)]
            for fp in range(11):
                for n in range(2):
                    hi, lo, tsp, key = next_split()
                    if late:
                        close()
                    for fq in range(2):
                        f = 2 * fp + fq
                        bk = 4 + f % 4
                        for c in range(8):
                            t = mm3(PS[:, bk, n * 256:n * 256 + 256],
                                    (hi[:, c, fq * 128:fq * 128 + 128], lo[:, c, fq * 128:fq * 128 + 128]),
                                    (HTH[:, c, :], HTL[:, c, :]), c == 0, c == 7, tsp, th[c], bank[bk], sig=(c == 7))
                        if n:
                            late.append((f, bk, t))
                            if fq == 0:
                                close()
                    sp_free[key] = t
                if fp == 2:
                    rows_for(follows(f"ffn{l}{k}"))
            close()
            t = down_proj(11, 0, (HFH, HFL), hl, th[7], lambda f: f)
            dve.wait(got[f"ffn{l}{k}"])
            ps_after[:] = post_norm((0, 2), RB[:, k, :], 0.5, t, (XS[:, 0, :], XS[:, 1, :]))
            read_row[k] = ps_after[1]
            x_after[:] = []

        def down_proj(pairs, bank0, acts, ready, also, chunk):
            ah, al_ = acts
            ends = []
            for fp in range(pairs):
                last = fp == pairs - 1
                hi, lo, tsp, key = issued.pop(0) if last else next_split()
                for part in ((0,), (1,)) if last else ((0, 1),):
                    for c in range(2):
                        f = chunk(2 * fp + c)
                        for b in part:
                            for h in range(2):
                                t = mm3(PS[:, bank0 + 2 * b + h, :],
                                        (ah[:, f, b * 128:b * 128 + 128], al_[:, f, b * 128:b * 128 + 128]),
                                        (hi[:, c, h * 512:h * 512 + 512], lo[:, c, h * 512:h * 512 + 512]),
                                        f == 0, last and c == 1, tsp, ready[f], also, sig=(h == 1))
                    ends.append(t)
                sp_free[key] = t
            return ends[-2:]

        def banks_pool(ids):
            return {"ids": list(ids), "at": 0, "tok": {i: None for i in ids}}

        def nb(bp):
            i = bp["ids"][bp["at"] % len(bp["ids"])]
            bp["at"] += 1
            return i

        def stage_mla():
            ring(4)
            w = [0]

            def al(n, of=None):
                w[0] += n
                assert w[0] <= 13440, w[0]
                return (WK if of is None else of)[:, w[0] - n:w[0]]
            HKH = al(2048, WR).rearrange("p (h n) -> p h n", h=8)
            QN = WK[:, 0:2048].rearrange("p (h n) -> p h n", h=8)
            HKL = al(2048, WR).rearrange("p (h n) -> p h n", h=8)
            KN = WK[:, 2048:4096].rearrange("p (h n) -> p h n", h=8)
            V = al(2048).rearrange("p (b n) -> p b n", b=2)
            QR = al(1024).rearrange("p (h n) -> p h n", h=4)
            CKH, CKL = (al(512, WR).rearrange("p (c n) -> p c n", c=2) for _ in range(2))
            CQH, CQL = (al(768, WR).rearrange("p (c n) -> p c n", c=3) for _ in range(2))
            KR = al(256)
            PT = al(768).rearrange("p (k n) -> p k n", k=2)
            TQ = al(512).rearrange("p (k n) -> p k n", k=2)
            R2 = al(256)
            P0 = al(1280)
            P = P0[:, 0:1152].rearrange("p (k n) -> p k n", k=3)
            CKX = P0[:, 0:512].rearrange("p (b n) -> p b n", b=2)
            CQX = P0[:, 512:1280].rearrange("p (b n) -> p b n", b=2)
            cos, sin = cs("cos"), cs("sin")
            tx = []
            ahead(lambda: tx.extend(norm_xs()))
            tb_, tk_, ta_ = {}, [], []
            for b in range(2):
                for c in range(8):
                    t = tr(PS[:, c // 2, (c % 2) * 256 + b * 128:(c % 2) * 256 + b * 128 + 128],
                           XS[:, b, c * 128:c * 128 + 128], 128, tx[b], sig=(b == 1 and c % 2 == 1))
                    tb_[c // 2] = t
            both = ((ve("kv_in"), HKH, HKL, tk_), (ve("attn"), HTH, HTL, ta_))
            for j in range(4):
                pair = [(c, PS[:, j, (c % 2) * 256:(c % 2) * 256 + 256]) for c in (2 * j, 2 * j + 1)]
                for gain, H, Lo, _ in both:
                    for c, o in pair:
                        h = av(H[:, c, :], o, ACT.Copy, tb_[j], scale=gain[:, c:c + 1])
                for gain, H, Lo, got in both:
                    for c, o in pair:
                        got.append([h, stt(Lo[:, c, :], o, gain[:, c:c + 1], H[:, c, :].bitcast(F32), ALU.mult,
                                           ALU.subtract, h, tb_[3] if Lo is HTL else None)])
            bt = {k: ta_[7] for k in range(4)}

            hi, lo, tsp, key = next_split()
            for b in range(2):
                for c in range(8):
                    tk = mm3(PS[:, 4, b * 256:b * 256 + 256],
                             (HKH[:, c, b * 128:b * 128 + 128], HKL[:, c, b * 128:b * 128 + 128]),
                             (hi[:, c, :], lo[:, c, :]), c == 0, c == 7, tsp, tk_[c], sig=(c == 7))
            sp_free[key] = tk
            hi, lo, tsp, key = next_split()
            for c in range(8):
                tr_ = mm3(PS[:, 5, 0:256], (hi[:, c, :], lo[:, c, :]), (HKH[:, c, :], HKL[:, c, :]), c == 0, c == 7, tsp,
                          sig=(c == 7))
            sp_free[key] = tr_
            ss, rs = SM[:, 8:12], SM[:, 12:16]

            def latent(X2, ps, n, z, tok):
                for b in range(2):
                    t = av(JK[:, 0:n], ps(b), ACT.Square, tok, act.last(), accum_out=ss[:, z + b:z + b + 1])
                t = rsq(rs[:, z:z + 2], ss[:, z:z + 2], n, t)
                return [ts(X2[:, b, :], ps(b), rs[:, z + b:z + b + 1], None, ALU.mult, None, t) for b in range(2)]

            def parts_of(H, Lo, gain, tok, ps):
                h = [av(H[:, c, :], o, ACT.Copy, tok, scale=gain[:, c:c + 1]) for c, o in enumerate(ps)][-1]
                return [stt(Lo[:, c, :], o, gain[:, c:c + 1], H[:, c, :].bitcast(F32), ALU.mult, ALU.subtract, h)
                        for c, o in enumerate(ps)]
            tckx = latent(CKX, lambda b: PS[:, 4, b * 256:b * 256 + 256], 256, 0, tk)
            tq0 = av(TQ[:, 0, :], PS[:, 5, 0:256], ACT.Copy, tr_)

            def finish_keys():
                t = mm(PS[:, 5, 256:512], cs("swap"), TQ[:, 0, :], True, True, tq0, sig=True)
                t3 = tt(KR, TQ[:, 0, :], cos, ALU.mult, tq0)
                t4 = tt(R2, PS[:, 5, 256:512], sin, ALU.mult, t)
                tkr = tt(KR, KR, R2, ALU.add, t3, t4)
                for c in range(2):
                    for b in range(2):
                        t = tr(PS[:, 0, c * 256 + b * 128:c * 256 + b * 128 + 128], CKX[:, b, c * 128:c * 128 + 128],
                               128, tckx, bt[0], sig=(b + c == 2))
                tck = parts_of(CKH, CKL, ve("kv_norm"), t, [PS[:, 0, 256 * c:256 * c + 256] for c in range(2)])
                bt[0] = tck
                return tck, tkr
            for j in range(2):
                hi, lo, tsp, key = next_split()
                for cc in range(4):
                    c = 4 * j + cc
                    if c == 6:
                        tck, tkr = finish_keys()
                    for b in range(2):
                        tq = mm3(PS[:, 6 + b, 0:384],
                                 (HTH[:, c, b * 128:b * 128 + 128], HTL[:, c, b * 128:b * 128 + 128]),
                                 (hi[:, cc, :], lo[:, cc, :]), c == 0, c == 7, tsp, ta_[c], sig=(cc == 3))
                sp_free[key] = tq
            hi, lo, tsp, key = next_split()
            tcqx = latent(CQX, lambda b: PS[:, 6 + b, 0:384], 384, 2, tq)
            bp = banks_pool(range(4, 8))
            bp["tok"] = {4: tckx, 5: tkr, 6: tcqx, 7: tcqx}
            for h in range(8):
                if h % 2 == 0:
                    bk = nb(bp)
                for c in range(2):
                    t = mm3(PS[:, bk, (h % 2) * 256:(h % 2) * 256 + 256],
                            (hi[:, c, h * 128:h * 128 + 128], lo[:, c, h * 128:h * 128 + 128]),
                            (CKH[:, c, :], CKL[:, c, :]), c == 0, c == 1, tsp, tck, bp["tok"][bk], sig=(c == 1))
                if h % 2 == 1:
                    bp["tok"][bk] = tkn = cp(KN[:, h - 1:h + 1, :], PS[:, bk, :].rearrange("p (h n) -> p h n", h=2), t)
            sp_free[key] = t
            for c in range(3):
                for b in range(2):
                    t = tr(PS[:, 1 + c // 2, (c % 2) * 256 + b * 128:(c % 2) * 256 + b * 128 + 128],
                           CQX[:, b, c * 128:c * 128 + 128], 128, tcqx, bt[1], sig=(b == 1))
            tcq = parts_of(CQH, CQL, ve("q_norm"), t,
                           [PS[:, 1 + c // 2, (c % 2) * 256:(c % 2) * 256 + 256] for c in range(3)])
            bt[1] = bt[2] = tcq
            hi, lo, tsp, key = next_split()
            for b in range(2):
                for hf in range(2):
                    bk = nb(bp)
                    for c in range(2):
                        t = mm3(PS[:, bk, :], (CKH[:, c, b * 128:b * 128 + 128], CKL[:, c, b * 128:b * 128 + 128]),
                                (hi[:, c, hf * 512:hf * 512 + 512], lo[:, c, hf * 512:hf * 512 + 512]), c == 0, c == 1,
                                tsp, bp["tok"][bk], sig=(c == 1))
                    bp["tok"][bk] = tv = av(V[:, b, hf * 512:hf * 512 + 512], PS[:, bk, :], ACT.Copy, t)
            sp_free[key] = t
            pend, rot = [], {0: tkr, 1: tkr, 2: None}
            tqn, tqr = {}, {}

            def q_nope(q):
                hi, lo, tsp, key = next_split()
                for hh in range(4):
                    h = 4 * q + hh
                    if h % 2 == 0:
                        bk = nb(bp)
                    for c in range(3):
                        t = mm3(PS[:, bk, (h % 2) * 256:(h % 2) * 256 + 256],
                                (hi[:, c, hh * 128:hh * 128 + 128], lo[:, c, hh * 128:hh * 128 + 128]),
                                (CQH[:, c, :], CQL[:, c, :]), c == 0, c == 2, tsp, tcq, bp["tok"][bk], sig=(c == 2))
                    if h % 2 == 1:
                        bp["tok"][bk] = tqn[h] = tqn[h - 1] = av(
                            QN[:, h - 1:h + 1, :], PS[:, bk, :].rearrange("p (h n) -> p h n", h=2), ACT.Copy, t)
                sp_free[key] = t

            def rotate():
                if pend:
                    bk, pr, k, tq = pend.pop()
                    t = mm(PS[:, bk, 256:512], cs("swap"), TQ[:, k, :], True, True, tq, sig=True)
                    t3 = tt(QR[:, pr, :], TQ[:, k, :], cos, ALU.mult, tq)
                    t4 = bp["tok"][bk] = tt(R2, PS[:, bk, 256:512], sin, ALU.mult, t, rot[0])
                    rot[0] = rot[k + 1] = tqr[pr] = tt(QR[:, pr, :], QR[:, pr, :], R2, ALU.add, t3, t4)

            def q_rope(q, mid=None):
                hi, lo, tsp, key = next_split(mid)
                for k in range(2):
                    bk = nb(bp)
                    for c in range(3):
                        t = mm3(PS[:, bk, 0:256], (hi[:, c, k * 128:k * 128 + 128], lo[:, c, k * 128:k * 128 + 128]),
                                (CQH[:, c, :], CQL[:, c, :]), c == 0, c == 2, tsp, bp["tok"][bk], sig=(c == 2))
                    tq = av(TQ[:, k, :], PS[:, bk, 0:256], ACT.Copy, t, rot[k + 1])
                    rotate()
                    pend.append((bk, 2 * q + k, k, tq))
                sp_free[key] = t
            scale = 1.0 / math.sqrt(192.0)
            mask = cs("mask")
            pt, pv, prob, ready = {}, {}, {}, {}

            def scores(h):
                bk = h % 2
                pr, dp = h // 2, 64 * (h % 2)
                for i in range(2):
                    o = PS[:, bk, 0:128] if i == 0 else PS[:, bk, 128:384]
                    n = 128 + 128 * i
                    mm(o, QN[:, h, i * 128:i * 128 + 128], KN[:, h, 0:n], True, False, bt[bk], tqn[h], tkn)
                    t = mm(o, QR[dp:dp + 64, pr, i * 128:i * 128 + 128], KR[dp:dp + 64, 0:n], False, True, tqr[pr],
                           tkr, sig=True)
                p = P[:, h % 3, :]
                bt[bk] = t = stt(p, PS[:, bk, 0:384], scale, mask, ALU.mult, ALU.add, t, prob.get(h - 3))
                m, s = SM[:, 32 + 2 * (h % 3):34 + 2 * (h % 3)], SM[:, 40 + 2 * (h % 3):42 + 2 * (h % 3)]
                for i, (a, z) in enumerate(((0, 128), (128, 384))):
                    tm = dve(lambda e, i=i, a=a, z=z: e.tensor_reduce(m[:, i:i + 1], p[:, a:z], AX.X, ALU.max,
                                                                      negate=True), t)
                for i, (a, z) in enumerate(((0, 128), (128, 384))):
                    te = av(p[:, a:z], p[:, a:z], ACT.Exp, tm, bias=m[:, i:i + 1], accum_out=s[:, i:i + 1])
                pt[h] = te

            def weigh(h):
                p, s = P[:, h % 3, :], SM[:, 40 + 2 * (h % 3):42 + 2 * (h % 3)]
                t = dve(lambda e: e.reciprocal(s, s), pt[h])
                for i, (a, z) in enumerate(((0, 128), (128, 384))):
                    pt[h] = ts(p[:, a:z], p[:, a:z], s[:, i:i + 1], None, ALU.mult, None, t)

            def turn(h):
                for j in range(3):
                    t = tr(PS[:, 2, j * 128:j * 128 + 128], P[:, h % 3, j * 128:j * 128 + 128], 128, pt[h], bt[2],
                           sig=(j == 2))
                prob[h] = t
                bt[2] = pt[h] = av(PT[:, h % 2, :], PS[:, 2, 0:384], ACT.Copy, t, pv.get(h - 2))

            def values(h):
                q = PT[:, h % 2, :]
                v0, v1 = V[:, 0, h * 128:h * 128 + 128], V[:, 1, h * 128:h * 128 + 128]
                mm(PS[:, 3, 0:128], v0, q[:, 0:128], True, True, pt[h], bt[3], tv)
                mm(PS[:, 3, 128:256], v0, q[:, 128:256], True, False)
                pv[h] = mm(PS[:, 3, 128:256], v1, q[:, 256:384], False, True, sig=True)
                t = av(HTH[:, h, :], PS[:, 3, 0:256], ACT.Copy, pv[h])
                bt[3] = ready[h] = tt(HTL[:, h, :], PS[:, 3, 0:256], HTH[:, h, :].bitcast(F32), ALU.subtract, t)

            def out_unit(units, blocks=(0, 1), half=None):
                for s, (hi, lo, tsp, key) in units:
                    for c in range(2):
                        if c and half:
                            half()
                        f = 2 * s + c
                        for b in blocks:
                            for h in range(2):
                                t = mm3(PS[:, 4 + 2 * b + h, :],
                                        (HTH[:, f, b * 128:b * 128 + 128], HTL[:, f, b * 128:b * 128 + 128]),
                                        (hi[:, c, h * 512:h * 512 + 512], lo[:, c, h * 512:h * 512 + 512]),
                                        f == 0, f == 7, tsp, ready[f], bp["tok"][4 + 2 * b + h], sig=(h == 1))
                    sp_free[key] = t
                return t
            q_nope(0)
            q_rope(0)
            q_nope(1)
            rotate()
            q_rope(1, lambda: scores(0))
            weigh(0)
            scores(1)
            rotate()
            weigh(1)
            for h in range(8):
                turn(h)
                if h == 7:
                    break
                if h < 6:
                    scores(h + 2)
                if h < 6:
                    weigh(h + 2)
                values(h)
                if h == 3:
                    out_unit([(0, next_split())])
                if h == 5:
                    out_unit([(1, next_split())])
            out_unit([(2, next_split())], half=lambda: values(7))
            last = [(3, issued.pop(0))]
            for b in range(2):
                t = out_unit(last, (b,))
                x = X[:, b, :].rearrange("p (a n) -> p a n", a=2)
                xt[b] = tt(x, x, PS[:, 4 + 2 * b:6 + 2 * b, :], ALU.add, t)
            x_after[:] = [t]

        def stage_mix(l):
            ring(4)
            w = [0]

            def al(n):
                w[0] += n
                assert w[0] <= 13440, w[0]
                return WK[:, w[0] - n:w[0]]
            DQ = al(1024).rearrange("p (h n) -> p h n", h=4)
            DK = al(1024).rearrange("p (h n) -> p h n", h=4)
            DV = al(1024).rearrange("p (b n) -> p b n", b=2)
            QK = al(4 * 260).rearrange("p (c n) -> p c n", c=4)
            CO = al(1024).rearrange("p (c n) -> p c n", c=4)
            MV = al(8 * 129).rearrange("p (b h n) -> p b h n", b=2, h=4)
            SO = al(1024).rearrange("p (b n) -> p b n", b=2)
            GI, GF, FC, U, MM, NEM, T5 = (al(256) for _ in range(7))
            P = al(4 * 384).rearrange("p (k c n) -> p k c n", k=2, c=2)
            AT = al(768).rearrange("p (k n) -> p k n", k=2)
            LR = SM[:, 256:512]
            GTM = al(16)
            UT = al(8).rearrange("p (b h) -> p b h", b=2)
            NT = al(8).rearrange("p (b h) -> p b h", b=2)
            LT = al(8)
            T1 = al(512)
            R2 = al(256)
            TQ = T1.rearrange("p (k n) -> p k n", k=2)
            YD = al(1024).rearrange("p (b n) -> p b n", b=2)
            YM = DQ.rearrange("p h n -> p (h n)").rearrange("p (b n) -> p b n", b=2)
            cos, sin = cs("cos"), cs("sin")
            lam_init = 0.8 - 0.6 * math.exp(-0.3 * l)
            tl = got[f"lammix{l}"]
            tx = norm_xs(*x_after)
            ahead()
            th = transposed3(ve(f"ng{l}2"), lambda b, c: XS[:, b, c * 128:c * 128 + 128], tx, free=ps_after)
            bp = banks_pool(range(4, 8))
            bp["tok"] = {i: ps_after for i in bp["ids"]}
            gv = {}
            t1 = av(GWH[:, :], ve(f"gw{l}"), ACT.Copy)
            t2 = tt(GWL[:, :], ve(f"gw{l}"), GWH[:, :].bitcast(F32), ALU.subtract, t1)

            def gate_steps():
                bk = nb(bp)
                for b in range(2):
                    for c in range(8):
                        t = mm3(PS[:, bk, b * 8:b * 8 + 8],
                                (HTH[:, c, b * 128:b * 128 + 128], HTL[:, c, b * 128:b * 128 + 128]),
                                (GWH[:, 8 * c:8 * c + 8], GWL[:, 8 * c:8 * c + 8]), c == 0, c == 7, t1, t2, th[c],
                                bp["tok"][bk], sig=(c == 7))
                tz = bp["tok"][bk] = cp(GTM, PS[:, bk, 0:16], t)
                lv = LR.rearrange("p (a k n) -> p a k n", a=2, k=2)
                t = tt(lv[:, :, 0, :], lv[:, :, 0, :], lv[:, :, 1, :], ALU.mult, tl)
                tlr = dve(lambda e: e.tensor_reduce(LT[:, 0:2], lv[:, :, 0, :], AX.X, ALU.add), t)
                yield
                bk = nb(bp)
                for n in range(2):
                    for b in range(2):
                        t = tr(PS[0:4, bk, n * 256 + b * 128:n * 256 + b * 128 + 128],
                               GTM[:, b * 8 + 4 * n:b * 8 + 4 * n + 4], 128, tz, bp["tok"][bk], sig=(n + b == 2))
                gb = ve(f"gb{l}")
                r4 = slice(0, 4)
                ta = ts(GI[r4, :], PS[0:4, bk, 0:256], gb[r4, 0:1], None, ALU.add, None, t)
                tb = bp["tok"][bk] = ts(GF[r4, :], PS[0:4, bk, 256:512], gb[r4, 1:2], None, ALU.add, None, t)
                t = stt(FC[r4, :], GF[r4, :], -1.0, GF[r4, :], ALU.mult, ALU.max, tb)
                te = av(LT[:, 2:4], LT[:, 0:2], ACT.Exp, tlr)
                t = av(T5[r4, :], FC[r4, :], ACT.Exp, t, scale=-1.0)
                yield
                t = av(T5[r4, :], T5[r4, :], ACT.Ln, t, bias=1.0)
                t = stt(GF[r4, :], GF[r4, :], 0.0, T5[r4, :], ALU.min, ALU.subtract, t)
                read_row["lam"] = t5 = tt(LT[:, 4:5], LT[:, 2:3], LT[:, 3:4], ALU.subtract, te)
                tF = dve(lambda e: e.tensor_tensor_scan(FC[r4, :], GF[r4, :], GF[r4, :], 0.0, ALU.add, ALU.bypass), t)
                gv["lam"] = ts(LT[:, 4:5], LT[:, 4:5], lam_init, None, ALU.add, None, t5)
                gv["u"] = tU = tt(U[r4, :], GI[r4, :], FC[r4, :], ALU.subtract, tF, ta)
                yield
                tM = dve(lambda e: e.tensor_tensor_scan(MM[r4, :], U[r4, :], U[r4, :], 0.0, ALU.max, ALU.bypass), tU)
                t = tt(NEM[r4, :], FC[r4, :], MM[r4, :], ALU.add, tM)
                gv["m"] = ts(MM[r4, :], MM[r4, :], -1.0, None, ALU.mult, None, t)
                gv["nem"] = av(NEM[r4, :], NEM[r4, :], ACT.Exp, t, scale=-1.0)
                yield
            NLAM = LT[:, 4:5]
            steps = gate_steps()
            pend = []

            def rotate():
                if pend:
                    bk, dst, k, tq, h = pend.pop()
                    t = mm(PS[:, bk, 256:512], cs("swap"), TQ[:, k, :], True, True, tq, sig=True)
                    t3 = tt(dst, TQ[:, k, :], cos, ALU.mult, tq)
                    t4 = bp["tok"][bk] = tt(R2, PS[:, bk, 256:512], sin, ALU.mult, t, rot[0])
                    rot[0] = rot[k + 1] = turned[h] = tt(dst, dst, R2, ALU.add, t3, t4)
            rot, turned = {0: None, 1: None, 2: None}, {}
            for n, dst in ((0, DQ), (1, DK)):
                for hs in range(2):
                    hi, lo, tsp, key = next_split()
                    for hh in range(2):
                        h = 2 * hs + hh
                        bk = nb(bp)
                        for c in range(8):
                            t = mm3(PS[:, bk, 0:256], (hi[:, c, hh * 128:hh * 128 + 128], lo[:, c, hh * 128:hh * 128 + 128]),
                                    (HTH[:, c, :], HTL[:, c, :]), c == 0, c == 7, tsp, bp["tok"][bk], th[c],
                                    sig=(c == 7))
                        tq = av(TQ[:, hh, :], PS[:, bk, 0:256], ACT.Copy, t, rot[hh + 1])
                        rotate()
                        pend.append((bk, dst[:, h, :], hh, tq, h))
                    sp_free[key] = t
                    next(steps)

            tU, tN, tM, tlam = gv["u"], gv["nem"], gv["m"], gv["lam"]

            def token_unit(hs, box, evac=None, mid=None, half=None):
                if hs == 0:
                    box["b"] = [nb(bp), nb(bp)]
                bks = box["b"]
                hi, lo, tsp, key = next_split(mid)
                for cc in range(4):
                    c = 4 * hs + cc
                    if half and cc == 2:
                        half()
                    for b in range(2):
                        t = mm3(PS[:, bks[b], :], (HTH[:, c, b * 128:b * 128 + 128], HTL[:, c, b * 128:b * 128 + 128]),
                                (hi[:, cc, :], lo[:, cc, :]), c == 0, c == 7, tsp, bp["tok"][bks[b]], sig=(cc == 3))
                sp_free[key] = t
                if evac:
                    for b in range(2):
                        bp["tok"][bks[b]] = evac(b, PS[:, bks[b], :], t)
            mask = cs("mask")
            bt = {bk: th[7] for bk in range(4)}
            at, used, pu = {}, {}, {}
            ssd, rsd, ssm, rsm = (SM[:, 80 + 8 * z:88 + 8 * z] for z in range(4))
            sqd = []

            def scores(h):
                for d in range(2):
                    bk = d
                    for i in range(2):
                        o = PS[:, bk, 0:128] if i == 0 else PS[:, bk, 128:384]
                        t = mm(o, DQ[64 * d:64 * d + 64, h, i * 128:i * 128 + 128],
                               DK[64 * d:64 * d + 64, h, 0:128 + 128 * i], True, True, bt[bk], turned[h], sig=True)
                    p = P[:, h % 2, d, :]
                    bt[bk] = t = stt(p, PS[:, bk, 0:384], 0.125, mask, ALU.mult, ALU.add, t, pu.get(h - 2))
                    q = 4 * (h % 2) + 2 * d
                    m, s = SM[:, 32 + q:34 + q], SM[:, 40 + q:42 + q]
                    for i, (a, z) in enumerate(((0, 128), (128, 384))):
                        tm = dve(lambda e, i=i, a=a, z=z, m=m, p=p: e.tensor_reduce(m[:, i:i + 1], p[:, a:z], AX.X,
                                                                                     ALU.max, negate=True), t)
                    for i, (a, z) in enumerate(((0, 128), (128, 384))):
                        te = av(p[:, a:z], p[:, a:z], ACT.Exp, tm, bias=m[:, i:i + 1], accum_out=s[:, i:i + 1])
                    exps[h, d] = te

            def mix_probs(h):
                q = 4 * (h % 2)
                s = SM[:, 40 + q:44 + q]
                t = dve(lambda e: e.reciprocal(s, s), exps[h, 0], exps[h, 1])
                t = ts(s[:, 2:4], s[:, 2:4], NLAM, None, ALU.mult, None, t, tlam)
                for i, (a, z) in enumerate(((0, 128), (128, 384))):
                    t5 = av(P[:, h % 2, 1, a:z], P[:, h % 2, 1, a:z], ACT.Copy, t, scale=s[:, 2 + i:3 + i])
                    at[h] = stt(P[:, h % 2, 0, a:z], P[:, h % 2, 0, a:z], s[:, i:i + 1], P[:, h % 2, 1, a:z], ALU.mult,
                                ALU.subtract, t5)
            exps = {}

            def values(h):
                bk = 2
                for j in range(3):
                    t = tr(PS[:, bk, j * 128:j * 128 + 128], P[:, h % 2, 0, j * 128:j * 128 + 128], 128, at[h], bt[bk],
                           sig=(j == 2))
                pu[h] = t
                bt[bk] = t = av(AT[:, h % 2, :], PS[:, bk, 0:384], ACT.Copy, t, used.get(h - 2))
                at[h] = t

            def outs(h):
                t = at[h]
                a = AT[:, h % 2, :]
                bo = 3
                v0, v1 = DV[:, 0, h * 128:h * 128 + 128], DV[:, 1, h * 128:h * 128 + 128]
                mm(PS[:, bo, 0:128], a[:, 0:128], v0, True, True, t, bt[bo], tdv)
                mm(PS[:, bo, 128:256], a[:, 128:256], v0, True, False)
                used[h] = mm(PS[:, bo, 128:256], a[:, 256:384], v1, False, True, sig=True)
                bt[bo] = t = av(YD[:, :, h * 128:h * 128 + 128], PS[:, bo, 0:256].rearrange("p (b n) -> p b n", b=2),
                                ACT.Copy, used[h])
                for b in range(2):
                    sqd.append(av(JK[:, 0:128], YD[:, b, h * 128:h * 128 + 128], ACT.Square, t, act.last(),
                                  accum_out=ssd[:, 4 * b + h:4 * b + h + 1]))

            tz = dve(lambda e: e.memset(QK[:, :, 0:3], 0.0))
            cw, cb = ve(f"cw{l}"), ve(f"cb{l}")
            co = {}

            def ml_qk(hp, mid, half):
                hi, lo, tsp, key = next_split(mid)
                for hh in range(2):
                    if hh:
                        half()
                    h = 2 * hp + hh
                    bk = nb(bp)
                    o = hh * 128
                    for c in range(8):
                        t = mm3(PS[:, bk, 0:256], (hi[:, c, o:o + 128], lo[:, c, o:o + 128]), (HTH[:, c, :], HTL[:, c, :]),
                                c == 0, c == 7, tsp, bp["tok"][bk], sig=(c == 7))
                    bp["tok"][bk] = co[h] = av(QK[:, h, 3:259], PS[:, bk, 0:256], ACT.Copy, t)
                sp_free[key] = t

            def conv(hp):
                for h in (2 * hp, 2 * hp + 1):
                    t = ts(CO[:, h, :], QK[:, h, 0:256], cw[:, h:h + 1], cb[:, h:h + 1], ALU.mult, ALU.add, co[h], tz)
                    for j in range(1, 4):
                        t = stt(CO[:, h, :], QK[:, h, j:j + 256], cw[:, 4 * j + h:4 * j + h + 1], CO[:, h, :], ALU.mult,
                                ALU.add, t)
                    co[h] = t

            def rows_v(b, ps, t):
                return av(MV[:, b, :, 0:128], ps.rearrange("p (h n) -> p h n", h=4), ACT.Copy, t)

            def both_of(*fs):
                def go():
                    for f, h in fs:
                        f(h)
                return go
            tdv = []

            def rows_dv(b, ps, t):
                tdv.append(av(DV[:, b, :], ps, ACT.Copy, t))
                return tdv[-1]
            box = {}
            token_unit(0, box, mid=both_of((scores, 0)), half=rotate)
            mix_probs(0)
            token_unit(1, box, rows_dv, mid=both_of((scores, 1)), half=both_of((values, 0)))
            mix_probs(1)
            ml_qk(0, both_of((scores, 2)), both_of((values, 1)))
            outs(0)
            mix_probs(2)
            ml_qk(1, both_of((scores, 3)), both_of((values, 2), (outs, 1)))
            mix_probs(3)
            rows_for(follows(f"mix{l}"))
            dve(lambda e: e.memset(MV[:, :, :, 128:129], 1.0))
            token_unit(0, box, half=both_of((values, 3), (outs, 2), (conv, 0)))
            outs(3)
            token_unit(1, box, rows_v, half=both_of((conv, 1)))
            tyd = []

            def norm_heads():
                t = rsq(rsd, ssd, 128, sqd, times=1.0 - lam_init)
                t = tt(YD.rearrange("p b (h n) -> p (b h) n", h=4), YD.rearrange("p b (h n) -> p (b h) n", h=4),
                         rsd.unsqueeze(2).to_broadcast([128, 8, 128]), ALU.mult, t, dve.last())
                tyd.append(t)
                for h in range(4):
                    co[h] = av(CO[:, h, :], CO[:, h, :], ACT.Silu, co[h])
            token_unit(0, box, half=norm_heads)
            chunks_read, tco = pe.last(), co[3]
            thy = {}

            def early():
                for b in range(2):
                    tr(PS[:, 0, b * 4:b * 4 + 4], U[0:4, b * 128:b * 128 + 128], 4, tU, bt[0])
                    t = tr(PS[:, 0, 8 + b * 4:12 + b * 4], NEM[0:4, b * 128:b * 128 + 128], 4, tN, tM, sig=True)
                cp(UT, PS[:, 0, 0:8].rearrange("p (b h) -> p b h", b=2), t)
                bt[0] = cp(NT, PS[:, 0, 8:16].rearrange("p (b h) -> p b h", b=2), t)
                thy.update(transposed3(yg, lambda b, c: YD[:, b, c * 128:c * 128 + 128], [tyd, tyd], range(4), (2, 3),
                                       chunks_read, chunks_read, [bt[2], bt[3]]))
            yg = ve(f"yg{l}")
            token_unit(1, box, lambda b, ps, t: av(SO[:, b, :], ps, ACT.Sigmoid, t), half=early)
            tnt = bt[0]
            tso = act.last()
            bt[2] = bt[3] = [thy[c] for c in range(4)]
            bt[4] = bt[5] = bt[6] = bt[7] = [bp["tok"][z] for z in range(4, 8)]
            E = [P[:, 0, 0, :], P[:, 1, 0, :]]
            sel = cs("sel")
            caus = cs("caus")
            tw_, nu = {}, {}
            rs_of, tym = {}, {}

            def wts(h):
                k = h % 2
                dp, ch = 64 * (h % 2), h // 2
                b0, b1 = 0, 1
                mm(PS[:, b0, 0:256], sel[0:4, h * 128:h * 128 + 128], MM[0:4, :], True, True, bt[b0], tM)
                t0 = mm(PS[:, b0, 256:384], sel[0:4, h * 128:h * 128 + 128], MM[0:4, 128:256], True, True, sig=True)
                mm(PS[:, b1, 0:256], CO[dp:dp + 64, 2 + ch, 0:128], CO[dp:dp + 64, ch, :], True, True, bt[b1], tco)
                t1 = mm(PS[:, b1, 256:384], CO[dp:dp + 64, 2 + ch, 128:256], CO[dp:dp + 64, ch, 128:256], True, True,
                        sig=True)
                e = E[k]
                ta = ts(e[:, 0:256], PS[:, b0, 0:256], UT[:, 0, h:h + 1], 0.0, ALU.add, ALU.min, t0, nu.get(h - 2),
                        tnt, pu[3])
                tb = ts(e[:, 256:384], PS[:, b0, 256:384], UT[:, 1, h:h + 1], 0.0, ALU.add, ALU.min, t0)
                bt[b0] = tb
                te = av(e, e, ACT.Exp, ta, tb)
                t = stt(e, PS[:, b1, 0:384], 0.125, e, ALU.mult, ALU.mult, te, t1)
                bt[b1] = t
                tt(e[:, 0:128], e[:, 0:128], caus, ALU.mult, t)
                tw_[h] = tt(e[:, 256:384], e[:, 256:384], caus, ALU.mult, t)

            def num(h):
                e = E[h % 2]
                bo = 2 + h % 2
                mm(PS[:, bo, 0:129], e[:, 0:128], MV[:, 0, h, :], True, True, tw_[h], bt[bo])
                mm(PS[:, bo, 129:258], e[:, 128:256], MV[:, 0, h, :], True, False)
                nu[h] = t = mm(PS[:, bo, 129:258], e[:, 256:384], MV[:, 1, h, :], False, True, sig=True)
                o = PS[:, bo, 0:258].rearrange("p (b n) -> p b n", b=2)
                dn = SM[:, 64 + 2 * h:66 + 2 * h]
                t = ts(dn, o[:, :, 128], -1.0, None, ALU.mult, None, t)
                t = tt(dn, dn, o[:, :, 128], ALU.max, t)
                t = tt(dn, dn, NT[:, :, h], ALU.max, t)
                t = dve(lambda e_: e_.reciprocal(dn, dn), t)
                bt[bo] = t = tt(YM[:, :, h * 128:h * 128 + 128], o[:, :, 0:128],
                                dn.unsqueeze(2).to_broadcast([128, 2, 128]), ALU.mult, t)
                for b in range(2):
                    ta = av(JK[:, 0:128], YM[:, b, h * 128:h * 128 + 128], ACT.Square, t, act.last(),
                            accum_out=ssm[:, 2 * h + b:2 * h + b + 1])
                rs_of[h] = rsq(rsm[:, 2 * h:2 * h + 2], ssm[:, 2 * h:2 * h + 2], 128, ta)

            def close(h):
                for b in range(2):
                    y = YM[:, b, h * 128:h * 128 + 128]
                    tym[h] = stt(y, y, rsm[:, 2 * h + b:2 * h + b + 1], SO[:, b, h * 128:h * 128 + 128], ALU.mult,
                                 ALU.mult, rs_of[h], tso)

            def turn(h, bk):
                return transposed3(yg, lambda b, c: YM[:, b, (c - 4) * 128:(c - 4) * 128 + 128],
                                   [[tym[h], tym[h + 1]]] * 2, range(4 + h, 6 + h), (bk,), None, None, bt[bk])

            def out_unit(s, ready, mid, half=None):
                hi, lo, tsp, key = next_split(mid)
                for c in range(2):
                    if c and half:
                        half()
                    f = 2 * s + c
                    for b in range(2):
                        for h in range(2):
                            t = mm3(PS[:, 4 + 2 * b + h, :],
                                    (HTH[:, f, b * 128:b * 128 + 128], HTL[:, f, b * 128:b * 128 + 128]),
                                    (hi[:, c, h * 512:h * 512 + 512], lo[:, c, h * 512:h * 512 + 512]),
                                    f == 0, False, tsp, ready[f], bt[4], sig=(b + h == 2))
                sp_free[key] = t
            out_unit(0, thy, both_of((wts, 0)))
            wts(1)
            num(0)
            out_unit(1, thy, both_of((wts, 2), (num, 1)), both_of((close, 0), (close, 1), (wts, 3)))
            thm = turn(0, 0)
            num(2)
            num(3)
            out_unit(2, thm, both_of((close, 2), (close, 3)))
            thm.update(turn(2, 1))
            hi, lo, tsp, key = issued.pop(0)
            ends = []
            for b in range(2):
                for f in (6, 7):
                    for h in range(2):
                        t = mm3(PS[:, 4 + 2 * b + h, :],
                                (HTH[:, f, b * 128:b * 128 + 128], HTL[:, f, b * 128:b * 128 + 128]),
                                (hi[:, f - 6, h * 512:h * 512 + 512], lo[:, f - 6, h * 512:h * 512 + 512]),
                                False, f == 7, tsp, thm[f], sig=(h == 1))
                ends.append(t)
            sp_free[key] = t
            dve.wait(got[f"mix{l}"])
            tmp = CO.rearrange("p c n -> p (c n)"), WK[:, 1024:2048]
            ps_after[:] = post_norm((4, 6), RB[:, 2, :], 1.0, ends, tmp)
            read_row[2] = ps_after[1]
            x_after[:] = [t]

        def follows(name):
            n = plan.index(name) + 1
            return plan[n] if n < len(plan) else "end"
        ps_after, x_after = [], []
        stages = {"pool": stage_pool, "moe0": lambda: stage_moe(0), "moe1": lambda: stage_moe(1), "mla": stage_mla,
                  "fin": stage_fin, "mix0": lambda: stage_mix(0), "mix1": lambda: stage_mix(1)}
        for l in range(2):
            for k in range(2):
                stages[f"ffn{l}{k}"] = lambda l=l, k=k: stage_ffn(l, k)
        for name in plan:
            if name == "mla":
                want_mla()
            elif name.startswith("ffn"):
                want_ffn(int(name[3]), int(name[4]))
            elif name.startswith("mix"):
                want_mix(int(name[3]))
        if plan[0][:3] in ("ffn", "mix") or plan[0] == "fin":
            rows_for(plan[0] if plan[0] != "fin" else "ffn00")
        for name in plan:
            stages[name]()

        issue_loads(len(loads))
        if len(loads) in breaks:
            enter_break(len(loads))
        s_out = sem("s_out")
        sp.wait(*t_rows.values())
        for b in range(2):
            sp.wait(xt[b])
            sp.ops.append(lambda e, b=b: e.dma_start(W["out"][128 * b:128 * b + 128, :], X[:, b, :]).then_inc(s_out, 16))
        sp.wait(dve.last(), act.last(), pe.last())
        sp.ops.append(lambda e: e.wait_ge(s_out, 32))

        block = ctx.enter_context(nc.Block())

        @block.sync
        def _(e):
            sp.play(e)

        @block.tensor
        def _(e):
            pe.play(e)

        @block.vector
        def _(e):
            dve.play(e)

        @block.scalar
        def _(e):
            act.play(e)

        @block.gpsimd
        def _(e):
            pool.play(e)


def constants():
    cst = np.zeros((128, NCST), np.float32)

    def put(name, a):
        o, w = CST[name]
        cst[:a.shape[0], o:o + w] = a
    p = np.arange(128)
    put("ident", np.eye(128, dtype=np.float32))
    put("tri", (p[:, None] < p[None, :]).astype(np.float32))
    put("ones", np.ones((128, 128), np.float32))
    put("caus", (p[:, None] <= p[None, :]).astype(np.float32))
    k = np.arange(256)
    m0 = np.where(k[None, :128] // 64 <= p[:, None] // 64, 0.0, NEG)
    m1 = np.where(k[None, :] // 64 <= (p[:, None] + 128) // 64, 0.0, NEG)
    put("mask", np.concatenate([m0, m1], 1).astype(np.float32))
    inv = np.float32(10000.0) ** (-np.arange(32, dtype=np.float32) / np.float32(32))
    ang = (np.arange(256, dtype=np.float32)[None, :] * inv[:, None]).astype(np.float32)
    co, si = np.cos(ang), np.sin(ang)
    put("cos", np.concatenate([co, co, co, co], 0))
    put("sin", np.concatenate([-si, si, -si, si], 0))
    put("iota", np.broadcast_to(np.arange(32, dtype=np.float32), (128, 32)))
    sel = np.zeros((4, 4, 128), np.float32)
    for h in range(4):
        sel[h, h, :] = 1.0
    put("sel", sel.reshape(4, 512))
    put("swap", (p[:, None] == (p[None, :] ^ 32)).astype(np.float32))
    pm = np.zeros((2, 128, 4, 256), np.float32)
    for g, win in enumerate((2, 4, 8, 16)):
        for t in range(256):
            lo = max(t + 1 - win, 0)
            for s in range(lo, t + 1):
                pm[s // 128, s % 128, g, t] = 1.0 / (t + 1 - lo)
            pm[t // 128, t % 128, g, t] -= 1.0
    return cst, np.ascontiguousarray(pm.transpose(1, 0, 2, 3).reshape(128, 2048))


def layouts(a):
    vec = np.zeros((128, NVEC), np.float32)

    def put(name, v):
        o, w = VEC[name]
        vec[:v.shape[0], o:o + w] = v
    for name, v in (("pool_norm", a["pool_norm"][0]), ("kv_in", a["kv_in_norm"]), ("attn", a["attn_norm"][0]),
                    ("ffn0", a["ffn_norm"][0]), ("ffn1", a["ffn_norm"][1]), ("kv_norm", a["kv_norm"]),
                    ("q_norm", a["q_norm"][0])):
        put(name, v.reshape(-1, 128).T)
    ng = a["norm_gains_2"]
    for l in range(2):
        for k in (0, 2, 4):
            put(f"ng{l}{k}", ng[l, k].reshape(8, 128).T)
        put(f"yg{l}", np.stack([a["da_subln_g_2"][l]] * 4 + [a["ml_norm_g_2"][l]] * 4, 1))
        put(f"cw{l}", a["ml_conv_w_2"][l].reshape(16, 128).T)
        put(f"cb{l}", a["ml_conv_b_2"][l].reshape(4, 128).T)
        put(f"gb{l}", a["ml_gate_b_2"][l].reshape(2, 4).T)
        put(f"gw{l}", a["mix_w_in_2"][l][:, 3072:].reshape(8, 128, 8).transpose(1, 0, 2).reshape(128, 64))
        rw = np.concatenate([a["router_group_w"][l], a["router_expert_w"][l]], 1)
        put(f"rw{l}", rw.reshape(8, 128, 36).transpose(1, 0, 2).reshape(128, 288))
    rows = np.zeros((1, NROWS), np.float32)

    def rput(name, v):
        o, w = ROWS[name]
        rows[0, o:o + w] = v.reshape(-1)
    rput("pool_b", a["pool_b"])
    rput("pool_scale", a["pool_scale"])
    rput("final", a["final_norm"])
    for l in range(2):
        rput(f"r{l}", np.concatenate([a["router_group_b"][l], a["router_expert_b"][l]]))
        rput(f"lam{l}", a["da_lambda_2"][l])
        for k in (1, 3, 5):
            rput(f"ng{l}{k}", ng[l, k])
    return vec, rows


BIGS = [("pool_w", "pool_w"), ("w_dkv", "w_dkv"), ("w_uk", "w_uk"), ("w_uv", "w_uv"), ("wq_down", "wq_down"),
        ("wq_up", "wq_up"), ("wo", "wo"), ("w_gate", "w_gate"), ("w_up", "w_up"), ("w_down", "w_down"),
        ("ffn_w_in", "ffn_w_in_2"), ("ffn_w_out", "ffn_w_out_2"), ("mix_w_in", "mix_w_in_2"),
        ("mix_w_out", "mix_w_out_2")]


def feeds(inputs):
    a = {k: np.asarray(v) for k, v in inputs.items()}
    cst, pm = constants()
    vec, rows = layouts(a)
    f = {"cst": cst, "pm": pm, "vec": vec, "rows": rows, "x": np.ascontiguousarray(a["x"].reshape(256, 1024))}
    for k, n in BIGS:
        f[k] = np.ascontiguousarray(a[n])
    return f


def declare(nc, f):
    W = {k: nc.dram_tensor("in_" + k, v.shape, mybir.dt.from_np(v.dtype), kind="ExternalInput").ap()
         for k, v in f.items()}
    W["out"] = nc.dram_tensor("out_0_dram", (256, 1024), F32, kind="ExternalOutput").ap()
    return W


def kernel(**inputs):
    import concourse.bacc as _bacc
    from concourse.bass_utils import run_bass_kernel_spmd as _run

    f = feeds(inputs)
    nc = _bacc.Bacc("TRN2", target_bir_lowering=False, num_devices=1)
    W = declare(nc, f)
    build(nc, W, PLAN)
    r = _run(nc, [{"in_" + k: v for k, v in f.items()}], core_ids=[0])
    return r.results[0]["out_0_dram"].reshape(1, 256, 1024)
```
